# Optimizing a Trainium2 kernel written in Bass

```python
import jax, jax.numpy as jnp
from jax import lax
import numpy as np

D_MODEL = 1024
BATCH = 1
SEQ = 512
DEPTH = 1

MEM_LEN = 256

NSA_HEADS = 8
NSA_HEAD_DIM = 64
NSA_KV_GROUPS = 2
NSA_HEADS_PER_GROUP = NSA_HEADS // NSA_KV_GROUPS
NSA_WIDTH = NSA_HEADS * NSA_HEAD_DIM
KV_WIDTH = NSA_KV_GROUPS * NSA_HEAD_DIM
NSA_GATE_WIDTH = NSA_HEADS * 3
CMP_BLOCK = 32
CMP_STRIDE = 16
CMP_HIDDEN = 256
SLC_BLOCK = 64
SLC_TOPN = 16
WINDOW = 512
Q_BLOCK = 128
FORCE_BONUS = 1e4

GMLP_WIDTH = 512
GMLP_GROUPS = 4
GMLP_GROUP_DIM = GMLP_WIDTH // GMLP_GROUPS
GMLP_CHUNK = 128

N_BRANCHES = 2
IN_SPLITS = (NSA_WIDTH, KV_WIDTH, KV_WIDTH, KV_WIDTH, KV_WIDTH, KV_WIDTH, KV_WIDTH,
             NSA_GATE_WIDTH, GMLP_WIDTH, GMLP_WIDTH, N_BRANCHES * D_MODEL)
IN_PROJ_WIDTH = NSA_WIDTH + 6 * KV_WIDTH + NSA_GATE_WIDTH + 2 * GMLP_WIDTH + N_BRANCHES * D_MODEL

XATTN_HEADS = 4
XATTN_HEAD_DIM = D_MODEL // XATTN_HEADS

PEER_HEADS = 8
PEER_KEYS = 128
PEER_EXPERTS = PEER_KEYS * PEER_KEYS
PEER_QUERY_DIM = 256
PEER_HALF = PEER_QUERY_DIM // 2
PEER_TOPK = 16
PEER_TOKEN_CHUNK = 128

NORM_EPS = 1e-6
NEG_INF = -1e30
TINY = 1e-30

kernel_name = "hybrid_nsa_gmlp_peer_block"

def rms_norm(x, g):
    xf = x.astype(jnp.float32)
    y = xf * lax.rsqrt(jnp.mean(xf * xf, axis=-1, keepdims=True) + NORM_EPS)
    return (y * g.astype(jnp.float32)).astype(x.dtype)

def masked_softmax(s, mask):
    s = jnp.where(mask, s.astype(jnp.float32), NEG_INF)
    m = jnp.max(s, axis=-1, keepdims=True)
    p = jnp.where(mask, jnp.exp(s - m), 0.0)
    return p / jnp.maximum(jnp.sum(p, axis=-1, keepdims=True), TINY)

def gelu(x):
    return jax.nn.gelu(x, approximate=False)

def compress_tokens(tok, pe, w1, b1, w2):
    B, S, G, dk = tok.shape
    r = CMP_BLOCK // CMP_STRIDE
    n_chunks = S // CMP_STRIDE
    n_cmp = n_chunks - r + 1
    chunks = tok.reshape(B, n_chunks, CMP_STRIDE, G, dk)
    blocks = jnp.concatenate([chunks[:, j:j + n_cmp] for j in range(r)], axis=2)
    blocks = blocks + pe[None, None, :, None, :]
    flat = blocks.transpose(0, 1, 3, 2, 4).reshape(B, n_cmp, G, CMP_BLOCK * dk)
    return gelu(flat @ w1 + b1) @ w2

def nsa_attention(q, kc, vc, ks, vs, kw, vw, gates,
                  cmp_pe_k, cmp_w1_k, cmp_b1_k, cmp_w2_k,
                  cmp_pe_v, cmp_w1_v, cmp_b1_v, cmp_w2_v):
    B, S, G, R, dk = q.shape
    scale = dk ** -0.5
    k_cmp = compress_tokens(kc, cmp_pe_k, cmp_w1_k, cmp_b1_k, cmp_w2_k)
    v_cmp = compress_tokens(vc, cmp_pe_v, cmp_w1_v, cmp_b1_v, cmp_w2_v)
    n_cmp = k_cmp.shape[1]
    n_slc = S // SLC_BLOCK
    n_sel = min(SLC_TOPN, n_slc)
    n_qblk = S // Q_BLOCK

    k_blocks = ks.reshape(B, n_slc, SLC_BLOCK, G, dk).transpose(0, 3, 1, 2, 4)
    v_blocks = vs.reshape(B, n_slc, SLC_BLOCK, G, dk).transpose(0, 3, 1, 2, 4)
    pad = ((0, 0), (WINDOW, 0), (0, 0), (0, 0))
    kw_pad = jnp.pad(kw, pad)
    vw_pad = jnp.pad(vw, pad)

    c_start = jnp.arange(n_cmp) * CMP_STRIDE
    j_start = jnp.arange(n_slc) * SLC_BLOCK
    ov = jnp.clip(jnp.minimum(c_start[:, None] + CMP_BLOCK, j_start[None, :] + SLC_BLOCK)
                  - jnp.maximum(c_start[:, None], j_start[None, :]), 0, None)
    overlap = ov.astype(jnp.float32) / CMP_BLOCK
    cmp_end = c_start + CMP_BLOCK - 1
    blk = jnp.arange(n_slc)
    b_ix = jnp.arange(B)[:, None, None, None]
    g_ix = jnp.arange(G)[None, :, None, None]

    def one_block(i):
        q0 = i * Q_BLOCK
        qb = lax.dynamic_slice_in_dim(q, q0, Q_BLOCK, axis=1)
        gb = lax.dynamic_slice_in_dim(gates, q0, Q_BLOCK, axis=1)
        t = q0 + jnp.arange(Q_BLOCK)

        s_c = jnp.einsum('bqgrd,bcgd->bgrqc', qb, k_cmp) * scale
        mask_c = cmp_end[None, :] <= t[:, None]
        p_c = masked_softmax(s_c, mask_c)
        o_c = jnp.einsum('bgrqc,bcgd->bqgrd', p_c.astype(v_cmp.dtype), v_cmp)

        imp = jnp.einsum('bgrqc,cj->bgqj', p_c, overlap)
        allowed = blk[None, :] * SLC_BLOCK <= t[:, None]
        cur = (t // SLC_BLOCK)[:, None]
        forced = (blk[None, :] == 0) | (blk[None, :] == cur) | (blk[None, :] == cur - 1)
        score = jnp.where(forced & allowed, FORCE_BONUS, jnp.where(allowed, imp, NEG_INF))
        top_score, idx = lax.top_k(score, n_sel)
        valid_blk = top_score > 0.5 * NEG_INF

        kb = k_blocks[b_ix, g_ix, idx]
        vb = v_blocks[b_ix, g_ix, idx]
        n_tok = n_sel * SLC_BLOCK
        s_s = jnp.einsum('bqgrd,bgqnkd->bgrqnk', qb, kb) * scale
        tok_pos = idx[..., None] * SLC_BLOCK + jnp.arange(SLC_BLOCK)
        mask_s = valid_blk[..., None] & (tok_pos <= t[None, None, :, None, None])
        p_s = masked_softmax(s_s.reshape(B, G, R, Q_BLOCK, n_tok),
                             mask_s.reshape(B, G, 1, Q_BLOCK, n_tok))
        o_s = jnp.einsum('bgrqm,bgqmd->bqgrd', p_s.astype(vb.dtype),
                         vb.reshape(B, G, Q_BLOCK, n_tok, dk))

        kwb = lax.dynamic_slice_in_dim(kw_pad, q0, Q_BLOCK + WINDOW, axis=1)
        vwb = lax.dynamic_slice_in_dim(vw_pad, q0, Q_BLOCK + WINDOW, axis=1)
        s_pos = q0 - WINDOW + jnp.arange(Q_BLOCK + WINDOW)
        diff = t[:, None] - s_pos[None, :]
        mask_w = (s_pos >= 0)[None, :] & (diff >= 0) & (diff < WINDOW)
        s_w = jnp.einsum('bqgrd,bkgd->bgrqk', qb, kwb) * scale
        p_w = masked_softmax(s_w, mask_w)
        o_w = jnp.einsum('bgrqk,bkgd->bqgrd', p_w.astype(vwb.dtype), vwb)

        return gb[..., 0:1] * o_c + gb[..., 1:2] * o_s + gb[..., 2:3] * o_w

    out = lax.map(one_block, jnp.arange(n_qblk))
    return out.transpose(1, 0, 2, 3, 4, 5).reshape(B, S, G * R * dk)

def chunked_gmlp(u_raw, v_raw, ln_g, ln_b, ws, bs):
    B, S, W = u_raw.shape
    u = gelu(u_raw)
    v = gelu(v_raw).astype(jnp.float32)
    mu = jnp.mean(v, axis=-1, keepdims=True)
    var = jnp.mean(jnp.square(v - mu), axis=-1, keepdims=True)
    v = ((v - mu) * lax.rsqrt(var + NORM_EPS) * ln_g + ln_b).astype(u.dtype)
    v = v.reshape(B, S // GMLP_CHUNK, GMLP_CHUNK, GMLP_GROUPS, GMLP_GROUP_DIM)
    causal = jnp.tril(jnp.ones((GMLP_CHUNK, GMLP_CHUNK), dtype=ws.dtype))
    s = jnp.einsum('gts,bcsgd->bctgd', ws * causal, v) + bs.T[None, None, :, :, None]
    return u * s.reshape(B, S, W)

def memory_cross_attention(hn, mn, w_xq, w_xkv, w_xo):
    B, S, D = hn.shape
    M = mn.shape[1]
    q = (hn @ w_xq).reshape(B, S, XATTN_HEADS, XATTN_HEAD_DIM)
    k, v = jnp.split(mn @ w_xkv, 2, axis=-1)
    k = k.reshape(B, M, XATTN_HEADS, XATTN_HEAD_DIM)
    v = v.reshape(B, M, XATTN_HEADS, XATTN_HEAD_DIM)
    s = jnp.einsum('bshd,bmhd->bhsm', q, k) * (XATTN_HEAD_DIM ** -0.5)
    p = jax.nn.softmax(s.astype(jnp.float32), axis=-1).astype(v.dtype)
    o = jnp.einsum('bhsm,bmhd->bshd', p, v).reshape(B, S, D)
    return o @ w_xo

def peer_ffn(hn, w_peer_q, sub_keys, peer_u, peer_v):
    B, S, D = hn.shape
    q = (hn @ w_peer_q).reshape(B, S, PEER_HEADS, 2, PEER_HALF)
    sc = jnp.einsum('bshpd,hpkd->bshpk', q, sub_keys).astype(jnp.float32)
    half_s, half_i = lax.top_k(sc, PEER_TOPK)
    cand_s = half_s[..., 0, :, None] + half_s[..., 1, None, :]
    cand_i = half_i[..., 0, :, None] * PEER_KEYS + half_i[..., 1, None, :]
    cand_s = cand_s.reshape(B, S, PEER_HEADS, PEER_TOPK * PEER_TOPK)
    cand_i = cand_i.reshape(B, S, PEER_HEADS, PEER_TOPK * PEER_TOPK)
    best_s, pos = lax.top_k(cand_s, PEER_TOPK)
    expert = jnp.take_along_axis(cand_i, pos, axis=-1)
    gate = jax.nn.softmax(best_s, axis=-1).astype(hn.dtype)

    n_e = PEER_HEADS * PEER_TOPK
    n_chunk = S // PEER_TOKEN_CHUNK
    def to_chunks(a):
        return jnp.moveaxis(a.reshape(B, n_chunk, PEER_TOKEN_CHUNK, *a.shape[2:]), 1, 0)
    xs = to_chunks(hn)
    es = to_chunks(expert.reshape(B, S, n_e))
    gs = to_chunks(gate.reshape(B, S, n_e))

    def one_chunk(args):
        xc, ec, gc = args
        u = peer_u[ec]
        a = gelu(jnp.einsum('btd,bted->bte', xc, u))
        return jnp.einsum('bte,bted->btd', gc * a, peer_v[ec])

    out = lax.map(one_chunk, (xs, es, gs))
    return jnp.moveaxis(out, 0, 1).reshape(B, S, D)

def setup_inputs(seed: int = 0) -> dict:
    key = jax.random.key(seed)
    ks = jax.random.split(key, 32)
    f32 = jnp.float32
    D = D_MODEL
    dk = NSA_HEAD_DIM

    def nrm(k, shape, scale):
        return jax.random.normal(k, shape, f32) * scale

    def gain(k, n):
        return 1.0 + 0.02 * jax.random.normal(k, (n,), f32)

    return {
        "x": nrm(ks[0], (BATCH, SEQ, D), 1.0),
        "mem": nrm(ks[1], (BATCH, MEM_LEN, D), 1.0),
        "g_mix": gain(ks[2], D),
        "w_in": nrm(ks[3], (D, IN_PROJ_WIDTH), D ** -0.5),
        "cmp_pe_k": nrm(ks[4], (CMP_BLOCK, dk), 0.02),
        "cmp_w1_k": nrm(ks[5], (CMP_BLOCK * dk, CMP_HIDDEN), (CMP_BLOCK * dk) ** -0.5),
        "cmp_b1_k": nrm(ks[6], (CMP_HIDDEN,), 0.01),
        "cmp_w2_k": nrm(ks[7], (CMP_HIDDEN, dk), CMP_HIDDEN ** -0.5),
        "cmp_pe_v": nrm(ks[8], (CMP_BLOCK, dk), 0.02),
        "cmp_w1_v": nrm(ks[9], (CMP_BLOCK * dk, CMP_HIDDEN), (CMP_BLOCK * dk) ** -0.5),
        "cmp_b1_v": nrm(ks[10], (CMP_HIDDEN,), 0.01),
        "cmp_w2_v": nrm(ks[11], (CMP_HIDDEN, dk), CMP_HIDDEN ** -0.5),
        "gmlp_ln_g": gain(ks[12], GMLP_WIDTH),
        "gmlp_ln_b": nrm(ks[13], (GMLP_WIDTH,), 0.01),
        "gmlp_ws": nrm(ks[14], (GMLP_GROUPS, GMLP_CHUNK, GMLP_CHUNK), GMLP_CHUNK ** -0.5),
        "gmlp_bs": 1.0 + 0.1 * jax.random.normal(ks[15], (GMLP_GROUPS, GMLP_CHUNK), f32),
        "w_nsa_out": nrm(ks[16], (NSA_WIDTH, D), NSA_WIDTH ** -0.5),
        "w_gmlp_out": nrm(ks[17], (GMLP_WIDTH, D), GMLP_WIDTH ** -0.5),
        "w_mix_out": nrm(ks[18], (D, D), D ** -0.5),
        "g_xattn": gain(ks[19], D),
        "g_mem": gain(ks[20], D),
        "w_xq": nrm(ks[21], (D, D), D ** -0.5),
        "w_xkv": nrm(ks[22], (D, 2 * D), D ** -0.5),
        "w_xo": nrm(ks[23], (D, D), D ** -0.5),
        "g_peer": gain(ks[24], D),
        "w_peer_q": nrm(ks[25], (D, PEER_HEADS * PEER_QUERY_DIM), D ** -0.5),
        "peer_sub_keys": nrm(ks[26], (PEER_HEADS, 2, PEER_KEYS, PEER_HALF), PEER_HALF ** -0.5),
        "peer_u": nrm(ks[27], (PEER_EXPERTS, D), D ** -0.5),
        "peer_v": nrm(ks[28], (PEER_EXPERTS, D), (PEER_HEADS * PEER_TOPK) ** -0.5),
        "g_final": gain(ks[29], D),
    }

def reference(x, mem, g_mix, w_in,
              cmp_pe_k, cmp_w1_k, cmp_b1_k, cmp_w2_k,
              cmp_pe_v, cmp_w1_v, cmp_b1_v, cmp_w2_v,
              gmlp_ln_g, gmlp_ln_b, gmlp_ws, gmlp_bs,
              w_nsa_out, w_gmlp_out, w_mix_out,
              g_xattn, g_mem, w_xq, w_xkv, w_xo,
              g_peer, w_peer_q, peer_sub_keys, peer_u, peer_v,
              g_final):
    B, S, D = x.shape
    G, R, dk = NSA_KV_GROUPS, NSA_HEADS_PER_GROUP, NSA_HEAD_DIM
    split_points = [int(p) for p in np.cumsum(IN_SPLITS)[:-1]]
    h = x
    for _ in range(DEPTH):
        hn = rms_norm(h, g_mix)
        proj = hn @ w_in
        (q, kc, vc, ks_, vs_, kw, vw, nsa_gate_raw,
         u_raw, v_raw, merge_raw) = jnp.split(proj, split_points, axis=-1)
        q = q.reshape(B, S, G, R, dk)
        kc, vc, ks_, vs_, kw, vw = [a.reshape(B, S, G, dk) for a in (kc, vc, ks_, vs_, kw, vw)]
        nsa_gates = jax.nn.sigmoid(nsa_gate_raw).reshape(B, S, G, R, 3)
        o_nsa = nsa_attention(q, kc, vc, ks_, vs_, kw, vw, nsa_gates,
                              cmp_pe_k, cmp_w1_k, cmp_b1_k, cmp_w2_k,
                              cmp_pe_v, cmp_w1_v, cmp_b1_v, cmp_w2_v)
        o_gmlp = chunked_gmlp(u_raw, v_raw, gmlp_ln_g, gmlp_ln_b, gmlp_ws, gmlp_bs)
        mg = jax.nn.sigmoid(merge_raw).reshape(B, S, N_BRANCHES, D)
        y = mg[:, :, 0] * (o_nsa @ w_nsa_out) + mg[:, :, 1] * (o_gmlp @ w_gmlp_out)
        h = h + y @ w_mix_out
        h = h + memory_cross_attention(rms_norm(h, g_xattn), rms_norm(mem, g_mem),
                                       w_xq, w_xkv, w_xo)
        h = h + peer_ffn(rms_norm(h, g_peer), w_peer_q, peer_sub_keys, peer_u, peer_v)
    return rms_norm(h, g_final)


_drawn_inputs = setup_inputs


def setup_inputs(seed=0):
    import zlib

    import numpy as np

    out = dict(_drawn_inputs(seed))
    spreads = {}
    factors = {'g_mix': 4.89,
     'cmp_pe_k': 8.0,
     'cmp_b1_k': 25.83,
     'cmp_pe_v': 26.117,
     'cmp_b1_v': 29.085,
     'gmlp_ln_g': 8.0,
     'gmlp_ln_b': 8.0,
     'g_xattn': 8.0,
     'g_mem': 8.0,
     'g_peer': 64.0,
     'g_final': 8.567}
    for name, (base, spread) in spreads.items():
        noise = np.random.default_rng([zlib.crc32(name.encode()), seed]).standard_normal(out[name].shape)
        drawn = base * np.exp(spread * noise) if base else spread * noise
        out[name] = __import__('jax').numpy.asarray(drawn.astype(out[name].dtype))
    for name, factor in factors.items():
        out[name] = (out[name] * factor).astype(out[name].dtype)
    return out
```

```python
import numpy as np
from contextlib import ExitStack

import concourse.bass as bass
from concourse import mybir

F32 = mybir.dt.float32
U32 = mybir.dt.uint32
ALU = mybir.AluOpType
ACT = mybir.ActivationFunctionType
AX = mybir.AxisListType

P = 128
S = 512
D = 1024
NT = S // P
KD = D // P
MEM = 256
NM = MEM // P
HEADS, DK, GROUPS = 8, 64, 2
BLOCK, STRIDE = 32, 16
NCMP = S // STRIDE - BLOCK // STRIDE + 1
HID = 256
GW = 512
XH, XD = 4, 256
PH, TOPK, KEYS = 8, 16, 128
EPS = 1e-6
NEG = -1e30
TINY = 1e-30
DK_SCALE = DK ** -0.5
XD_SCALE = XD ** -0.5

GE = 4
NG = TOPK // GE
UG, VG = 4, 2

PANELS = [("q", 0), ("kvc", 1), ("kvsw", 2), ("v", 3), ("w1k", 0), ("w1v", 1), ("u", 2),
          ("nsa_out", 3), ("gmlp_out", 0), ("merge0", 1), ("merge1", 2), ("merge2", 1), ("merge3", 2),
          ("mix0", 3), ("mix1", 0), ("xkv0", 1), ("xkv1", 2), ("xkv2", 3), ("xkv3", 0),
          ("xq0", 1), ("xq1", 2), ("xo0", 3), ("xo1", 0)]
NSLOT = 4


LAST_RESULT = {"q": ("q", 3), "kvc": ("kvc", 3), "kvsw": ("vsw", NT - 1), "v": ("v", NT - 1), "w1k": ("hid", 0),
               "w1v": ("hid", 1), "u": ("u", 3), "nsa_out": ("m1", KD - 1), "gmlp_out": ("m1", KD - 1),
               "merge0": ("m1", 1), "merge1": ("m1", 3), "merge2": ("m1", 5), "merge3": ("m1", 7),
               "mix0": ("mix", 0, NT - 1), "mix1": ("mix", 1, NT - 1), "xkv0": ("xk", 3), "xkv1": ("xk", 7),
               "xkv2": ("xv", 0, NM - 1), "xkv3": ("xv", 1, NM - 1), "xq0": ("xqt", 3), "xq1": ("xqt", 7)}


def slot_turns():
    seen, last, out = [0] * NSLOT, [None] * NSLOT, {}
    for name, s in PANELS:
        out[name] = (s, seen[s], last[s])
        seen[s] += 1
        last[s] = name
    return out


def psum_turns():
    names = []
    for t in range(NT):
        names += [("turn", t, 0), ("turn", t, 1)]
    names += [("q", c) for c in range(4)] + [("kvc", c) for c in range(4)] + [("ks",), ("kw",)]
    names += [("vsw", t) for t in range(NT)] + [("gates",)] + [("v", t) for t in range(NT)]
    names += [("hid", 0), ("hid", 1)] + [("u", c) for c in range(4)]
    names += [("kcmp",), ("vcmp",)] + [("spatial", t) for t in range(NT)]
    for t in range(NT):
        names += [("cs", t, 0), ("cs", t, 1), ("cpt", t, 0), ("cpt", t, 1), ("co", t)]
    names += attention_names()
    names += [("ot", t) for t in range(NT)]
    for c in range(KD):
        names += [("a", c), ("b", c), ("m0", c), ("m1", c)]
    for j in range(2):
        names += [("mix", j, t) for t in range(NT)]
    for t in range(NM):
        names += [("turn", NT + t, 0), ("turn", NT + t, 1)]
    names += [("xk", c) for c in range(KD)]
    for j in range(2):
        names += [("xv", j, t) for t in range(NM)]
    for t in range(NT):
        names += [("turn", NT + NM + t, 0), ("turn", NT + NM + t, 1)]
    names += [("xqt", c) for c in range(KD)]
    for e in range(XH * NT + 2):
        if e < XH * NT:
            names += [("xs", e)]
        if e >= 2:
            names += [("xpt", e - 2)]
            if (e - 2) % NT == NT - 1:
                names += [("xot", (e - 2) // NT, 0), ("xot", (e - 2) // NT, 1)]
    for j in range(2):
        names += [("xo", j, t) for t in range(NT)]
    for t in range(NT):
        names += [("turn", 2 * NT + NM + t, 0), ("turn", 2 * NT + NM + t, 1)]
    out = {n: (i % 8, i // 8, names[i - 8] if i >= 8 else None) for i, n in enumerate(names)}
    return out, names[-8:]


def units():
    return [(t, br, h) for t in range(NT) for br in (1, 2) for h in range(HEADS)]


def attention_names():
    n, names = len(units()), []
    for i in range(n + 2):
        if i < n:
            names.append(("s", i))
        if 1 <= i <= n:
            names.append(("pt", i - 1))
        if i >= 2:
            names.append(("o", i - 2))
    return names


def at_least(eng, sem, value):
    if not isinstance(value, int) or value > 0:
        eng.wait_ge(sem, value)


def stand(eng, sem, value):
    at_least(eng, sem, value)
    if not isinstance(value, int):
        eng.nop(nofuse=True)


class Chain:

    def __init__(self, eng, sem):
        self.eng, self.sem, self.base, self.n = eng, sem, 0, 0

    def step(self, ins):
        ins.then_inc(self.sem, 1)
        self.n += 1

    def join(self):
        stand(self.eng, self.sem, self.base + self.n)

    def link(self, ins):
        self.step(ins)
        self.join()


def hybrid_block(nc, x, mem, gains, w_panels, w_gates, cmp_pe, cmp_b1, cmp_w2, ln_gb, ws_t, bs, peer_w,
                 peer_u, peer_v, out):
    ctx = ExitStack()
    with ctx:
        BASE = 16640

        def at(name, shape, kb, dt=F32):
            return nc.alloc_sbuf_tensor_at(name, shape, dt, offset=BASE + int(kb * 1024))

        ctx.enter_context(nc.sbuf_tensor("arena", [P, 52992], F32))

        h = at("h", [P, NT, D], 0)
        hnT = at("hnT", [P, KD, S], 16)
        W = [at(f"W{s}", [P, 4096], 40 + 16 * s) for s in range(NSLOT)]
        small_at = [32.0]

        def small(name, shape, dt=F32):
            n = int(np.prod(shape[1:])) * 4
            n = (n + 31) // 32 * 32
            v = at(name, shape, small_at[0], dt)
            small_at[0] += n / 1024
            assert small_at[0] <= 40
            return v

        ident = small("ident", [P, P])
        wg = small("wg", [P, KD, 24])
        gates = small("gates", [P, NT, 24])
        pe_sb = small("pe_sb", [P, 2, BLOCK // 2])
        b1_sb = small("b1_sb", [P, 2, 2])
        w2_sb = small("w2_sb", [P, 2, 2, DK])
        hidT = small("hidT", [P, 2, 2, GROUPS * NCMP])
        kcT = small("kcT", [P, NCMP])
        vc = small("vc", [NCMP, GROUPS, DK])
        cmask = small("cmask", [P, NT, NCMP])
        ckeep = small("ckeep", [P, NT, NCMP])
        ssq = small("ssq", [P, 20])
        rms = small("rms", [P, 20])
        rinv = small("rinv", [P, 20])
        vsum = small("vsum", [P, 4, NT])
        cst = small("cst", [P, 4, HEADS])
        rmax = small("rmax", [P, 64])
        nmax = small("nmax", [P, 64])
        rsum = small("rsum", [P, 64])
        coef = small("coef", [P, 64])
        xst = small("xst", [P, 4, XH * NT])
        eps_col = small("eps_col", [P, 1])
        iota16 = small("iota16", [P, TOPK])

        qT = at("qT", [P, 4, S], 104)
        ksT = at("ksT", [P, S], 112)
        kwT = at("kwT", [P, S], 114)
        vsw = at("vsw", [P, NT, 2, P], 116)
        blk = at("blk", [P, 2, BLOCK // 2, GROUPS, NCMP], 120)
        oT = at("oT", [P, 4, S], 120)
        vn = at("vn", [P, NT, GW], 128)
        uT = at("uT", [P, 4, S], 136)
        ogT = at("ogT", [P, 4, S], 144)
        otok = at("otok", [P, NT, GW], 152)
        sm = at("sm", [P, 3, S], 160)
        pr = at("pr", [P, 3, S], 166)
        pt = at("pt", [P, 2, S], 172)
        yT = at("yT", [P, KD, S], 160)
        causal = at("causal", [P, 7 * P], 176)
        ln_sb = at("ln_sb", [P, 2, GW], 180)
        xn = at("xn", [P, 2, D], 184)
        sg = at("sg", [P, 2, 2, S], 184)
        junk = at("junk", [P, D], 136)
        junk_peer = at("junk_peer", [P, D], 176)
        wsT = at("wsT", [P, 4, P], 192)
        bs_sb = at("bs_sb", [P, 4, P], 194)
        gv = at("gv", [P, GW], 196)
        gb = at("gb", [P, 2, D], 198)
        xkT = at("xkT", [P, KD, MEM], 104)
        xv = at("xv", [P, NM, D], 112)
        xqT = at("xqT", [P, KD, S], 120)
        xoT = at("xoT", [P, KD, S], 136)
        mnT = at("mnT", [P, KD, MEM], 152)
        xpT = at("xpT", [P, 2, NM, S], 152)
        mtok = at("mtok", [P, NM, D], 176)
        xp = at("xp", [P, 2, MEM], 192)
        xpn = at("xpn", [P, 2, MEM], 194)
        U = at("U", [P, UG * GE, D], 40)
        V = [at(f"V{g}", [P, GE, D], kb) for g, kb in enumerate((104, 136))]
        hp = at("hp", [P, NT, D], 120)
        pq = at("pq", [P, 2, S], 152)
        diag = at("diag", [P, 2, GE, P], 156)
        pw = at("pw", [P, 9, 256], 160)
        eidx = at("eidx", [P, NT, TOPK], 170, U32)
        row_no = at("row_no", [P, NT, TOPK], 170.25, U32)
        gate = at("gate", [P, NT, TOPK], 171)
        sc_rest = at("sc_rest", [P, 2, KEYS], 176)
        cand = at("cand", [P, TOPK, TOPK], 177)
        cand_rest = at("cand_rest", [P, TOPK * TOPK], 178)
        hot = at("hot", [P, 2, TOPK, TOPK], 179)
        picked = at("picked", [P, 2, TOPK, TOPK], 181)
        hv = at("hv", [P, 2, TOPK], 183)
        hi = at("hi", [P, 2, TOPK], 183.25, U32)
        hif = at("hif", [P, 2, TOPK], 183.5)
        best = at("best", [P, TOPK], 183.75)
        pos = at("pos", [P, TOPK], 184, U32)
        ij = at("ij", [P, 2, TOPK], 184.25, U32)
        ijf = at("ijf", [P, 2, TOPK], 184.5)
        sel = at("sel", [P, 2, TOPK], 184.75)
        ex = at("ex", [P, TOPK], 185)
        pst = at("pst", [P, 4], 185.25)
        dot = at("dot", [P, TOPK], 185.5)
        gel = at("gel", [P, TOPK], 185.75)
        wgt = at("wgt", [P, TOPK], 186)

        bank = ctx.enter_context(nc.psum_tensor("bank", [P, 8, 512], F32))

        def sem(name):
            return ctx.enter_context(nc.semaphore(name))

        panel_loaded = [sem(f"panel_loaded{s}") for s in range(NSLOT)]
        bank_filled = [sem(f"bank_filled{b}") for b in range(8)]
        x_loaded = [sem(f"x_loaded{t}") for t in range(NT)]
        mem_loaded, gain_loaded, small_loaded = sem("mem_loaded"), [sem("gain0"), sem("gain1")], sem("small_loaded")
        consts_ready = sem("consts_ready")
        rms_ready, normed, turned_act, turned_dve = sem("rms_ready"), sem("normed"), sem("turned_act"), sem("turned_dve")
        spatial_read, cs_read, co_read, s_read, a_read, b_read = (sem("spatial_read"), sem("cs_read"), sem("co_read"),
                                                                  sem("s_read"), sem("a_read"), sem("b_read"))
        q_ready, blk_ready, kt_ready, vsw_ready = sem("q_ready"), sem("blk_ready"), sem("kt_ready"), sem("vsw_ready")
        gates_ready, v_gelu, v_centred, v_std = sem("gates_ready"), sem("v_gelu"), sem("v_centred"), sem("v_std")
        vn_ready, hid_ready, u_ready, cmp_ready = sem("vn_ready"), sem("hid_ready"), sem("u_ready"), sem("cmp_ready")
        og_ready, cs_ready, cexp_ready, cp_ready, cpt_ready = (sem("og_ready"), sem("cs_ready"), sem("cexp_ready"),
                                                              sem("cp_ready"), sem("cpt_ready"))
        nmax_ready, probs_ready, pt_ready, o_added = sem("nmax_ready"), sem("probs_ready"), sem("pt_ready"), sem("o_added")
        ot_ready, mg_ready, y_ready, h1_ready = sem("ot_ready"), sem("mg_ready"), sem("y_ready"), sem("h1_ready")
        xk_ready, xv_ready, xq_ready = sem("xk_ready"), sem("xv_ready"), sem("xq_ready")
        xnmax_ready, xexp_ready, xp_ready, xpt_ready, xo_ready, h2_ready = (
            sem("xnmax_ready"), sem("xexp_ready"), sem("xp_ready"), sem("xpt_ready"), sem("xo_ready"), sem("h2_ready"))
        pw_loaded, proj_done, pq_ready, scores_done = (
            sem("pw_loaded"), sem("proj_done"), sem("pq_ready"), sem("scores_done"))
        picks_taken, picks_ready, soft_bias, soft_exp, gate_ready = sem("picks_taken"), sem("picks_ready"), sem("soft_bias"), sem("soft_exp"), sem("gate_ready")
        u_loaded = [sem(f"u_loaded{g}") for g in range(UG)]
        v_loaded = [sem(f"v_loaded{g}") for g in range(VG)]
        dots_done, gelu_done, w_ready, diag_ready, v_used = (
            sem("dots_done"), sem("gelu_done"), sem("w_ready"), sem("diag_ready"), sem("v_used"))
        out_done, out_added, final_ss, final_ready, stored = (
            sem("out_done"), sem("out_added"), sem("final_ss"), sem("final_ready"), sem("stored"))
        dve_chain, act_chain, pool_chain, dve_peer = sem("dve_chain"), sem("act_chain"), sem("pool_chain"), sem("dve_peer")

        slot_of = slot_turns()
        bank_of, last_results = psum_turns()
        UNITS = units()
        XU = XH * NT

        def panel(name, k, n):
            return W[slot_of[name][0]][:, :].rearrange("p (k n) -> p k n", k=k, n=n)

        def has_panel(eng, name):
            s, n, _ = slot_of[name]
            eng.wait_ge(panel_loaded[s], 16 * (n + 1))

        def need(eng, name):
            b, n, _ = bank_of[name]
            eng.wait_ge(bank_filled[b], n + 1)
            return bank[:, b, :]

        def read_signal(name):
            key, i = name[0], name[1] if len(name) > 1 else 0
            j = name[2] if len(name) > 2 else 0
            return {"turn": (turned_dve if j else turned_act, i + 1), "q": (q_ready, i + 1), "kvc": (blk_ready, 4 * i + 4),
                    "ks": (kt_ready, 1), "kw": (kt_ready, 2), "vsw": (vsw_ready, i + 1), "gates": (gates_ready, 1),
                    "v": (v_gelu, i + 1), "hid": (hid_ready, 2 * i + 2), "u": (u_ready, i + 1),
                    "kcmp": (cmp_ready, 1), "vcmp": (cmp_ready, 2), "spatial": (spatial_read, i + 1),
                    "cs": (cs_read, 2 * i + j + 1), "cpt": (cpt_ready, 2 * i + j + 1), "co": (co_read, i + 1),
                    "s": (s_read, i + 1), "pt": (pt_ready, i + 1), "o": (o_added, i + 1), "ot": (ot_ready, i + 1),
                    "a": (a_read, i + 1), "b": (b_read, i + 1), "m0": (mg_ready, 2 * i + 1),
                    "m1": (mg_ready, 2 * i + 2), "mix": (h1_ready, NT * i + j + 1), "xk": (xk_ready, i + 1),
                    "xv": (xv_ready, NM * i + j + 1), "xqt": (xq_ready, i + 1), "xs": (xexp_ready, i + 1),
                    "xpt": (xpt_ready, i + 1), "xot": (xo_ready, 2 * i + j + 1),
                    "xo": (h2_ready, NT * i + j + 1)}[key]

        def free(ins, name):
            ins.then_inc(read_signal(name)[0], 1)

        def was_read(eng, name):
            eng.wait_ge(*read_signal(name))

        NORMS = [(0, NT, h, 0), (NT, NM, mtok, 1), (NT + NM, NT, h, 0), (2 * NT + NM, NT, h, 1)]

        def norm_dst(n, t):
            return hp[:, t, :] if n == 3 else xn[:, (NORMS[n][0] + t) % 2, :]

        block = ctx.enter_context(nc.Block())

        @block.sync
        def _(sp):
            def gain(slot, n):
                sp.dma_start(gb[:, slot, :], gains[n, :].partition_broadcast(P)).then_inc(gain_loaded[slot], 16)

            for t in range(NT):
                sp.dma_start(h[:, t, :], x[t * P:(t + 1) * P, :]).then_inc(x_loaded[t], 16)
                if t == 0:
                    gain(0, 0)
            smalls = [(wg[:], w_gates), (pe_sb[:], cmp_pe), (b1_sb[:], cmp_b1), (w2_sb[:], cmp_w2),
                      (ln_sb[:], ln_gb.partition_broadcast(P)), (wsT[:], ws_t), (bs_sb[:], bs.partition_broadcast(P))]
            for i, (name, s) in enumerate(PANELS):
                before = slot_of[name][2]
                if before:
                    need(sp, LAST_RESULT[before])
                sp.dma_start(W[s][:, :], w_panels[i]).then_inc(panel_loaded[s], 16)
                if i == 1:
                    for dst, src in smalls:
                        sp.dma_start(dst, src).then_inc(small_loaded, 16)
                    gain(1, 1)
                if name == "mix0":
                    sp.wait_ge(y_ready, 1)
                    for t in range(NM):
                        sp.dma_start(mtok[:, t, :], mem[t * P:(t + 1) * P, :]).then_inc(mem_loaded, 16)
                if name == "kvsw":
                    sp.wait_ge(normed, NT)
                    gain(0, 2)
                if name == "xq1":
                    sp.wait_ge(normed, NT + NM)
                    gain(1, 3)
            need(sp, ("mix", 1, NT - 1))
            sp.dma_start(pw[:], peer_w[0]).then_inc(pw_loaded, 16)
            sp.wait_ge(normed, 2 * NT + NM)
            gain(0, 4)
            with sp.Fori(1, PH) as hd:
                sp.wait_ge(scores_done, NT * hd)
                sp.dma_start(pw[:], peer_w[bass.ds(hd, 1)].rearrange("o p k n -> (o p) k n")).then_inc(pw_loaded, 16)
            for t in range(NT):
                sp.wait_ge(final_ready, t + 1)
                sp.dma_start(out[t * P:(t + 1) * P, :], hp[:, t, :]).then_inc(stored, 16)
            sp.wait_ge(stored, 16 * NT)

        @block.gpsimd
        def _(pool):
            pool.memset(ident[:], 0.0).then_inc(pool_chain, 1)
            pool.memset(causal[:], 0.0).then_inc(pool_chain, 1)
            pool.memset(cmask[:], 0.0).then_inc(pool_chain, 1)
            pool.memset(ckeep[:], 1.0).then_inc(pool_chain, 1)
            pool.memset(eps_col[:], EPS).then_inc(consts_ready, 1)
            pool.wait_ge(pool_chain, 4)
            pool.affine_select(out=ident[:], in_=ident[:], compare_op=ALU.not_equal, fill=1.0, base=0,
                               pattern=[[-1, P]], channel_multiplier=1).then_inc(consts_ready, 1)
            pool.affine_select(out=causal[:], in_=causal[:], compare_op=ALU.is_ge, fill=NEG, base=3 * P,
                               pattern=[[-1, 7 * P]], channel_multiplier=1).then_inc(consts_ready, 1)
            for m, f in ((cmask, NEG), (ckeep, 0.0)):
                pool.affine_select(out=m[:], in_=m[:], compare_op=ALU.is_ge, fill=f, base=1 - BLOCK,
                                   pattern=[[P, NT], [-STRIDE, NCMP]], channel_multiplier=1).then_inc(consts_ready, 1)
            pool.iota(iota16[:], [[1, TOPK]], base=0, channel_multiplier=0,
                      allow_small_or_imprecise_dtypes=True).then_inc(consts_ready, 1)
            pool.wait_ge(small_loaded, 16 * 7)
            pool.affine_select(out=wsT[:], in_=wsT[:], compare_op=ALU.is_ge, fill=0.0, base=0,
                               pattern=[[0, 4], [1, P]], channel_multiplier=-1).then_inc(consts_ready, 1)

            def gather(hd, t):
                b = hd * NT + t
                stand(pool, picks_ready, b + 1)
                stand(pool, v_used, NG * (b - NT + 1))
                pool.tensor_copy(row_no[:, t, :], eidx[:, t, :]).then_inc(picks_taken, 1)
                stand(pool, picks_taken, b + 1)

                def rows_u(k):
                    stand(pool, dots_done, b * NG + k - 3)
                    for j in range(GE):
                        e = k * GE + j
                        pool.indirect_dma_start(U[:, e, :], None, peer_u, bass.IndirectOffsetOnAxis(
                            ap=row_no[:, t, e:e + 1], axis=0)).then_inc(u_loaded[k], 16)

                def rows_v(k):
                    stand(pool, v_used, b * NG + k - 1)
                    for j in range(GE):
                        e = k * GE + j
                        pool.indirect_dma_start(V[k % VG][:, j, :], None, peer_v, bass.IndirectOffsetOnAxis(
                            ap=row_no[:, t, e:e + 1], axis=0)).then_inc(v_loaded[k % VG], 16)

                rows_u(0)
                rows_u(1)
                rows_v(0)
                rows_u(2)
                rows_v(1)
                rows_u(3)
                rows_v(2)
                rows_v(3)

            for t in range(NT):
                gather(0, t)
            with pool.Fori(1, PH) as hd:
                for t in range(NT):
                    gather(hd, t)

        @block.tensor
        def _(pe):
            def begin(name):
                b, _, before = bank_of[name]
                if before:
                    was_read(pe, before)
                return bank[:, b, :]

            def all_turned(tiles):
                pe.wait_ge(turned_act, tiles)
                pe.wait_ge(turned_dve, tiles)

            def filled(mm, name):
                mm.then_inc(bank_filled[bank_of[name][0]], 1)

            def turn(m):
                n = max(i for i in range(4) if NORMS[i][0] <= m)
                pe.wait_ge(normed, m + 1)
                src = norm_dst(n, m - NORMS[n][0])
                for half in range(2):
                    dst = begin(("turn", m, half))
                    for k in range(4):
                        kk = 4 * half + k
                        mm = pe.transpose(dst[:, k * P:(k + 1) * P], src[:, kk * P:(kk + 1) * P], ident[:])
                    filled(mm, ("turn", m, half))

            def rows_out(name, w, act, k_tiles, cols, width=None):
                dst = begin(name)
                if width:
                    dst = dst[:, 0:width]
                for k in range(k_tiles):
                    mm = pe.matmul(dst, w(k), act(k), start=(k == 0), stop=(k == k_tiles - 1))
                filled(mm, name)
                return mm

            def hn(k):
                return hnT[:, k, :]

            pe.wait_ge(consts_ready, 6)
            for t in range(NT):
                turn(t)
            all_turned(NT)
            for name, key in (("q", "q"), ("kvc", "kvc")):
                has_panel(pe, name)
                w = panel(name, KD, 512)
                for c in range(4):
                    rows_out((key, c), lambda k: w[:, k, c * P:(c + 1) * P], hn, KD, 512)
            has_panel(pe, "kvsw")
            w = panel("kvsw", KD, 512)
            for c, key in enumerate((("ks",), ("kw",))):
                rows_out(key, lambda k: w[:, k, c * P:(c + 1) * P], hn, KD, 512)
            for t in range(NT):
                rows_out(("vsw", t), lambda k: hnT[:, k, t * P:(t + 1) * P], lambda k: w[:, k, 256:512], KD, 256, 256)
            pe.wait_ge(small_loaded, 16 * 7)
            dst = begin(("gates",))
            for t in range(NT):
                for k in range(KD):
                    mm = pe.matmul(dst[:, t * 24:(t + 1) * 24], hnT[:, k, t * P:(t + 1) * P], wg[:, k, :],
                                   start=(k == 0), stop=(k == KD - 1))
            filled(mm, ("gates",))
            has_panel(pe, "v")
            w = panel("v", KD, 512)
            for t in range(NT):
                rows_out(("v", t), lambda k: hnT[:, k, t * P:(t + 1) * P], lambda k: w[:, k, :], KD, 512)
            for i, name in enumerate(("w1k", "w1v")):
                has_panel(pe, name)
                pe.wait_ge(blk_ready, 8 * (i + 1))
                w = panel(name, BLOCK // 2, HID)
                dst = begin(("hid", i))
                for c in range(2):
                    for k in range(BLOCK // 2):
                        mm = pe.matmul(dst[:, c * P:c * P + 2 * NCMP], w[:, k, c * P:(c + 1) * P],
                                       blk[:, i, k, :, :].rearrange("p g c -> p (g c)"),
                                       start=(k == 0), stop=(k == BLOCK // 2 - 1))
                filled(mm, ("hid", i))
            has_panel(pe, "u")
            w = panel("u", KD, 512)
            for c in range(4):
                rows_out(("u", c), lambda k: w[:, k, c * P:(c + 1) * P], hn, KD, 512)
            pe.wait_ge(hid_ready, 4)
            dst = begin(("kcmp",))
            for g in range(GROUPS):
                for c in range(2):
                    mm = pe.matmul(dst[g * DK:(g + 1) * DK, 0:NCMP], w2_sb[:, 0, c, :],
                                   hidT[:, 0, c, g * NCMP:(g + 1) * NCMP], start=(c == 0), stop=(c == 1))
            filled(mm, ("kcmp",))
            dst = begin(("vcmp",))
            for g in range(GROUPS):
                for c in range(2):
                    mm = pe.matmul(dst[0:NCMP, g * DK:(g + 1) * DK], hidT[:, 1, c, g * NCMP:(g + 1) * NCMP],
                                   w2_sb[:, 1, c, :], start=(c == 0), stop=(c == 1))
            filled(mm, ("vcmp",))
            pe.wait_ge(consts_ready, 7)
            for t in range(NT):
                pe.wait_ge(vn_ready, t + 1)
                dst = begin(("spatial", t))
                for g in range(4):
                    mm = pe.matmul(dst[:, g * P:(g + 1) * P], vn[:, t, g * P:(g + 1) * P], wsT[:, g, :],
                                   start=True, stop=True)
                filled(mm, ("spatial", t))
            pe.wait_ge(q_ready, 4)
            pe.wait_ge(cmp_ready, 2)

            def q_of(hd, t):
                g = hd // 4
                return qT[g * DK:(g + 1) * DK, hd % 4, t * P:(t + 1) * P]

            for t in range(NT):
                for g in range(GROUPS):
                    dst = begin(("cs", t, g))
                    for c in range(4):
                        mm = pe.matmul(dst[:, c * NCMP:(c + 1) * NCMP], q_of(4 * g + c, t),
                                       kcT[g * DK:(g + 1) * DK, :], start=True, stop=True)
                    filled(mm, ("cs", t, g))
                pe.wait_ge(cp_ready, t + 1)
                for half in range(2):
                    dst = begin(("cpt", t, half))
                    for j in range(4):
                        hd = 4 * half + j
                        mm = pe.transpose(dst[0:NCMP, j * P:(j + 1) * P],
                                          sm[:, t % 3, hd * NCMP:(hd + 1) * NCMP], ident[:])
                    filled(mm, ("cpt", t, half))
                pe.wait_ge(cpt_ready, 2 * (t + 1))
                dst = begin(("co", t))
                for hd in range(HEADS):
                    mm = pe.matmul(dst[:, hd * DK:(hd + 1) * DK], pt[0:NCMP, hd // 4, hd % 4 * P:(hd % 4 + 1) * P],
                                   vc[:, hd // 4, :], start=True, stop=True)
                filled(mm, ("co", t))
            pe.wait_ge(kt_ready, 2)
            pe.wait_ge(vsw_ready, NT)
            nu = len(UNITS)
            for i in range(nu + 2):
                if i < nu:
                    t, br, hd = UNITS[i]
                    g = hd // 4
                    kT = (ksT, kwT)[br - 1]
                    dst = begin(("s", i))
                    n = (t + 1) * P
                    filled(pe.matmul(dst[:, 0:n], q_of(hd, t), kT[g * DK:(g + 1) * DK, 0:n], start=True, stop=True),
                           ("s", i))
                if 1 <= i <= nu:
                    t = UNITS[i - 1][0]
                    pe.wait_ge(probs_ready, i)
                    dst = begin(("pt", i - 1))
                    for kb in range(t + 1):
                        mm = pe.transpose(dst[:, kb * P:(kb + 1) * P], pr[:, (i - 1) % 3, kb * P:(kb + 1) * P], ident[:])
                    filled(mm, ("pt", i - 1))
                if i >= 2:
                    t, br, hd = UNITS[i - 2]
                    g = hd // 4
                    pe.wait_ge(pt_ready, i - 1)
                    dst = begin(("o", i - 2))
                    for kb in range(t + 1):
                        mm = pe.matmul(dst[:, 0:DK], pt[:, (i - 2) % 2, kb * P:(kb + 1) * P],
                                       vsw[:, kb, br - 1, g * DK:(g + 1) * DK], start=(kb == 0), stop=(kb == t))
                    filled(mm, ("o", i - 2))
            for t in range(NT):
                pe.wait_ge(o_added, 16 * (t + 1))
                dst = begin(("ot", t))
                for k in range(4):
                    mm = pe.transpose(dst[:, k * P:(k + 1) * P], otok[:, t, k * P:(k + 1) * P], ident[:])
                filled(mm, ("ot", t))
            pe.wait_ge(ot_ready, NT)
            pe.wait_ge(og_ready, NT)
            has_panel(pe, "nsa_out")
            has_panel(pe, "gmlp_out")
            wa, wb = panel("nsa_out", 4, D), panel("gmlp_out", 4, D)
            for c in range(KD):
                rows_out(("a", c), lambda k: wa[:, k, c * P:(c + 1) * P], lambda k: oT[:, k, :], 4, 512)
                rows_out(("b", c), lambda k: wb[:, k, c * P:(c + 1) * P], lambda k: ogT[:, k, :], 4, 512)
                name = f"merge{c // 2}"
                has_panel(pe, name)
                w = panel(name, KD, 512)
                for i in range(2):
                    at_col = (2 * i + c % 2) * P
                    rows_out((f"m{i}", c), lambda k: w[:, k, at_col:at_col + P], hn, KD, 512)
            pe.wait_ge(y_ready, KD)
            for j in range(2):
                has_panel(pe, f"mix{j}")
                w = panel(f"mix{j}", KD, 512)
                for t in range(NT):
                    rows_out(("mix", j, t), lambda k: yT[:, k, t * P:(t + 1) * P], lambda k: w[:, k, :], KD, 512)
            for t in range(NM):
                turn(NT + t)
            all_turned((NT + NM))
            for c in range(KD):
                name = f"xkv{c // 4}"
                if c % 4 == 0:
                    has_panel(pe, name)
                w = panel(name, KD, 512)
                rows_out(("xk", c), lambda k: w[:, k, c % 4 * P:(c % 4 + 1) * P], lambda k: mnT[:, k, :], KD, MEM, MEM)
            for j in range(2):
                name = f"xkv{2 + j}"
                has_panel(pe, name)
                w = panel(name, KD, 512)
                for t in range(NM):
                    rows_out(("xv", j, t), lambda k: mnT[:, k, t * P:(t + 1) * P], lambda k: w[:, k, :], KD, 512)
            for t in range(NT):
                turn(NT + NM + t)
            all_turned((2 * NT + NM))
            for c in range(KD):
                name = f"xq{c // 4}"
                if c % 4 == 0:
                    has_panel(pe, name)
                w = panel(name, KD, 512)
                rows_out(("xqt", c), lambda k: w[:, k, c % 4 * P:(c % 4 + 1) * P], hn, KD, 512)
            pe.wait_ge(xk_ready, KD)
            pe.wait_ge(xv_ready, 2 * NM)
            for e in range(XU + 2):
                if e < XU:
                    hd, t = divmod(e, NT)
                    pe.wait_ge(xq_ready, 2 * (hd + 1))
                    dst = begin(("xs", e))
                    for k in range(2):
                        mm = pe.matmul(dst[:, 0:MEM], xqT[:, 2 * hd + k, t * P:(t + 1) * P], xkT[:, 2 * hd + k, :],
                                       start=(k == 0), stop=(k == 1))
                    filled(mm, ("xs", e))
                if e >= 2:
                    hd, t = divmod(e - 2, NT)
                    pe.wait_ge(xp_ready, e - 1)
                    dst = begin(("xpt", e - 2))
                    for m in range(NM):
                        mm = pe.transpose(dst[:, m * P:(m + 1) * P], xpn[:, e % 2, m * P:(m + 1) * P], ident[:])
                    filled(mm, ("xpt", e - 2))
                    if t == NT - 1:
                        pe.wait_ge(xpt_ready, e - 1)
                        for c in range(2):
                            rows_out(("xot", hd, c), lambda m: xv[:, m, hd * XD + c * P:hd * XD + (c + 1) * P],
                                     lambda m: xpT[:, hd % 2, m, :], NM, 512)
            pe.wait_ge(xo_ready, KD)
            for j in range(2):
                has_panel(pe, f"xo{j}")
                w = panel(f"xo{j}", KD, 512)
                for t in range(NT):
                    rows_out(("xo", j, t), lambda k: xoT[:, k, t * P:(t + 1) * P], lambda k: w[:, k, :], KD, 512)
            for t in range(NT):
                turn(2 * NT + NM + t)
            all_turned((3 * NT + NM))
            for name in last_results:
                was_read(pe, name)

            def project(hd, p):
                if p == 0:
                    pe.wait_ge(pw_loaded, 16 * (hd + 1))
                for k in range(KD):
                    mm = pe.matmul(bank[:, p, :], pw[:, k, p * P:(p + 1) * P], hnT[:, k, :],
                                   start=(k == 0), stop=(k == KD - 1))
                mm.then_inc(proj_done, 1)

            def scores(hd):
                pe.wait_ge(pq_ready, 2 * (hd + 1))
                at_least(pe, gate_ready, hd * NT)
                for t in range(NT):
                    for p in range(2):
                        mm = pe.matmul(bank[:, 2 + t // 2, (t % 2 * 2 + p) * KEYS:(t % 2 * 2 + p + 1) * KEYS],
                                       pq[:, p, t * P:(t + 1) * P], pw[:, KD, p * P:(p + 1) * P],
                                       start=True, stop=True)
                    mm.then_inc(scores_done, 1)

            def mix(hd, t, k):
                b = hd * NT + t
                G = b * NG + k
                pe.wait_ge(v_loaded[k % VG], 16 * GE * (2 * b + k // VG + 1))
                pe.wait_ge(diag_ready, G + 1)
                if k == 0:
                    at_least(pe, out_added, b - 1)
                for j in range(GE):
                    for n in range(2):
                        mm = pe.matmul(bank[:, 4 + 2 * (t % 2) + n, :], diag[:, k % 2, j, :],
                                       V[k % VG][:, j, n * 512:(n + 1) * 512],
                                       start=(k == 0 and j == 0), stop=(k == NG - 1 and j == GE - 1))
                mm.then_inc(v_used, 1)

            def head(hd, more):
                for t in range(NT):
                    for k in range(NG):
                        mix(hd, t, k)
                        if more and t == 0 and k in (0, 1):
                            project(hd + 1, k)
                        if more and t == 0 and k == 2:
                            scores(hd + 1)

            project(0, 0)
            project(0, 1)
            scores(0)
            head(0, True)
            with pe.Fori(1, PH - 1) as hd:
                head(hd, True)
            head(PH - 1, False)

        @block.scalar
        def _(act):
            link = Chain(act, act_chain)

            def rms_of(m, src, waste=None):
                link.link(act.activation((waste or junk)[:], src, ACT.Square, accum_out=ssq[:, m:m + 1]))
                act.activation(rms[:, m:m + 1], ssq[:, m:m + 1], ACT.Sqrt, bias=eps_col[:], scale=1.0 / D)\
                   .then_inc(rms_ready, 1)

            def copy_turned(m):
                n = max(i for i in range(4) if NORMS[i][0] <= m)
                t = m - NORMS[n][0]
                dst = (mnT if n == 1 else hnT)[:, 0:4, t * P:(t + 1) * P]
                src = need(act, ("turn", m, 0)).rearrange("p (k n) -> p k n", k=4)
                free(act.activation(dst, src, ACT.Copy), ("turn", m, 0))

            act.wait_ge(consts_ready, 6)
            for t in range(NT):
                act.wait_ge(x_loaded[t], 16)
                rms_of(t, h[:, t, :])
            for t in range(NT):
                copy_turned(t)
            for c in range(4):
                src = need(act, ("q", c))
                free(act.activation(qT[:, c, :], src, ACT.Copy), ("q", c))
            for key, dst in ((("ks",), ksT), (("kw",), kwT)):
                src = need(act, key)
                free(act.activation(dst[:], src, ACT.Copy), key)
            src = need(act, ("gates",))
            free(act.activation(gates[:].rearrange("p t n -> p (t n)"), src[:, 0:NT * 24], ACT.Sigmoid),
                  ("gates",))
            for t in range(NT):
                src = need(act, ("v", t))
                at_least(act, v_centred, t)
                free(act.activation(gv[:], src, ACT.Gelu, accum_out=vsum[:, 0, t:t + 1]), ("v", t))
                act.wait_ge(v_centred, t + 1)
                act.activation(vsum[:, 3, t:t + 1], vsum[:, 2, t:t + 1], ACT.Sqrt, bias=eps_col[:],
                               scale=1.0 / GW).then_inc(v_std, 1)
            act.wait_ge(small_loaded, 16 * 7)
            for i in range(2):
                src = need(act, ("hid", i))
                for c in range(2):
                    ins = act.activation(hidT[:, i, c, :], src[:, c * P:c * P + 2 * NCMP], ACT.Gelu,
                                         bias=b1_sb[:, i, c:c + 1])
                    ins.then_inc(hid_ready, 1)
            for c in range(4):
                src = need(act, ("u", c))
                free(act.activation(uT[:, c, :], src, ACT.Gelu), ("u", c))
            for t in range(NT):
                act.wait_ge(cs_ready, t + 1)
                act.activation(sm[:, t % 3, 0:HEADS * NCMP], sm[:, t % 3, 0:HEADS * NCMP], ACT.Exp,
                               scale=DK_SCALE).then_inc(cexp_ready, 1)
                if t:
                    need(act, ("co", t - 1))
                for half in range(2):
                    src = need(act, ("cpt", t, half))
                    free(act.activation(pt[0:NCMP, half, :], src[0:NCMP, :], ACT.Copy), ("cpt", t, half))
            need(act, ("co", NT - 1))
            nu = len(UNITS)
            for i in range(nu + 1):
                if i < nu:
                    n = (UNITS[i][0] + 1) * P
                    act.wait_ge(nmax_ready, i + 1)
                    if i >= 3:
                        need(act, ("pt", i - 3))
                    act.activation(pr[:, i % 3, 0:n], sm[:, i % 3, 0:n], ACT.Exp, bias=nmax[:, i:i + 1],
                                   scale=DK_SCALE, accum_out=rsum[:, i:i + 1]).then_inc(probs_ready, 1)
                if i >= 1:
                    n = (UNITS[i - 1][0] + 1) * P
                    src = need(act, ("pt", i - 1))
                    if i >= 3:
                        need(act, ("o", i - 3))
                    free(act.activation(pt[:, (i - 1) % 2, 0:n], src[:, 0:n], ACT.Copy), ("pt", i - 1))
            for t in range(NT):
                src = need(act, ("ot", t)).rearrange("p (k n) -> p k n", k=4)
                free(act.activation(oT[:, :, t * P:(t + 1) * P], src, ACT.Copy), ("ot", t))
            for c in range(KD):
                at_least(act, y_ready, c - 1)
                for i in range(2):
                    src = need(act, (f"m{i}", c))
                    free(act.activation(sg[:, c % 2, i, :], src, ACT.Sigmoid), (f"m{i}", c))
            act.wait_ge(y_ready, KD)
            act.wait_ge(mem_loaded, 16 * NM)
            for t in range(NM):
                rms_of(NT + t, mtok[:, t, :])
            for t in range(NT):
                act.wait_ge(h1_ready, NT + t + 1)
                rms_of(NT + NM + t, h[:, t, :])
            for t in range(NM):
                copy_turned(NT + t)
            for c in range(KD):
                src = need(act, ("xk", c))
                free(act.activation(xkT[:, c, :], src[:, 0:MEM], ACT.Copy), ("xk", c))
            for t in range(NT):
                copy_turned(NT + NM + t)
            for c in range(KD):
                src = need(act, ("xqt", c))
                free(act.activation(xqT[:, c, :], src, ACT.Copy), ("xqt", c))
            for e in range(XU + 2):
                if e < XU:
                    src = need(act, ("xs", e))
                    act.wait_ge(xnmax_ready, e + 1)
                    at_least(act, xp_ready, e - 1)
                    free(act.activation(xp[:, e % 2, :], src[:, 0:MEM], ACT.Exp, bias=xst[:, 1, e:e + 1],
                                         scale=XD_SCALE, accum_out=xst[:, 2, e:e + 1]), ("xs", e))
                if e >= 2:
                    hd, t = divmod(e - 2, NT)
                    src = need(act, ("xpt", e - 2)).rearrange("p (m n) -> p m n", n=P)
                    if hd >= 2 and t == 0:
                        need(act, ("xot", hd - 2, 1))
                    free(act.activation(xpT[:, hd % 2, :, t * P:(t + 1) * P], src[:, 0:NM, :], ACT.Copy),
                          ("xpt", e - 2))
            for t in range(NT):
                act.wait_ge(h2_ready, NT + t + 1)
                rms_of(2 * NT + NM + t, h[:, t, :], junk_peer)
            for t in range(NT):
                copy_turned(2 * NT + NM + t)

            def copy_query(hd, p):
                act.wait_ge(proj_done, 2 * hd + p + 1)
                act.activation(pq[:, p, :], bank[:, p, :], ACT.Copy).then_inc(pq_ready, 1)

            def soft(hd, t):
                act.wait_ge(soft_bias, hd * NT + t + 1)
                act.activation(ex[:], best[:], ACT.Exp, bias=pst[:, 0:1], accum_out=pst[:, 1:2])\
                   .then_inc(soft_exp, 1)

            def gelus(hd, t, k):
                act.wait_ge(dots_done, (hd * NT + t) * NG + k + 1)
                act.activation(gel[:, k * GE:(k + 1) * GE], dot[:, k * GE:(k + 1) * GE], ACT.Gelu)\
                   .then_inc(gelu_done, 1)

            def diags(hd, t, k):
                G = (hd * NT + t) * NG + k
                act.wait_ge(w_ready, G + 1)
                at_least(act, v_used, G - 1)
                for j in range(GE):
                    ins = act.activation(diag[:, k % 2, j, :], ident[:], ACT.Copy,
                                         scale=wgt[:, k * GE + j:k * GE + j + 1])
                ins.then_inc(diag_ready, 1)

            def head(hd, more):
                for t in range(NT):
                    for k in range(NG):
                        gelus(hd, t, k)
                        if k:
                            diags(hd, t, k - 1)
                        if more and t == 0 and k >= 2:
                            copy_query(hd + 1, k - 2)
                    diags(hd, t, NG - 1)
                    if more:
                        soft(hd + 1, t)

            copy_query(0, 0)
            copy_query(0, 1)
            for t in range(NT):
                soft(0, t)
            head(0, True)
            with act.Fori(1, PH - 1) as hd:
                head(hd, True)
            head(PH - 1, False)
            for t in range(NT):
                act.wait_ge(out_added, (PH - 1) * NT + t + 1)
                rms_of(3 * NT + NM + t, h[:, t, :], junk_peer)

        @block.vector
        def _(dve):
            link = Chain(dve, dve_chain)

            def normalise(m, src, gain_slot, dst, signal):
                dve.wait_ge(rms_ready, m + 1)
                link.link(dve.reciprocal(rinv[:, m:m + 1], rms[:, m:m + 1]))
                dve.scalar_tensor_tensor(out=dst, in0=src, scalar=rinv[:, m:m + 1], in1=gb[:, gain_slot, :],
                                         op0=ALU.mult, op1=ALU.mult).then_inc(signal, 1)

            def norm(n, t):
                first, _, src, slot = NORMS[n]
                m = first + t
                if n < 3 and m >= 2:
                    need(dve, ("turn", m - 2, 1))
                normalise(m, src[:, t, :], slot, norm_dst(n, t), normed)

            def copy_turned(m):
                n = max(i for i in range(4) if NORMS[i][0] <= m)
                t = m - NORMS[n][0]
                dst = (mnT if n == 1 else hnT)[:, 4:8, t * P:(t + 1) * P]
                src = need(dve, ("turn", m, 1)).rearrange("p (k n) -> p k n", k=4)
                free(dve.tensor_copy(dst, src), ("turn", m, 1))

            dve.wait_ge(gain_loaded[0], 16)
            for t in range(NT):
                dve.wait_ge(x_loaded[t], 16)
                norm(0, t)
            for t in range(NT):
                copy_turned(t)
            dve.wait_ge(small_loaded, 16 * 7)
            for i in range(2):
                for g in range(GROUPS):
                    src = need(dve, ("kvc", 2 * i + g))
                    for par in range(2):
                        rows = slice(par * DK, (par + 1) * DK)
                        tok = src[rows, :].rearrange("p (c l q) -> p q l c", q=2, l=STRIDE // 2)[:, par, :, :]
                        for part in range(2):
                            ls = slice(part * STRIDE // 2, (part + 1) * STRIDE // 2)
                            pe_b = pe_sb[rows, i, ls].unsqueeze(2).broadcast_to([DK, STRIDE // 2, NCMP])
                            dve.tensor_tensor(blk[rows, i, ls, g, :], tok[:, :, part:part + NCMP], pe_b, ALU.add)\
                               .then_inc(blk_ready, 1)
            for t in range(NT):
                src = need(dve, ("vsw", t))
                free(dve.tensor_copy(vsw[:, t, :, :].rearrange("p b n -> p (b n)"), src[:, 0:256]), ("vsw", t))
            for t in range(NT):
                dve.wait_ge(v_gelu, t + 1)
                link.link(dve.tensor_scalar(vsum[:, 1, t:t + 1], vsum[:, 0, t:t + 1], -1.0 / GW, None, ALU.mult))
                link.link(dve.tensor_scalar(vn[:, t, :], gv[:], vsum[:, 1, t:t + 1], None, ALU.add))
                dve.tensor_tensor_reduce(out=gv[:], in0=vn[:, t, :], in1=vn[:, t, :], scale=1.0, scalar=0.0,
                                         op0=ALU.mult, op1=ALU.add, accum_out=vsum[:, 2, t:t + 1])\
                   .then_inc(v_centred, 1)
                dve.wait_ge(v_std, t + 1)
                link.link(dve.reciprocal(vsum[:, 0, t:t + 1], vsum[:, 3, t:t + 1]))
                link.link(dve.scalar_tensor_tensor(out=vn[:, t, :], in0=vn[:, t, :], scalar=vsum[:, 0, t:t + 1],
                                                   in1=ln_sb[:, 0, :], op0=ALU.mult, op1=ALU.mult))
                dve.tensor_tensor(vn[:, t, :], vn[:, t, :], ln_sb[:, 1, :], ALU.add).then_inc(vn_ready, 1)
            src = need(dve, ("kcmp",))
            free(dve.tensor_copy(kcT[:], src[:, 0:NCMP]), ("kcmp",))
            src = need(dve, ("vcmp",))
            free(dve.tensor_copy(vc[:].rearrange("p g n -> p (g n)"), src[0:NCMP, 0:GROUPS * DK]), ("vcmp",))
            dve.wait_ge(u_ready, 4)
            for t in range(NT):
                src = need(dve, ("spatial", t))
                tmp = gv[:].rearrange("p (g n) -> p g n", g=4)
                at_least(dve, og_ready, t)
                ins = dve.tensor_tensor(gv[:], src, bs_sb[:].rearrange("p g n -> p (g n)"), ALU.add)
                free(ins, ("spatial", t))
                was_read(dve, ("spatial", t))
                cols = slice(t * P, (t + 1) * P)
                dve.tensor_tensor(ogT[:, :, cols], tmp, uT[:, :, cols], ALU.mult).then_inc(og_ready, 1)
            dve.wait_ge(gates_ready, 1)
            for t in range(NT):
                s8 = sm[:, t % 3, 0:HEADS * NCMP].rearrange("p (h c) -> p h c", h=HEADS)
                shape = [P, HEADS, NCMP]
                mask = cmask[:, t, :].unsqueeze(1).broadcast_to([P, 4, NCMP])
                keep = ckeep[:, t, :].unsqueeze(1).broadcast_to(shape)
                for g in range(GROUPS):
                    src = need(dve, ("cs", t, g))[:, 0:4 * NCMP].rearrange("p (h c) -> p h c", h=4)
                    free(dve.tensor_tensor(s8[:, 4 * g:4 * g + 4, :], src, mask, ALU.add), ("cs", t, g))
                was_read(dve, ("cs", t, 1))
                link.link(dve.tensor_reduce(cst[:, 0, :], s8, AX.X, ALU.max))
                dve.tensor_tensor(s8, s8, cst[:, 0, :].unsqueeze(2).broadcast_to(shape), ALU.subtract)\
                   .then_inc(cs_ready, 1)
                dve.wait_ge(cexp_ready, t + 1)
                dve.tensor_tensor(s8, s8, keep, ALU.mult).then_inc(cp_ready, 1)
                dve.wait_ge(cp_ready, t + 1)
                link.link(dve.tensor_reduce(cst[:, 1, :], s8, AX.X, ALU.add))
                link.link(dve.tensor_scalar(cst[:, 2, :], cst[:, 1, :], TINY, None, ALU.max))
                link.link(dve.reciprocal(cst[:, 3, :], cst[:, 2, :]))
                gate_c = gates[:, t, :].rearrange("p (h b) -> p h b", b=3)[:, :, 0]
                link.link(dve.tensor_tensor(cst[:, 2, :], cst[:, 3, :], gate_c, ALU.mult))
                src = need(dve, ("co", t)).rearrange("p (h d) -> p h d", h=HEADS)
                free(dve.tensor_tensor(otok[:, t, :].rearrange("p (h d) -> p h d", h=HEADS), src,
                                       cst[:, 2, :].unsqueeze(2).broadcast_to([P, HEADS, DK]), ALU.mult), ("co", t))
                was_read(dve, ("co", t))
            nu = len(UNITS)
            for i in range(nu + 2):
                if i < nu:
                    t = UNITS[i][0]
                    n = (t + 1) * P
                    src = need(dve, ("s", i))
                    if i >= 3:
                        dve.wait_ge(probs_ready, i - 2)
                    free(dve.tensor_tensor_reduce(out=sm[:, i % 3, 0:n], in0=src[:, 0:n],
                                                  in1=causal[:, (3 - t) * P:(3 - t) * P + n], scale=1.0, scalar=NEG,
                                                  op0=ALU.add, op1=ALU.max, accum_out=rmax[:, i:i + 1]), ("s", i))
                    was_read(dve, ("s", i))
                    dve.tensor_scalar(nmax[:, i:i + 1], rmax[:, i:i + 1], -DK_SCALE, None, ALU.mult)\
                       .then_inc(nmax_ready, 1)
                if i >= 2:
                    t, br, hd = UNITS[i - 2]
                    dve.wait_ge(probs_ready, i - 1)
                    link.link(dve.reciprocal(coef[:, i - 2:i - 1], rsum[:, i - 2:i - 1]))
                    link.link(dve.tensor_tensor(coef[:, i - 2:i - 1], coef[:, i - 2:i - 1],
                                                gates[:, t, 3 * hd + br:3 * hd + br + 1], ALU.mult))
                    src = need(dve, ("o", i - 2))
                    if br == 2:
                        dve.wait_ge(o_added, i - 2 - HEADS + 1)
                    o = otok[:, t, hd * DK:(hd + 1) * DK]
                    free(dve.scalar_tensor_tensor(out=o, in0=src[:, 0:DK], scalar=coef[:, i - 2:i - 1], in1=o,
                                                   op0=ALU.mult, op1=ALU.add), ("o", i - 2))
            for c in range(KD):
                dve.wait_ge(mg_ready, 2 * c + 2)
                src = need(dve, ("a", c))
                free(dve.tensor_tensor(yT[:, c, :], src, sg[:, c % 2, 0, :], ALU.mult), ("a", c))
                src = need(dve, ("b", c))
                free(dve.tensor_tensor(sg[:, c % 2, 1, :], src, sg[:, c % 2, 1, :], ALU.mult), ("b", c))
                was_read(dve, ("a", c))
                was_read(dve, ("b", c))
                dve.tensor_tensor(yT[:, c, :], yT[:, c, :], sg[:, c % 2, 1, :], ALU.add).then_inc(y_ready, 1)
            dve.wait_ge(gain_loaded[1], 16)
            for t in range(NM):
                norm(1, t)
            for j in range(2):
                for t in range(NT):
                    src = need(dve, ("mix", j, t))
                    cols = slice(j * 512, (j + 1) * 512)
                    free(dve.tensor_tensor(h[:, t, cols], src, h[:, t, cols], ALU.add), ("mix", j, t))
            for t in range(NM):
                copy_turned(NT + t)
            dve.wait_ge(gain_loaded[0], 32)
            norm(2, 0)
            norm(2, 1)
            for j in range(2):
                for t in range(NM):
                    src = need(dve, ("xv", j, t))
                    free(dve.tensor_copy(xv[:, t, j * 512:(j + 1) * 512], src), ("xv", j, t))
            norm(2, 2)
            copy_turned(NT + NM)
            norm(2, 3)
            for t in range(1, NT):
                copy_turned(NT + NM + t)
            for e in range(XU + 2):
                if e < XU:
                    src = need(dve, ("xs", e))
                    link.link(dve.tensor_reduce(xst[:, 0, e:e + 1], src[:, 0:MEM], AX.X, ALU.max))
                    dve.tensor_scalar(xst[:, 1, e:e + 1], xst[:, 0, e:e + 1], -XD_SCALE, None, ALU.mult)\
                       .then_inc(xnmax_ready, 1)
                if 1 <= e <= XU:
                    f = e - 1
                    dve.wait_ge(xexp_ready, f + 1)
                    link.link(dve.reciprocal(xst[:, 3, f:f + 1], xst[:, 2, f:f + 1]))
                    if f >= 2:
                        need(dve, ("xpt", f - 2))
                    dve.tensor_scalar(xpn[:, f % 2, :], xp[:, f % 2, :], xst[:, 3, f:f + 1], None, ALU.mult)\
                       .then_inc(xp_ready, 1)
                if e >= 2 and (e - 2) % NT == NT - 1:
                    hd = (e - 2) // NT
                    for c in range(2):
                        src = need(dve, ("xot", hd, c))
                        free(dve.tensor_copy(xoT[:, 2 * hd + c, :], src), ("xot", hd, c))
            for j in range(2):
                for t in range(NT):
                    src = need(dve, ("xo", j, t))
                    cols = slice(j * 512, (j + 1) * 512)
                    free(dve.tensor_tensor(h[:, t, cols], src, h[:, t, cols], ALU.add), ("xo", j, t))
            dve.wait_ge(gain_loaded[1], 32)
            for t in range(NT):
                norm(3, t)
            for t in range(NT):
                copy_turned(2 * NT + NM + t)
            dve.wait_ge(normed, 3 * NT + NM)

            peer = Chain(dve, dve_peer)

            def top16(values, rest, val, idx):
                flat = rest
                peer.link(dve.max(val[:, 0:8], values))
                peer.step(dve.max_index(idx[:, 0:8], val[:, 0:8], values))
                peer.link(dve.match_replace(flat, val[:, 0:8], values, -3.0e38))
                peer.link(dve.max(val[:, 8:16], flat))
                peer.link(dve.max_index(idx[:, 8:16], val[:, 8:16], flat))

            def topk(hd, t):
                b = hd * NT + t
                at_least(dve, gate_ready, b)
                stand(dve, scores_done, hd * NT + t // 2 * 2 + 2)
                for p in range(2):
                    at_col = (t % 2 * 2 + p) * KEYS
                    top16(bank[:, 2 + t // 2, at_col:at_col + KEYS], sc_rest[:, p, :], hv[:, p, :], hi[:, p, :])
                grid = [P, TOPK, TOPK]
                peer.link(dve.tensor_tensor(cand[:], hv[:, 0, :].unsqueeze(2).broadcast_to(grid),
                                            hv[:, 1, :].unsqueeze(1).broadcast_to(grid), ALU.add))
                top16(cand[:].rearrange("p i j -> p (i j)"), cand_rest[:], best[:], pos[:])
                dve.tensor_scalar(pst[:, 0:1], best[:, 0:1], -1.0, None, ALU.mult).then_inc(soft_bias, 1)
                peer.step(dve.tensor_scalar(ij[:, 0, :], pos[:], 4, None, ALU.logical_shift_right))
                peer.step(dve.tensor_scalar(ij[:, 1, :], pos[:], TOPK - 1, None, ALU.bitwise_and))
                peer.link(dve.tensor_copy(hif[:], hi[:]))
                peer.link(dve.tensor_copy(ijf[:], ij[:]))
                for p in range(2):
                    peer.step(dve.tensor_tensor(hot[:, p, :, :], ijf[:, p, :].unsqueeze(2).broadcast_to(grid),
                                                iota16[:].unsqueeze(1).broadcast_to(grid), ALU.is_equal))
                peer.join()
                for p in range(2):
                    peer.step(dve.tensor_tensor(picked[:, p, :, :], hot[:, p, :, :],
                                                hif[:, p, :].unsqueeze(1).broadcast_to(grid), ALU.mult))
                peer.join()
                peer.link(dve.tensor_reduce(sel[:], picked[:], AX.X, ALU.add))
                at_least(dve, picks_taken, b - NT + 1)
                dve.scalar_tensor_tensor(out=eidx[:, t, :], in0=sel[:, 0, :], scalar=float(KEYS), in1=sel[:, 1, :],
                                         op0=ALU.mult, op1=ALU.add).then_inc(picks_ready, 1)
                dve.wait_ge(soft_exp, b + 1)
                peer.link(dve.reciprocal(pst[:, 2:3], pst[:, 1:2]))
                dve.tensor_scalar(gate[:, t, :], ex[:], pst[:, 2:3], None, ALU.mult).then_inc(gate_ready, 1)

            def dots(hd, t, k):
                b = hd * NT + t
                dve.wait_ge(u_loaded[k], 16 * GE * (b + 1))
                for j in range(GE):
                    e = k * GE + j
                    ins = dve.tensor_tensor_reduce(out=U[:, e, :], in0=U[:, e, :], in1=hp[:, t, :], scale=1.0,
                                                   scalar=0.0, op0=ALU.mult, op1=ALU.add, accum_out=dot[:, e:e + 1])
                ins.then_inc(dots_done, 1)

            def weigh(hd, t, k):
                dve.wait_ge(gelu_done, (hd * NT + t) * NG + k + 1)
                es = slice(k * GE, (k + 1) * GE)
                dve.tensor_tensor(wgt[:, es], gel[:, es], gate[:, t, es], ALU.mult).then_inc(w_ready, 1)

            def add_out(b, t):
                dve.wait_ge(v_used, NG * (b + 1))
                src = bank[:, 4 + 2 * (t % 2):6 + 2 * (t % 2), :].rearrange("p n c -> p (n c)")
                dve.tensor_tensor(h[:, t, :], src, h[:, t, :], ALU.add).then_inc(out_added, 1)

            def head(hd, more):
                for t in range(NT):
                    b = hd * NT + t
                    dve.wait_ge(gate_ready, b + 1)
                    for k in range(NG):
                        dots(hd, t, k)
                        if k:
                            weigh(hd, t, k - 1)
                    weigh(hd, t, NG - 1)
                    if not (isinstance(b, int) and b == 0):
                        add_out(b - 1, (t - 1) % NT)
                    if more:
                        topk(hd + 1, t)

            for t in range(NT):
                topk(0, t)
            head(0, True)
            steps = peer.n // (2 * NT) * NT
            with dve.Fori(1, PH - 1) as hd:
                peer.base, peer.n = (hd + 1) * steps, 0
                head(hd, True)
            peer.base, peer.n = PH * steps, 0
            head(PH - 1, False)
            add_out(PH * NT - 1, NT - 1)
            dve.wait_ge(gain_loaded[0], 48)
            for t in range(NT):
                normalise(3 * NT + NM + t, h[:, t, :], 0, hp[:, t, :], final_ready)


def _panels(w):
    k, n = w.shape
    wide = 4096 // (k // P)
    return np.ascontiguousarray(w.reshape(k // P, P, n // wide, wide).transpose(2, 1, 0, 3)).reshape(-1, P, 4096)


def kernel(**inputs):
    import concourse.bacc as bacc
    from concourse.bass_utils import run_bass_kernel_spmd

    a = {k: np.asarray(v) for k, v in inputs.items()}
    w_in = a["w_in"]
    q0, kc0, vc0, ks0, vs0, kw0, vw0, g0, u0, v0, m0 = [int(i) for i in np.cumsum(
        [0, 512, 128, 128, 128, 128, 128, 128, 24, 512, 512])]
    cols = []
    for c in range(4):
        cols += [q0 + hd * DK + i for hd in (c, 4 + c) for i in range(DK)]
    for s in (kc0, vc0):
        for g in range(GROUPS):
            cols += [s + g * DK + i for _ in range(2) for i in range(DK)]
    for s, n in ((ks0, P), (kw0, P), (vs0, P), (vw0, P), (v0, GW), (u0, GW)):
        cols += list(range(s, s + n))
    for c in range(0, KD, 2):
        for b in range(2):
            cols += list(range(m0 + b * D + c * P, m0 + b * D + (c + 2) * P))
    win = _panels(w_in[:, cols])
    w1 = [np.ascontiguousarray(a[f"cmp_w1_{s}"].reshape(BLOCK // 2, P, HID).transpose(1, 0, 2)).reshape(1, P, 4096)
          for s in "kv"]
    w_panels = np.concatenate([win[0:4], w1[0], w1[1], win[4:5], _panels(a["w_nsa_out"]), _panels(a["w_gmlp_out"]),
                               win[5:9], _panels(a["w_mix_out"]), _panels(a["w_xkv"]), _panels(a["w_xq"]),
                               _panels(a["w_xo"])])
    peer_w = a["w_peer_q"].reshape(KD, P, PH, 2 * KEYS).transpose(2, 1, 0, 3)
    keys = a["peer_sub_keys"].transpose(0, 3, 1, 2).reshape(PH, P, 1, 2 * KEYS)
    pe = [a[f"cmp_pe_{s}"].reshape(BLOCK // 2, 2, DK).transpose(1, 2, 0).reshape(P, BLOCK // 2) for s in "kv"]
    arrays = {
        "x": a["x"].reshape(S, D), "mem": a["mem"].reshape(MEM, D),
        "gains": np.stack([a[k] for k in ("g_mix", "g_mem", "g_xattn", "g_peer", "g_final")]),
        "w_panels": w_panels,
        "w_gates": w_in[:, g0:g0 + 24].reshape(KD, P, 24).transpose(1, 0, 2),
        "cmp_pe": np.stack(pe, axis=1),
        "cmp_b1": np.stack([a[f"cmp_b1_{s}"].reshape(2, P).T for s in "kv"], axis=1),
        "cmp_w2": np.stack([a[f"cmp_w2_{s}"].reshape(2, P, DK).transpose(1, 0, 2) for s in "kv"], axis=1),
        "ln_gb": np.stack([a["gmlp_ln_g"], a["gmlp_ln_b"]]),
        "ws_t": a["gmlp_ws"].transpose(2, 0, 1),
        "bs": a["gmlp_bs"],
        "peer_w": np.concatenate([peer_w, keys], axis=2),
        "peer_u": a["peer_u"], "peer_v": a["peer_v"],
    }
    nc = bacc.Bacc("TRN2", target_bir_lowering=False, num_devices=1)
    feed, args = {}, []
    for name, v in arrays.items():
        v = np.ascontiguousarray(v)
        feed[name + "_dram"] = v
        args.append(nc.dram_tensor(name + "_dram", v.shape, mybir.dt.from_np(v.dtype), kind="ExternalInput").ap())
    args.append(nc.dram_tensor("out_dram", (S, D), F32, kind="ExternalOutput").ap())
    hybrid_block(nc, *args)
    r = run_bass_kernel_spmd(nc, [feed], core_ids=[0])
    return r.results[0]["out_dram"].reshape(1, S, D)
```

```python
import numpy as np
from contextlib import ExitStack

import concourse.bass as bass
from concourse import mybir

F32 = mybir.dt.float32
U32 = mybir.dt.uint32
ALU = mybir.AluOpType
ACT = mybir.ActivationFunctionType
AX = mybir.AxisListType

P = 128
S = 512
D = 1024
NT = S // P
KD = D // P
MEM = 256
NM = MEM // P
HEADS, DK, GROUPS = 8, 64, 2
BLOCK, STRIDE = 32, 16
NCMP = S // STRIDE - BLOCK // STRIDE + 1
HID = 256
GW = 512
XH, XD = 4, 256
PH, TOPK, KEYS = 8, 16, 128
EPS = 1e-6
NEG = -1e30
TINY = 1e-30
DK_SCALE = DK ** -0.5
XD_SCALE = XD ** -0.5

CHUNKS = [(0, 1), (1, NT - 1)]
N1 = NT - 1
PICKS0 = PH

GE = 4
NG = TOPK // GE
UG, VG = 4, 2
GE0 = 2
NG0 = TOPK // GE0
UG0, VG0 = 3, 2
ALL0 = PH * NG0

NSLOT = 4


def chunk_panels(ch):
    out = []
    for c in range(KD):
        if c % 4 == 0:
            out += [((ch, "nsa_out", c // 4), 0), ((ch, "gmlp_out", c // 4), 1)]
        out.append(((ch, "merge", c), 2 + c % 2))
    rest = [(ch, "mix", j) for j in range(4)] + [(ch, "xq", j) for j in range(4)] + [(ch, "xo", j) for j in range(4)]
    return out + [(p, i % NSLOT) for i, p in enumerate(rest)]


PRE = ([("q", j) for j in range(2)] + [("kvc", j) for j in range(2)] + [("kT",), ("vsw",)] +
       [("v", j) for j in range(2)] + [("w1k", j) for j in range(2)] + [("w1v", j) for j in range(2)] +
       [("u", j) for j in range(2)] + [("xkv", j) for j in range(8)])
PANELS = [(p, (i + 2) % NSLOT) for i, p in enumerate(PRE)] + chunk_panels(0) + chunk_panels(1)


def source_panel(name):
    if not isinstance(name[0], int):
        return PRE.index(name)
    _, key, j = name
    first = {"nsa_out": 0, "gmlp_out": 2, "merge": 4, "mix": 12, "xq": 16, "xo": 20}[key]
    return len(PRE) + first + j


def last_result(panel):
    if isinstance(panel[0], int):
        ch, key, j = panel
        n = CHUNKS[ch][1]
        return {"nsa_out": ("m1", ch, 4 * j + 3), "gmlp_out": ("m1", ch, 4 * j + 3), "merge": ("m1", ch, j),
                "mix": ("mix", ch, j // 2, n - 1), "xq": ("xqt", ch, 2 * j + 1), "xo": ("xo", ch, j // 2, n - 1)}[key]
    key, j = panel[0], panel[1] if len(panel) > 1 else 0
    return {"q": ("q", 2 * j + 1), "kvc": ("kvc", 2 * j + 1), "kT": ("kw",), "vsw": ("vsw", NT - 1),
            "v": ("v", NT - 1), "w1k": ("hid", 0), "w1v": ("hid", 1), "u": ("u", 2 * j + 1),
            "xkv": ("xk", 2 * j + 1) if j < 4 else ("xv", (j - 4) // 2, NM - 1)}[key]


def slot_turns():
    seen, last, out = [0] * NSLOT, [None] * NSLOT, {}
    for name, s in PANELS:
        out[name] = (s, seen[s], last[s])
        seen[s] += 1
        last[s] = name
    return out


NORMS = ([("mix", t) for t in range(NT)] + [("mem", t) for t in range(NM)] +
         [(k, t) for t0, n in CHUNKS for k in "xp" for t in range(t0, t0 + n)])


def items(ch):
    n = CHUNKS[ch][1]
    out = [(k, c) for c in range(KD) for k in ("ab", "m")]
    out += [("mix", j, i) for j in range(2) for i in range(n)] + [("nx", i) for i in range(n + 1)]
    out += [("xq", c) for c in range(KD)] + [("xa", e) for e in range(XH * n + 2)]
    return out + [("xo", j, i) for j in range(2) for i in range(n)] + [("np", i) for i in range(n + 1)]


def item_results(ch, item):
    k, i = item[0], item[1]
    t0, n = CHUNKS[ch]
    if k == "ab":
        return [("a", ch, i), ("b", ch, i)]
    if k == "m":
        return [("m0", ch, i), ("m1", ch, i)]
    if k in ("mix", "xo"):
        return [(k, ch, i, item[2])]
    if k in ("nx", "np"):
        if i == n:
            return []
        m = NORMS.index((k[1], t0 + i))
        return [("turn", m, 0), ("turn", m, 1)]
    if k == "xq":
        return [("xqt", ch, i)]
    out = [("xs", ch, i)] if i < XH * n else []
    if i >= 2:
        out.append(("xpt", ch, i - 2))
        if (i - 2) % n == n - 1:
            out += [("xot", ch, (i - 2) // n, 0), ("xot", ch, (i - 2) // n, 1)]
    return out


def interleaved():
    cost = {"ab": 5, "m": 10, "mix": 7, "nx": 1, "xq": 5, "xa": 2, "xo": 7, "np": 1, "q1": 6, "s1": 2, "t1": 3}
    seq = items(1) + [("q1", 0), ("q1", 1), ("s1", 0), ("s1", 1)] + [("t1", i) for i in range(N1)]
    total, done, out = sum(cost[i[0]] for i in seq), 0, [[] for _ in range(ALL0)]
    for it in seq:
        out[done * ALL0 // total].append(it)
        done += cost[it[0]]
    return out


def psum_turns():
    names = []
    for m in range(NT):
        names += [("turn", m, 0), ("turn", m, 1)]
    names += [("q", c) for c in range(4)] + [("kvc", c) for c in range(4)] + [("ks",), ("kw",)]
    names += [("vsw", t) for t in range(NT)] + [("gates",)] + [("v", t) for t in range(NT)]
    names += [("hid", 0), ("hid", 1)] + [("u", c) for c in range(4)]
    names += [("kcmp",), ("vcmp",)] + [("spatial", t) for t in range(NT)]
    for t in range(NT):
        names += [("cs", t, 0), ("cs", t, 1), ("cpt", t, 0), ("cpt", t, 1), ("co", t)]
    names += attention_names()
    names += [("ot", t) for t in range(NT)]
    for m in range(NT, NT + NM):
        names += [("turn", m, 0), ("turn", m, 1)]
    names += [("xk", c) for c in range(KD)]
    for j in range(2):
        names += [("xv", j, t) for t in range(NM)]
    for it in items(0):
        names += item_results(0, it)
    out, last, used = {}, [None] * 8, [0] * 8
    beside = [n for it in items(1) for n in item_results(1, it)]
    for group, banks in ((names, 8), (beside, 6)):
        for i, n in enumerate(group):
            b = i % banks
            out[n] = (b, used[b], last[b])
            used[b] += 1
            last[b] = n
        if banks == 8:
            last_before = list(last)
    return out, last_before, last


def units():
    return [(t, br, h) for t in range(NT) for br in (1, 2) for h in range(HEADS)]


def attention_names():
    n, names = len(units()), []
    for i in range(n + 2):
        if i < n:
            names.append(("s", i))
        if 1 <= i <= n:
            names.append(("pt", i - 1))
        if i >= 2:
            names.append(("o", i - 2))
    return names


def at_least(eng, sem, value):
    if not isinstance(value, int) or value > 0:
        eng.wait_ge(sem, value)


def stand(eng, sem, value):
    at_least(eng, sem, value)
    if not isinstance(value, int):
        eng.nop(nofuse=True)


class Chain:

    def __init__(self, eng, sem):
        self.eng, self.sem, self.base, self.n = eng, sem, 0, 0

    def step(self, ins):
        ins.then_inc(self.sem, 1)
        self.n += 1

    def join(self):
        stand(self.eng, self.sem, self.base + self.n)

    def link(self, ins):
        self.step(ins)
        self.join()


def hybrid_block(nc, x, mem, gains, w_panels, w_gates, cmp_pe, cmp_b1, cmp_w2, ln_gb, ws_t, bs, peer_w,
                 peer_u, peer_v, out):
    ctx = ExitStack()
    with ctx:
        BASE = 16640

        def at(name, shape, kb, dt=F32):
            return nc.alloc_sbuf_tensor_at(name, shape, dt, offset=BASE + int(kb * 1024))

        ctx.enter_context(nc.sbuf_tensor("arena", [P, 52992], F32))

        h = at("h", [P, NT, D], 0)
        hnT = at("hnT", [P, KD, S], 16)
        hnX = [at("hnX0", [P, KD, P], 172), at("hnX1", [P, KD, N1 * P], 16)]
        W = [at(f"W{s}", [P, 2048], 40 + 8 * s) for s in range(NSLOT)]
        small_at = [32.0]

        def small(name, shape, dt=F32):
            n = (int(np.prod(shape[1:])) * 4 + 31) // 32 * 32
            v = at(name, shape, small_at[0], dt)
            small_at[0] += n / 1024
            assert small_at[0] <= 40
            return v

        ident = small("ident", [P, P])
        wg = small("wg", [P, KD, 24])
        gates = small("gates", [P, NT, 24])
        pe_sb = small("pe_sb", [P, 2, BLOCK // 2])
        b1_sb = small("b1_sb", [P, 2, 2])
        w2_sb = small("w2_sb", [P, 2, 2, DK])
        hid_kb = small_at[0]
        hidT = small("hidT", [P, 2, 2, GROUPS * NCMP])
        kcT = small("kcT", [P, NCMP])
        vc = small("vc", [NCMP, GROUPS, DK])
        cmask = small("cmask", [P, NT, NCMP])
        ckeep = small("ckeep", [P, NT, NCMP])
        ssq = small("ssq", [P, 20])
        rms = small("rms", [P, 20])
        rinv = small("rinv", [P, 20])
        vsum = small("vsum", [P, 4, NT])
        cst = small("cst", [P, 4, HEADS])
        rmax = small("rmax", [P, 64])
        nmax = small("nmax", [P, 64])
        rsum = small("rsum", [P, 64])
        coef = small("coef", [P, 64])
        xst = small("xst", [P, 4, XH * NT])
        eps_col = small("eps_col", [P, 1])
        iota16 = small("iota16", [P, TOPK])

        qT = at("qT", [P, 4, S], 72)
        ksT = at("ksT", [P, S], 80)
        kwT = at("kwT", [P, S], 82)
        vsw = at("vsw", [P, NT, 2, P], 84)
        blk = at("blk", [P, 2, BLOCK // 2, GROUPS, NCMP], 88)
        vn = at("vn", [P, NT, GW], 96)
        oT = at("oT", [P, 4, S], 104)
        uT = at("uT", [P, 4, S], 112)
        sm = at("sm", [P, 3, S], 120)
        pr = at("pr", [P, 3, S], 126)
        pt = at("pt", [P, 2, S], 132)
        yT = [at("yT0", [P, KD, P], 120), at("yT1", [P, KD, N1 * P], 124)]
        otok = at("otok", [P, NT, GW], 136)
        causal = at("causal", [P, 7 * P], 144)
        ln_sb = at("ln_sb", [P, 2, GW], 148)
        wsT = at("wsT", [P, 4, P], 152)
        bs_sb = at("bs_sb", [P, 4, P], 154)
        gv = at("gv", [P, GW], 156)
        xn = at("xn", [P, 2, D], 96)
        sg = at("sg", [P, 2, N1 * P], 180)
        gb = [at(f"gain{n}", [P, D], kb) for n, kb in enumerate((168, 172, 199, 203, 199))]
        xkT = at("xkT", [P, KD, MEM], 136)
        xv = at("xv", [P, NM, D], 144)
        xqT = [at("xqT0", [P, KD, P], 152), at("xqT1", [P, KD, N1 * P], 104)]
        xoT = [at("xoT0", [P, KD, P], 120), at("xoT1", [P, KD, N1 * P], 124)]
        mnT = at("mnT", [P, KD, MEM], 152)
        mtok = at("mtok", [P, NM, D], 160)
        xpT = at("xpT", [P, NM, N1 * P], 176)
        xp = at("xp", [P, 2, MEM], 100)
        xpn = at("xpn", [P, 2, MEM], 102)
        hp0 = at("hp0", [P, D], 168)
        hp1 = at("hp1", [P, N1, D], 104)
        pw = at("pw", [P, KD + 1, 2 * KEYS], 190)
        eidx = at("eidx", [P, N1 + 2, TOPK], hid_kb, U32)
        row_no = at("row_no", [P, N1 + 2, TOPK], hid_kb + 0.3125, U32)
        gate = at("gate", [P, N1 + 2, TOPK], hid_kb + 0.625)
        sc_rest = at("sc_rest", [P, 2, KEYS], 185)
        cand = at("cand", [P, TOPK, TOPK], 186)
        cand_rest = at("cand_rest", [P, TOPK * TOPK], 187)
        hot = at("hot", [P, TOPK, TOPK], 187)
        picked = at("picked", [P, TOPK, TOPK], 188)
        hv = at("hv", [P, 2, TOPK], 189)
        hi = at("hi", [P, 2, TOPK], 189.125, U32)
        hif = at("hif", [P, 2, TOPK], 189.25)
        ij = at("ij", [P, 2, TOPK], 189.375, U32)
        ijf = at("ijf", [P, 2, TOPK], 189.5)
        sel = at("sel", [P, 2, TOPK], 189.625)
        best = at("best", [P, TOPK], 189.75)
        pos = at("pos", [P, TOPK], 189.8125, U32)
        ex = at("ex", [P, TOPK], 189.875)
        pst = at("pst", [P, 4], 189.9375)
        dot = at("dot", [P, TOPK], hid_kb - 1)
        gel = at("gel", [P, TOPK], hid_kb - 1 + 0.0625)
        wgt = at("wgt", [P, TOPK], hid_kb - 1 + 0.125)
        U0 = at("U0", [P, UG0, GE0, D], 72)
        V0 = at("V0", [P, VG0, GE0, D], 152)
        pq0 = at("pq0", [P, 2, P], 179)
        U1 = at("U1", [P, UG * GE, D], 40)
        V1 = [at(f"V1_{g}", [P, GE, D], kb) for g, kb in enumerate((136, 120))]
        pq1 = at("pq1", [P, 2, N1 * P], 176)
        scs = at("scs", [P, N1, 2, KEYS], 180)
        diag1 = at("diag1", [P, 2, GE, P], 152)

        bank = ctx.enter_context(nc.psum_tensor("bank", [P, 8, 512], F32))
        PROJ0, SCORES0 = 6, 7
        PROJ1, SCORES1, OUT1 = 0, 1, 2

        def sem(name):
            return ctx.enter_context(nc.semaphore(name))

        panel_loaded = [sem(f"panel_loaded{s}") for s in range(NSLOT)]
        bank_filled = [sem(f"bank_filled{b}") for b in range(8)]
        x_loaded = [sem(f"x_loaded{t}") for t in range(NT)]
        gain_loaded = [sem(f"gain_loaded{n}") for n in range(5)]
        mem_loaded, small_loaded, consts_ready = sem("mem_loaded"), sem("small_loaded"), sem("consts_ready")
        rms_ready, normed, turned_act, turned_dve = sem("rms_ready"), sem("normed"), sem("turned_act"), sem("turned_dve")
        spatial_read, cs_read, co_read, s_read, a_read, b_read = (sem("spatial_read"), sem("cs_read"), sem("co_read"),
                                                                  sem("s_read"), sem("a_read"), sem("b_read"))
        q_ready, blk_ready, kt_ready, vsw_ready = sem("q_ready"), sem("blk_ready"), sem("kt_ready"), sem("vsw_ready")
        gates_ready, v_gelu, v_centred, v_std = sem("gates_ready"), sem("v_gelu"), sem("v_centred"), sem("v_std")
        vn_ready, hid_ready, u_ready, cmp_ready = sem("vn_ready"), sem("hid_ready"), sem("u_ready"), sem("cmp_ready")
        og_ready, cs_ready, cexp_ready, cp_ready, cpt_ready = (sem("og_ready"), sem("cs_ready"), sem("cexp_ready"),
                                                              sem("cp_ready"), sem("cpt_ready"))
        nmax_ready, probs_ready, pt_ready, o_added = sem("nmax_ready"), sem("probs_ready"), sem("pt_ready"), sem("o_added")
        ot_ready, mg_ready, y_ready, h1_ready = sem("ot_ready"), sem("mg_ready"), sem("y_ready"), sem("h1_ready")
        xk_ready, xv_ready, xq_ready = sem("xk_ready"), sem("xv_ready"), sem("xq_ready")
        xnmax_ready, xexp_ready, xp_ready, xpt_ready, xo_ready, h2_ready = (
            sem("xnmax_ready"), sem("xexp_ready"), sem("xp_ready"), sem("xpt_ready"), sem("xo_ready"), sem("h2_ready"))
        pw_loaded, picks_taken, picks_ready, soft_bias, soft_exp, gate_ready = (
            sem("pw_loaded"), sem("picks_taken"), sem("picks_ready"), sem("soft_bias"), sem("soft_exp"), sem("gate_ready"))
        u0_loaded = [sem(f"u0_loaded{g}") for g in range(UG0)]
        v0_loaded = [sem(f"v0_loaded{g}") for g in range(VG0)]
        proj0_done, pq0_ready, scores0_done, dots0_done, gelu0_done, w0_ready, row0_added = (
            sem("proj0_done"), sem("pq0_ready"), sem("scores0_done"), sem("dots0_done"), sem("gelu0_done"),
            sem("w0_ready"), sem("row0_added"))
        u1_loaded = [sem(f"u1_loaded{g}") for g in range(UG)]
        v1_loaded = [sem(f"v1_loaded{g}") for g in range(VG)]
        proj1_done, pq1_ready, scores1_done, sc_copied = (
            sem("proj1_done"), sem("pq1_ready"), sem("scores1_done"), sem("sc_copied"))
        dots1_done, gelu1_done, w1_ready, diag1_ready, v1_used, out1_added = (
            sem("dots1_done"), sem("gelu1_done"), sem("w1_ready"), sem("diag1_ready"), sem("v1_used"), sem("out1_added"))
        final_ready, stored = sem("final_ready"), sem("stored")
        dve_chain, act_chain, pool_chain, dve_peer = sem("dve_chain"), sem("act_chain"), sem("pool_chain"), sem("dve_peer")

        slot_of = slot_turns()
        bank_of, last_before, last_results = psum_turns()
        UNITS = units()
        BESIDE = interleaved()

        def panel(name, k, n):
            return W[slot_of[name][0]][:, :].rearrange("p (k n) -> p k n", k=k, n=n)

        def has_panel(eng, name):
            s, n, _ = slot_of[name]
            eng.wait_ge(panel_loaded[s], 16 * (n + 1))

        def need(eng, name):
            b, n, _ = bank_of[name]
            eng.wait_ge(bank_filled[b], n + 1)
            return bank[:, b, :]

        def nth(ch, j, i):
            return 2 * CHUNKS[0][1] * ch + j * CHUNKS[ch][1] + i + 1

        def unit_no(ch, e):
            return XH * CHUNKS[0][1] * ch + e + 1

        def read_signal(name):
            key, i = name[0], name[1] if len(name) > 1 else 0
            j = name[2] if len(name) > 2 else 0
            if key in ("mix", "xo"):
                return {"mix": h1_ready, "xo": h2_ready}[key], nth(*name[1:])
            if key in ("a", "b", "m0", "m1", "xqt"):
                n = KD * i + j + 1
                return {"a": (a_read, n), "b": (b_read, n), "m0": (mg_ready, 2 * n - 1), "m1": (mg_ready, 2 * n),
                        "xqt": (xq_ready, n)}[key]
            if key in ("xs", "xpt"):
                return {"xs": xexp_ready, "xpt": xpt_ready}[key], unit_no(i, j)
            if key == "xot":
                return xo_ready, KD * i + 2 * j + name[3] + 1
            return {"turn": (turned_dve if j else turned_act, i + 1), "q": (q_ready, i + 1), "kvc": (blk_ready, 4 * i + 4),
                    "ks": (kt_ready, 1), "kw": (kt_ready, 2), "vsw": (vsw_ready, i + 1), "gates": (gates_ready, 1),
                    "v": (v_gelu, i + 1), "hid": (hid_ready, 2 * i + 2), "u": (u_ready, i + 1),
                    "kcmp": (cmp_ready, 1), "vcmp": (cmp_ready, 2), "spatial": (spatial_read, i + 1),
                    "cs": (cs_read, 2 * i + j + 1), "cpt": (cpt_ready, 2 * i + j + 1), "co": (co_read, i + 1),
                    "s": (s_read, i + 1), "pt": (pt_ready, i + 1), "o": (o_added, i + 1), "ot": (ot_ready, i + 1),
                    "xk": (xk_ready, i + 1), "xv": (xv_ready, NM * i + j + 1)}[key]

        def free(ins, name):
            ins.then_inc(read_signal(name)[0], 1)

        def was_read(eng, name):
            eng.wait_ge(*read_signal(name))

        def norm_dst(m):
            kind, t = NORMS[m]
            if kind == "p":
                return hp0[:, :] if t == 0 else hp1[:, t - 1, :]
            return xn[:, m % 2, :]

        def xn_free(eng, m):
            if NORMS[m][0] != "p":
                before = [b for b in range(m) if b % 2 == m % 2 and NORMS[b][0] != "p"]
                if before:
                    need(eng, ("turn", before[-1], 1))

        def turned_dst(m, half):
            kind, t = NORMS[m]
            ks = slice(4 * half, 4 * half + 4)
            if kind == "mix":
                return hnT[:, ks, t * P:(t + 1) * P]
            if kind == "mem":
                return mnT[:, ks, t * P:(t + 1) * P]
            return hnX[0][:, ks, :] if t == 0 else hnX[1][:, ks, (t - 1) * P:t * P]

        def norm_no(kind, t):
            return NORMS.index((kind, t))

        def cols_of(ch):
            t0, n = CHUNKS[ch]
            return slice(t0 * P, (t0 + n) * P)

        def pick_no(hd, i):
            return PICKS0 + hd * N1 + i

        block = ctx.enter_context(nc.Block())

        @block.sync
        def _(sp):
            def gain(n):
                sp.dma_start(gb[n][:], gains[n, :].partition_broadcast(P)).then_inc(gain_loaded[n], 16)

            for t in range(NT):
                sp.dma_start(h[:, t, :], x[t * P:(t + 1) * P, :]).then_inc(x_loaded[t], 16)
                if t == 0:
                    gain(0)
            smalls = [(wg[:], w_gates), (pe_sb[:], cmp_pe), (b1_sb[:], cmp_b1), (w2_sb[:], cmp_w2),
                      (ln_sb[:], ln_gb.partition_broadcast(P)), (wsT[:], ws_t), (bs_sb[:], bs.partition_broadcast(P))]
            for i, (name, s) in enumerate(PANELS):
                before = slot_of[name][2]
                if before:
                    need(sp, last_result(before))
                sp.dma_start(W[s][:, :], w_panels[source_panel(name)]).then_inc(panel_loaded[s], 16)
                if i == 3:
                    for dst, src in smalls:
                        sp.dma_start(dst, src).then_inc(small_loaded, 16)
                    for n in (1, 2, 3):
                        gain(n)
                    for t in range(NM):
                        sp.dma_start(mtok[:, t, :], mem[t * P:(t + 1) * P, :]).then_inc(mem_loaded, 16)
                    sp.dma_start(pw[:], peer_w[0]).then_inc(pw_loaded, 16)
            sp.wait_ge(normed, norm_no("x", NT - 1) + 1)
            gain(4)
            with sp.Fori(1, PH) as hd:
                sp.wait_ge(scores1_done, 2 * hd)
                sp.dma_start(pw[:], peer_w[bass.ds(hd, 1)].rearrange("o p k n -> (o p) k n")).then_inc(pw_loaded, 16)
            for t in range(NT):
                sp.wait_ge(final_ready, t + 1)
                sp.dma_start(out[t * P:(t + 1) * P, :], hp0[:, :] if t == 0 else hp1[:, t - 1, :]).then_inc(stored, 16)
            sp.wait_ge(stored, 16 * NT)

        @block.gpsimd
        def _(pool):
            pool.memset(ident[:], 0.0).then_inc(pool_chain, 1)
            pool.memset(causal[:], 0.0).then_inc(pool_chain, 1)
            pool.memset(cmask[:], 0.0).then_inc(pool_chain, 1)
            pool.memset(ckeep[:], 1.0).then_inc(pool_chain, 1)
            pool.memset(eps_col[:], EPS).then_inc(consts_ready, 1)
            pool.wait_ge(pool_chain, 4)
            pool.affine_select(out=ident[:], in_=ident[:], compare_op=ALU.not_equal, fill=1.0, base=0,
                               pattern=[[-1, P]], channel_multiplier=1).then_inc(consts_ready, 1)
            pool.affine_select(out=causal[:], in_=causal[:], compare_op=ALU.is_ge, fill=NEG, base=3 * P,
                               pattern=[[-1, 7 * P]], channel_multiplier=1).then_inc(consts_ready, 1)
            for m, f in ((cmask, NEG), (ckeep, 0.0)):
                pool.affine_select(out=m[:], in_=m[:], compare_op=ALU.is_ge, fill=f, base=1 - BLOCK,
                                   pattern=[[P, NT], [-STRIDE, NCMP]], channel_multiplier=1).then_inc(consts_ready, 1)
            pool.iota(iota16[:], [[1, TOPK]], base=0, channel_multiplier=0,
                      allow_small_or_imprecise_dtypes=True).then_inc(consts_ready, 1)
            pool.wait_ge(small_loaded, 16 * 7)
            pool.affine_select(out=wsT[:], in_=wsT[:], compare_op=ALU.is_ge, fill=0.0, base=0,
                               pattern=[[0, 4], [1, P]], channel_multiplier=-1).then_inc(consts_ready, 1)

            def gather(dst, table, slot, e, signal):
                pool.indirect_dma_start(dst, None, table, bass.IndirectOffsetOnAxis(
                    ap=row_no[:, slot, e:e + 1], axis=0)).then_inc(signal, 16)

            def take_picks(q, slot):
                stand(pool, picks_ready, q + 1)
                pool.tensor_copy(row_no[:, slot, :], eidx[:, slot, :]).then_inc(picks_taken, 1)
                stand(pool, picks_taken, q + 1)

            for G in range(ALL0 + 1):
                if G < ALL0:
                    hd, k = divmod(G, NG0)
                    if k == 0:
                        at_least(pool, row0_added, (hd - 1) * TOPK)
                        take_picks(hd, N1 + hd % 2)
                    at_least(pool, dots0_done, GE0 * (G - UG0 + 1))
                    for j in range(GE0):
                        gather(U0[:, G % UG0, j, :], peer_u, N1 + hd % 2, k * GE0 + j, u0_loaded[G % UG0])
                if G:
                    hd, k = divmod(G - 1, NG0)
                    at_least(pool, row0_added, GE0 * (G - 1 - VG0 + 1))
                    for j in range(GE0):
                        gather(V0[:, (G - 1) % VG0, j, :], peer_v, N1 + hd % 2, k * GE0 + j, v0_loaded[(G - 1) % VG0])

            pool.wait_ge(dots0_done, ALL0 * GE0)
            pool.wait_ge(row0_added, ALL0 * GE0)

            def batch(hd, i):
                b = hd * N1 + i
                stand(pool, v1_used, NG * (b - N1 + 1))
                take_picks(PICKS0 + b, i)

                def rows_u(k):
                    stand(pool, dots1_done, b * NG + k - NG + 1)
                    for j in range(GE):
                        gather(U1[:, k * GE + j, :], peer_u, i, k * GE + j, u1_loaded[k])

                def rows_v(k):
                    stand(pool, v1_used, b * NG + k - VG + 1)
                    for j in range(GE):
                        gather(V1[k % VG][:, j, :], peer_v, i, k * GE + j, v1_loaded[k % VG])

                rows_u(0)
                rows_u(1)
                rows_v(0)
                rows_u(2)
                rows_v(1)
                rows_u(3)
                rows_v(2)
                rows_v(3)

            for i in range(N1):
                batch(0, i)
            with pool.Fori(1, PH) as hd:
                for i in range(N1):
                    batch(hd, i)

        @block.tensor
        def _(pe):
            order = list(bank_of)

            def begin(name):
                assert order.pop(0) == name, name
                b, _, before = bank_of[name]
                if before:
                    was_read(pe, before)
                return bank[:, b, :]

            def filled(mm, name):
                mm.then_inc(bank_filled[bank_of[name][0]], 1)

            def all_turned(tiles):
                pe.wait_ge(turned_act, tiles)
                pe.wait_ge(turned_dve, tiles)

            def turn(m):
                pe.wait_ge(normed, m + 1)
                src = norm_dst(m)
                for half in range(2):
                    dst = begin(("turn", m, half))
                    for k in range(4):
                        kk = 4 * half + k
                        mm = pe.transpose(dst[:, k * P:(k + 1) * P], src[:, kk * P:(kk + 1) * P], ident[:])
                    filled(mm, ("turn", m, half))

            def product(name, w, act, k_tiles, width=512):
                dst = begin(name)[:, 0:width]
                for k in range(k_tiles):
                    mm = pe.matmul(dst, w(k), act(k), start=(k == 0), stop=(k == k_tiles - 1))
                filled(mm, name)

            def rows(name, act, first, j):
                dst = begin(name)
                for n in range(2):
                    pan = first[:-1] + (2 * j + n,)
                    has_panel(pe, pan)
                    w = panel(pan, KD, 256)
                    for k in range(KD):
                        mm = pe.matmul(dst[:, n * 256:(n + 1) * 256], act(k), w[:, k, :],
                                       start=(k == 0), stop=(k == KD - 1))
                filled(mm, name)

            def cols(key, first, c, act, width=512):
                pan = first[:-1] + (c // 2,)
                has_panel(pe, pan)
                w = panel(pan, KD, 256)
                product(key, lambda k: w[:, k, c % 2 * P:(c % 2 + 1) * P], act, KD, width)

            def hn(k):
                return hnT[:, k, :]

            pe.wait_ge(consts_ready, 6)
            for t in range(NT):
                turn(t)
            all_turned(NT)
            for key in ("q", "kvc"):
                for c in range(4):
                    cols((key, c), (key, 0), c, hn)
            has_panel(pe, ("kT",))
            w = panel(("kT",), KD, 256)
            for c, key in enumerate((("ks",), ("kw",))):
                product(key, lambda k: w[:, k, c * P:(c + 1) * P], hn, KD)
            has_panel(pe, ("vsw",))
            w = panel(("vsw",), KD, 256)
            for t in range(NT):
                product(("vsw", t), lambda k: hnT[:, k, t * P:(t + 1) * P], lambda k: w[:, k, :], KD, 256)
            pe.wait_ge(small_loaded, 16 * 7)
            dst = begin(("gates",))
            for t in range(NT):
                for k in range(KD):
                    mm = pe.matmul(dst[:, t * 24:(t + 1) * 24], hnT[:, k, t * P:(t + 1) * P], wg[:, k, :],
                                   start=(k == 0), stop=(k == KD - 1))
            filled(mm, ("gates",))
            for t in range(NT):
                rows(("v", t), lambda k: hnT[:, k, t * P:(t + 1) * P], ("v", 0), 0)
            for i, name in enumerate(("w1k", "w1v")):
                pe.wait_ge(blk_ready, 8 * (i + 1))
                w = []
                for j in range(2):
                    has_panel(pe, (name, j))
                    w.append(panel((name, j), BLOCK // 4, HID))
                dst = begin(("hid", i))
                for c in range(2):
                    for k in range(BLOCK // 2):
                        mm = pe.matmul(dst[:, c * P:c * P + 2 * NCMP], w[k // 8][:, k % 8, c * P:(c + 1) * P],
                                       blk[:, i, k, :, :].rearrange("p g c -> p (g c)"),
                                       start=(k == 0), stop=(k == BLOCK // 2 - 1))
                filled(mm, ("hid", i))
            for c in range(4):
                cols(("u", c), ("u", 0), c, hn)
            pe.wait_ge(hid_ready, 4)
            dst = begin(("kcmp",))
            for g in range(GROUPS):
                for c in range(2):
                    mm = pe.matmul(dst[g * DK:(g + 1) * DK, 0:NCMP], w2_sb[:, 0, c, :],
                                   hidT[:, 0, c, g * NCMP:(g + 1) * NCMP], start=(c == 0), stop=(c == 1))
            filled(mm, ("kcmp",))
            dst = begin(("vcmp",))
            for g in range(GROUPS):
                for c in range(2):
                    mm = pe.matmul(dst[0:NCMP, g * DK:(g + 1) * DK], hidT[:, 1, c, g * NCMP:(g + 1) * NCMP],
                                   w2_sb[:, 1, c, :], start=(c == 0), stop=(c == 1))
            filled(mm, ("vcmp",))
            pe.wait_ge(consts_ready, 7)
            for t in range(NT):
                pe.wait_ge(vn_ready, t + 1)
                dst = begin(("spatial", t))
                for g in range(4):
                    mm = pe.matmul(dst[:, g * P:(g + 1) * P], vn[:, t, g * P:(g + 1) * P], wsT[:, g, :],
                                   start=True, stop=True)
                filled(mm, ("spatial", t))
            pe.wait_ge(q_ready, 4)
            pe.wait_ge(cmp_ready, 2)

            def q_of(hd, t):
                g = hd // 4
                return qT[g * DK:(g + 1) * DK, hd % 4, t * P:(t + 1) * P]

            for t in range(NT):
                for g in range(GROUPS):
                    dst = begin(("cs", t, g))
                    for c in range(4):
                        mm = pe.matmul(dst[:, c * NCMP:(c + 1) * NCMP], q_of(4 * g + c, t),
                                       kcT[g * DK:(g + 1) * DK, :], start=True, stop=True)
                    filled(mm, ("cs", t, g))
                pe.wait_ge(cp_ready, t + 1)
                for half in range(2):
                    dst = begin(("cpt", t, half))
                    for j in range(4):
                        hd = 4 * half + j
                        mm = pe.transpose(dst[0:NCMP, j * P:(j + 1) * P],
                                          sm[:, t % 3, hd * NCMP:(hd + 1) * NCMP], ident[:])
                    filled(mm, ("cpt", t, half))
                pe.wait_ge(cpt_ready, 2 * (t + 1))
                dst = begin(("co", t))
                for hd in range(HEADS):
                    mm = pe.matmul(dst[:, hd * DK:(hd + 1) * DK], pt[0:NCMP, hd // 4, hd % 4 * P:(hd % 4 + 1) * P],
                                   vc[:, hd // 4, :], start=True, stop=True)
                filled(mm, ("co", t))
            pe.wait_ge(kt_ready, 2)
            pe.wait_ge(vsw_ready, NT)
            nu = len(UNITS)
            for i in range(nu + 2):
                if i < nu:
                    t, br, hd = UNITS[i]
                    g = hd // 4
                    kT = (ksT, kwT)[br - 1]
                    dst = begin(("s", i))
                    n = (t + 1) * P
                    filled(pe.matmul(dst[:, 0:n], q_of(hd, t), kT[g * DK:(g + 1) * DK, 0:n], start=True, stop=True),
                           ("s", i))
                if 1 <= i <= nu:
                    t = UNITS[i - 1][0]
                    pe.wait_ge(probs_ready, i)
                    dst = begin(("pt", i - 1))
                    for kb in range(t + 1):
                        mm = pe.transpose(dst[:, kb * P:(kb + 1) * P], pr[:, (i - 1) % 3, kb * P:(kb + 1) * P], ident[:])
                    filled(mm, ("pt", i - 1))
                if i >= 2:
                    t, br, hd = UNITS[i - 2]
                    g = hd // 4
                    pe.wait_ge(pt_ready, i - 1)
                    dst = begin(("o", i - 2))
                    for kb in range(t + 1):
                        mm = pe.matmul(dst[:, 0:DK], pt[:, (i - 2) % 2, kb * P:(kb + 1) * P],
                                       vsw[:, kb, br - 1, g * DK:(g + 1) * DK], start=(kb == 0), stop=(kb == t))
                    filled(mm, ("o", i - 2))
            for t in range(NT):
                pe.wait_ge(o_added, 16 * (t + 1))
                dst = begin(("ot", t))
                for k in range(4):
                    mm = pe.transpose(dst[:, k * P:(k + 1) * P], otok[:, t, k * P:(k + 1) * P], ident[:])
                filled(mm, ("ot", t))
            for t in range(NM):
                turn(NT + t)
            all_turned(NT + NM)
            for c in range(KD):
                cols(("xk", c), ("xkv", 0), c, lambda k: mnT[:, k, :], MEM)
            for j in range(2):
                for t in range(NM):
                    rows(("xv", j, t), lambda k: mnT[:, k, t * P:(t + 1) * P], ("xkv", 0), 2 + j)
            pe.wait_ge(ot_ready, NT)
            pe.wait_ge(og_ready, NT)

            def item(ch, it):
                key, i = it[0], it[1]
                t0, n = CHUNKS[ch]
                tok = cols_of(ch)
                if key == "ab":
                    for r, pan, src in (("a", "nsa_out", oT), ("b", "gmlp_out", uT)):
                        name = (ch, pan, i // 4)
                        has_panel(pe, name)
                        w = panel(name, 4, 512)
                        product((r, ch, i), lambda k: w[:, k, i % 4 * P:(i % 4 + 1) * P], lambda k: src[:, k, tok],
                                4, n * P)
                elif key == "m":
                    name = (ch, "merge", i)
                    has_panel(pe, name)
                    w = panel(name, KD, 256)
                    for g in range(2):
                        product((f"m{g}", ch, i), lambda k: w[:, k, g * P:(g + 1) * P], lambda k: hnT[:, k, tok],
                                KD, n * P)
                elif key == "mix":
                    t = it[2]
                    pe.wait_ge(y_ready, KD * (ch + 1))
                    rows(("mix", ch, i, t), lambda k: yT[ch][:, k, t * P:(t + 1) * P], (ch, "mix", 0), i)
                elif key in ("nx", "np"):
                    if i < n:
                        turn(norm_no(key[1], t0 + i))
                elif key == "xq":
                    all_turned(norm_no("x", t0 + n - 1) + 1)
                    cols(("xqt", ch, i), (ch, "xq", 0), i, lambda k: hnX[ch][:, k, :], n * P)
                elif key == "xa":
                    if i < XH * n:
                        hd, t = divmod(i, n)
                        pe.wait_ge(xk_ready, KD)
                        pe.wait_ge(xq_ready, KD * ch + 2 * (hd + 1))
                        dst = begin(("xs", ch, i))
                        for k in range(2):
                            mm = pe.matmul(dst[:, 0:MEM], xqT[ch][:, 2 * hd + k, t * P:(t + 1) * P],
                                           xkT[:, 2 * hd + k, :], start=(k == 0), stop=(k == 1))
                        filled(mm, ("xs", ch, i))
                    if i >= 2:
                        hd, t = divmod(i - 2, n)
                        pe.wait_ge(xp_ready, unit_no(ch, i - 2))
                        dst = begin(("xpt", ch, i - 2))
                        for m in range(NM):
                            mm = pe.transpose(dst[:, m * P:(m + 1) * P], xpn[:, i % 2, m * P:(m + 1) * P], ident[:])
                        filled(mm, ("xpt", ch, i - 2))
                        if t == n - 1:
                            pe.wait_ge(xv_ready, 2 * NM)
                            pe.wait_ge(xpt_ready, unit_no(ch, i - 2))
                            for c in range(2):
                                product(("xot", ch, hd, c), lambda m: xv[:, m, hd * XD + c * P:hd * XD + (c + 1) * P],
                                        lambda m: xpT[:, m, 0:n * P], NM, n * P)
                elif key == "xo":
                    t = it[2]
                    pe.wait_ge(xo_ready, KD * (ch + 1))
                    rows(("xo", ch, i, t), lambda k: xoT[ch][:, k, t * P:(t + 1) * P], (ch, "xo", 0), i)

            for it in items(0):
                item(0, it)

            def project0(hd):
                pe.wait_ge(pw_loaded, 16 * (hd + 1))
                at_least(pe, pq0_ready, hd)
                for p in range(2):
                    for k in range(KD):
                        mm = pe.matmul(bank[:, PROJ0, p * P:(p + 1) * P], pw[:, k, p * P:(p + 1) * P], hnX[0][:, k, :],
                                       start=(k == 0), stop=(k == KD - 1))
                mm.then_inc(proj0_done, 1)

            def scores0(hd):
                pe.wait_ge(pq0_ready, hd + 1)
                at_least(pe, gate_ready, hd)
                for p in range(2):
                    mm = pe.matmul(bank[:, SCORES0, p * KEYS:(p + 1) * KEYS], pq0[:, p, :], pw[:, KD, p * P:(p + 1) * P],
                                   start=True, stop=True)
                mm.then_inc(scores0_done, 1)

            def project1(hd, p):
                if p == 0:
                    pe.wait_ge(pw_loaded, 16 * (PH + hd + 1))
                at_least(pe, pq1_ready, 2 * hd + p)
                for k in range(KD):
                    mm = pe.matmul(bank[:, PROJ1, 0:N1 * P], pw[:, k, p * P:(p + 1) * P], hnX[1][:, k, :],
                                   start=(k == 0), stop=(k == KD - 1))
                mm.then_inc(proj1_done, 1)

            def scores1(hd, part):
                pe.wait_ge(pq1_ready, 2 * hd + 2)
                at_least(pe, sc_copied, 2 * hd + part)
                tiles = range(2) if part == 0 else range(2, N1)
                for t in tiles:
                    for p in range(2):
                        at_col = (t % 2 * 2 + p) * KEYS
                        mm = pe.matmul(bank[:, SCORES1, at_col:at_col + KEYS], pq1[:, p, t * P:(t + 1) * P],
                                       pw[:, KD, p * P:(p + 1) * P], start=True, stop=True)
                mm.then_inc(scores1_done, 1)

            all_turned(norm_no("p", 0) + 1)
            for b in (PROJ0, SCORES0):
                was_read(pe, last_before[b])
            project0(0)
            scores0(0)
            for G in range(ALL0):
                hd, k = divmod(G, NG0)
                if hd + 1 < PH and k == 1:
                    project0(hd + 1)
                if hd + 1 < PH and k == 2:
                    scores0(hd + 1)
                for it in BESIDE[G]:
                    if it == ("q1", 0):
                        all_turned(len(NORMS))
                        for name in last_results:
                            was_read(pe, name)
                    if it[0] == "q1":
                        project1(0, it[1])
                    elif it[0] == "s1":
                        scores1(0, it[1])
                    elif it[0] != "t1":
                        item(1, it)

            pe.wait_ge(pq0_ready, PH)
            pe.wait_ge(gate_ready, PICKS0)

            def mix1(hd, i, k):
                b = hd * N1 + i
                pe.wait_ge(v1_loaded[k % VG], 16 * GE * (NG // VG * b + k // VG + 1))
                pe.wait_ge(diag1_ready, b * NG + k + 1)
                if k == 0:
                    at_least(pe, out1_added, b - N1 + 1)
                for j in range(GE):
                    for n in range(2):
                        mm = pe.matmul(bank[:, OUT1 + 2 * i + n, :], diag1[:, k % 2, j, :],
                                       V1[k % VG][:, j, n * 512:(n + 1) * 512],
                                       start=(k == 0 and j == 0), stop=(k == NG - 1 and j == GE - 1))
                mm.then_inc(v1_used, 1)

            def head(hd, more):
                for i in range(N1):
                    for k in range(NG):
                        mix1(hd, i, k)
                        if more and i == 0 and k in (0, 2):
                            project1(hd + 1, k // 2)
                        if more and i == 1 and k in (0, 2):
                            scores1(hd + 1, k // 2)

            head(0, True)
            with pe.Fori(1, PH - 1) as hd:
                head(hd, True)
            head(PH - 1, False)

        @block.scalar
        def _(act):
            link = Chain(act, act_chain)

            def rms_of(m, src, waste):
                link.link(act.activation(waste, src, ACT.Square, accum_out=ssq[:, m:m + 1]))
                act.activation(rms[:, m:m + 1], ssq[:, m:m + 1], ACT.Sqrt, bias=eps_col[:], scale=1.0 / D)\
                   .then_inc(rms_ready, 1)

            def copy_turned(m):
                src = need(act, ("turn", m, 0)).rearrange("p (k n) -> p k n", k=4)
                free(act.activation(turned_dst(m, 0), src, ACT.Copy), ("turn", m, 0))

            act.wait_ge(consts_ready, 6)
            for t in range(NT):
                act.wait_ge(x_loaded[t], 16)
                rms_of(t, h[:, t, :], sm[:].rearrange("p a n -> p (a n)")[:, 0:D])
            for t in range(NT):
                copy_turned(t)
            for c in range(4):
                src = need(act, ("q", c))
                free(act.activation(qT[:, c, :], src, ACT.Copy), ("q", c))
            for key, dst in ((("ks",), ksT), (("kw",), kwT)):
                src = need(act, key)
                free(act.activation(dst[:], src, ACT.Copy), key)
            src = need(act, ("gates",))
            free(act.activation(gates[:].rearrange("p t n -> p (t n)"), src[:, 0:NT * 24], ACT.Sigmoid), ("gates",))
            for t in range(NT):
                src = need(act, ("v", t))
                at_least(act, v_centred, t)
                free(act.activation(gv[:], src, ACT.Gelu, accum_out=vsum[:, 0, t:t + 1]), ("v", t))
                act.wait_ge(v_centred, t + 1)
                act.activation(vsum[:, 3, t:t + 1], vsum[:, 2, t:t + 1], ACT.Sqrt, bias=eps_col[:],
                               scale=1.0 / GW).then_inc(v_std, 1)
            act.wait_ge(small_loaded, 16 * 7)
            for i in range(2):
                src = need(act, ("hid", i))
                for c in range(2):
                    act.activation(hidT[:, i, c, :], src[:, c * P:c * P + 2 * NCMP], ACT.Gelu,
                                   bias=b1_sb[:, i, c:c + 1]).then_inc(hid_ready, 1)
            for c in range(4):
                src = need(act, ("u", c))
                free(act.activation(uT[:, c, :], src, ACT.Gelu), ("u", c))
            for t in range(NT):
                act.wait_ge(cs_ready, t + 1)
                act.activation(sm[:, t % 3, 0:HEADS * NCMP], sm[:, t % 3, 0:HEADS * NCMP], ACT.Exp,
                               scale=DK_SCALE).then_inc(cexp_ready, 1)
                if t:
                    need(act, ("co", t - 1))
                for half in range(2):
                    src = need(act, ("cpt", t, half))
                    free(act.activation(pt[0:NCMP, half, :], src[0:NCMP, :], ACT.Copy), ("cpt", t, half))
            need(act, ("co", NT - 1))
            nu = len(UNITS)
            for i in range(nu + 1):
                if i < nu:
                    n = (UNITS[i][0] + 1) * P
                    act.wait_ge(nmax_ready, i + 1)
                    if i >= 3:
                        need(act, ("pt", i - 3))
                    act.activation(pr[:, i % 3, 0:n], sm[:, i % 3, 0:n], ACT.Exp, bias=nmax[:, i:i + 1],
                                   scale=DK_SCALE, accum_out=rsum[:, i:i + 1]).then_inc(probs_ready, 1)
                if i >= 1:
                    n = (UNITS[i - 1][0] + 1) * P
                    src = need(act, ("pt", i - 1))
                    if i >= 3:
                        need(act, ("o", i - 3))
                    free(act.activation(pt[:, (i - 1) % 2, 0:n], src[:, 0:n], ACT.Copy), ("pt", i - 1))
            act.wait_ge(mem_loaded, 16 * NM)
            for t in range(NM):
                xn_free(act, NT + t)
                need(act, ("spatial", NT - 1))
                rms_of(NT + t, mtok[:, t, :], norm_dst(NT + t))
            for t in range(NT):
                src = need(act, ("ot", t)).rearrange("p (k n) -> p k n", k=4)
                free(act.activation(oT[:, :, t * P:(t + 1) * P], src, ACT.Copy), ("ot", t))
            for t in range(NM):
                copy_turned(NT + t)
            for c in range(KD):
                src = need(act, ("xk", c))
                free(act.activation(xkT[:, c, :], src[:, 0:MEM], ACT.Copy), ("xk", c))

            def item(ch, it):
                key, i = it[0], it[1]
                t0, n = CHUNKS[ch]
                if key == "m":
                    at_least(act, y_ready, KD * ch + i)
                    for g in range(2):
                        src = need(act, (f"m{g}", ch, i))
                        free(act.activation(sg[:, g, 0:n * P], src[:, 0:n * P], ACT.Sigmoid), (f"m{g}", ch, i))
                elif key in ("nx", "np"):
                    if i < n:
                        m = norm_no(key[1], t0 + i)
                        act.wait_ge(h1_ready if key == "nx" else h2_ready, nth(ch, 1, i))
                        xn_free(act, m)
                        rms_of(m, h[:, t0 + i, :], norm_dst(m))
                    if i:
                        copy_turned(norm_no(key[1], t0 + i - 1))
                elif key == "xq":
                    src = need(act, ("xqt", ch, i))
                    free(act.activation(xqT[ch][:, i, :], src[:, 0:n * P], ACT.Copy), ("xqt", ch, i))
                elif key == "xa":
                    if i < XH * n:
                        u = unit_no(ch, i)
                        src = need(act, ("xs", ch, i))
                        act.wait_ge(xnmax_ready, u)
                        at_least(act, xp_ready, u - 2)
                        free(act.activation(xp[:, i % 2, :], src[:, 0:MEM], ACT.Exp, bias=xst[:, 1, u - 1:u],
                                            scale=XD_SCALE, accum_out=xst[:, 2, u - 1:u]), ("xs", ch, i))
                    if i >= 2:
                        hd, t = divmod(i - 2, n)
                        src = need(act, ("xpt", ch, i - 2)).rearrange("p (m n) -> p m n", n=P)
                        if hd and t == 0:
                            need(act, ("xot", ch, hd - 1, 1))
                        free(act.activation(xpT[:, :, t * P:(t + 1) * P], src[:, 0:NM, :], ACT.Copy),
                             ("xpt", ch, i - 2))

            for it in items(0):
                item(0, it)

            def soft(q):
                act.wait_ge(soft_bias, q + 1)
                act.activation(ex[:], best[:], ACT.Exp, bias=pst[:, 0:1], accum_out=pst[:, 1:2])\
                   .then_inc(soft_exp, 1)

            def copy_query0(hd):
                act.wait_ge(proj0_done, hd + 1)
                act.activation(pq0[:].rearrange("p a n -> p (a n)"), bank[:, PROJ0, 0:2 * P], ACT.Copy)\
                   .then_inc(pq0_ready, 1)

            def next_head0(hd):
                act.wait_ge(scores0_done, hd + 1)
                act.dma_start(pw[:], peer_w[(hd + 1) % PH]).then_inc(pw_loaded, 16)

            def copy_query1(hd, p):
                act.wait_ge(proj1_done, 2 * hd + p + 1)
                act.activation(pq1[:, p, :], bank[:, PROJ1, 0:N1 * P], ACT.Copy).then_inc(pq1_ready, 1)

            def copy_scores1(hd, part):
                act.wait_ge(scores1_done, 2 * hd + part + 1)
                act.wait_ge(gate_ready, pick_no(hd, 0))
                tiles = slice(0, 2) if part == 0 else slice(2, N1)
                n = 2 * KEYS * (2 if part == 0 else N1 - 2)
                act.activation(scs[:, tiles, :, :].rearrange("p t a n -> p (t a n)"), bank[:, SCORES1, 0:n], ACT.Copy)\
                   .then_inc(sc_copied, 1)

            def diags(diag, slot, e0, count, signal):
                for j in range(count):
                    ins = act.activation(diag[:, slot, j, :], ident[:], ACT.Copy, scale=wgt[:, e0 + j:e0 + j + 1])
                ins.then_inc(signal, 1)

            copy_query0(0)
            next_head0(0)
            soft(0)
            for G in range(ALL0):
                hd, k = divmod(G, NG0)
                e = k * GE0
                act.wait_ge(dots0_done, (G + 1) * GE0)
                act.activation(gel[:, e:e + GE0], dot[:, e:e + GE0], ACT.Gelu).then_inc(gelu0_done, 1)
                if hd + 1 < PH and k == 1:
                    copy_query0(hd + 1)
                if hd + 1 < PH and k == 4:
                    next_head0(hd + 1)
                    soft(hd + 1)
                for it in BESIDE[G]:
                    if it[0] == "q1":
                        copy_query1(0, it[1])
                    elif it[0] == "s1":
                        copy_scores1(0, it[1])
                    elif it[0] == "t1":
                        soft(pick_no(0, it[1]))
                    else:
                        item(1, it)

            def gelus1(hd, i, k):
                act.wait_ge(dots1_done, (hd * N1 + i) * NG + k + 1)
                act.activation(gel[:, k * GE:(k + 1) * GE], dot[:, k * GE:(k + 1) * GE], ACT.Gelu)\
                   .then_inc(gelu1_done, 1)

            def diags1(hd, i, k):
                G = (hd * N1 + i) * NG + k
                act.wait_ge(w1_ready, G + 1)
                at_least(act, v1_used, G - 1)
                diags(diag1, k % 2, k * GE, GE, diag1_ready)

            def head(hd, more):
                for i in range(N1):
                    for k in range(NG):
                        gelus1(hd, i, k)
                        if k:
                            diags1(hd, i, k - 1)
                        if more and i == 0 and k == 2:
                            copy_query1(hd + 1, 0)
                        if more and i == 1 and k == 2:
                            copy_scores1(hd + 1, 0)
                        if more and i == 2 and k == 1:
                            soft(pick_no(hd + 1, 1))
                    diags1(hd, i, NG - 1)
                    if more and i == 0:
                        copy_query1(hd + 1, 1)
                    if more and i == 1:
                        copy_scores1(hd + 1, 1)
                        soft(pick_no(hd + 1, 0))
                    if more and i == 2:
                        soft(pick_no(hd + 1, 2))

            act.wait_ge(row0_added, ALL0 * GE0)
            head(0, True)
            with act.Fori(1, PH - 1) as hd:
                head(hd, True)
            head(PH - 1, False)
            act.wait_ge(v1_used, PH * N1 * NG)
            for t in range(NT):
                if t:
                    act.wait_ge(out1_added, (PH - 1) * N1 + t)
                rms_of(len(NORMS) + t, h[:, t, :], V1[0][:, t, :])

        @block.vector
        def _(dve):
            link = Chain(dve, dve_chain)

            def normalise(m, src, gain, dst, signal):
                dve.wait_ge(rms_ready, m + 1)
                link.link(dve.reciprocal(rinv[:, m:m + 1], rms[:, m:m + 1]))
                dve.scalar_tensor_tensor(out=dst, in0=src, scalar=rinv[:, m:m + 1], in1=gain,
                                         op0=ALU.mult, op1=ALU.mult).then_inc(signal, 1)

            def norm(m):
                kind, t = NORMS[m]
                n = ("mix", "mem", "x", "p").index(kind)
                dve.wait_ge(gain_loaded[n], 16)
                xn_free(dve, m)
                normalise(m, (mtok if kind == "mem" else h)[:, t, :], gb[n][:], norm_dst(m), normed)

            def copy_turned(m):
                src = need(dve, ("turn", m, 1)).rearrange("p (k n) -> p k n", k=4)
                free(dve.tensor_copy(turned_dst(m, 1), src), ("turn", m, 1))

            for t in range(NT):
                dve.wait_ge(x_loaded[t], 16)
                norm(t)
            for t in range(NT):
                copy_turned(t)
            dve.wait_ge(small_loaded, 16 * 7)
            for i in range(2):
                for g in range(GROUPS):
                    src = need(dve, ("kvc", 2 * i + g))
                    for par in range(2):
                        rows = slice(par * DK, (par + 1) * DK)
                        tok = src[rows, :].rearrange("p (c l q) -> p q l c", q=2, l=STRIDE // 2)[:, par, :, :]
                        for part in range(2):
                            ls = slice(part * STRIDE // 2, (part + 1) * STRIDE // 2)
                            pe_b = pe_sb[rows, i, ls].unsqueeze(2).broadcast_to([DK, STRIDE // 2, NCMP])
                            dve.tensor_tensor(blk[rows, i, ls, g, :], tok[:, :, part:part + NCMP], pe_b, ALU.add)\
                               .then_inc(blk_ready, 1)
            for t in range(NT):
                src = need(dve, ("vsw", t))
                free(dve.tensor_copy(vsw[:, t, :, :].rearrange("p b n -> p (b n)"), src[:, 0:256]), ("vsw", t))
            all_x_turned = NT
            dve.wait_ge(turned_act, all_x_turned)
            for t in range(NT):
                dve.wait_ge(v_gelu, t + 1)
                link.link(dve.tensor_scalar(vsum[:, 1, t:t + 1], vsum[:, 0, t:t + 1], -1.0 / GW, None, ALU.mult))
                link.link(dve.tensor_scalar(vn[:, t, :], gv[:], vsum[:, 1, t:t + 1], None, ALU.add))
                dve.tensor_tensor_reduce(out=gv[:], in0=vn[:, t, :], in1=vn[:, t, :], scale=1.0, scalar=0.0,
                                         op0=ALU.mult, op1=ALU.add, accum_out=vsum[:, 2, t:t + 1])\
                   .then_inc(v_centred, 1)
                dve.wait_ge(v_std, t + 1)
                link.link(dve.reciprocal(vsum[:, 0, t:t + 1], vsum[:, 3, t:t + 1]))
                link.link(dve.scalar_tensor_tensor(out=vn[:, t, :], in0=vn[:, t, :], scalar=vsum[:, 0, t:t + 1],
                                                   in1=ln_sb[:, 0, :], op0=ALU.mult, op1=ALU.mult))
                dve.tensor_tensor(vn[:, t, :], vn[:, t, :], ln_sb[:, 1, :], ALU.add).then_inc(vn_ready, 1)
            src = need(dve, ("kcmp",))
            free(dve.tensor_copy(kcT[:], src[:, 0:NCMP]), ("kcmp",))
            src = need(dve, ("vcmp",))
            free(dve.tensor_copy(vc[:].rearrange("p g n -> p (g n)"), src[0:NCMP, 0:GROUPS * DK]), ("vcmp",))
            dve.wait_ge(u_ready, 4)
            for t in range(NT):
                src = need(dve, ("spatial", t))
                tmp = gv[:].rearrange("p (g n) -> p g n", g=4)
                at_least(dve, og_ready, t)
                free(dve.tensor_tensor(gv[:], src, bs_sb[:].rearrange("p g n -> p (g n)"), ALU.add), ("spatial", t))
                was_read(dve, ("spatial", t))
                cols = slice(t * P, (t + 1) * P)
                dve.tensor_tensor(uT[:, :, cols], tmp, uT[:, :, cols], ALU.mult).then_inc(og_ready, 1)
            dve.wait_ge(gates_ready, 1)
            for t in range(NT):
                s8 = sm[:, t % 3, 0:HEADS * NCMP].rearrange("p (h c) -> p h c", h=HEADS)
                shape = [P, HEADS, NCMP]
                mask = cmask[:, t, :].unsqueeze(1).broadcast_to([P, 4, NCMP])
                keep = ckeep[:, t, :].unsqueeze(1).broadcast_to(shape)
                for g in range(GROUPS):
                    src = need(dve, ("cs", t, g))[:, 0:4 * NCMP].rearrange("p (h c) -> p h c", h=4)
                    free(dve.tensor_tensor(s8[:, 4 * g:4 * g + 4, :], src, mask, ALU.add), ("cs", t, g))
                was_read(dve, ("cs", t, 1))
                link.link(dve.tensor_reduce(cst[:, 0, :], s8, AX.X, ALU.max))
                dve.tensor_tensor(s8, s8, cst[:, 0, :].unsqueeze(2).broadcast_to(shape), ALU.subtract)\
                   .then_inc(cs_ready, 1)
                dve.wait_ge(cexp_ready, t + 1)
                dve.tensor_tensor(s8, s8, keep, ALU.mult).then_inc(cp_ready, 1)
                dve.wait_ge(cp_ready, t + 1)
                link.link(dve.tensor_reduce(cst[:, 1, :], s8, AX.X, ALU.add))
                link.link(dve.tensor_scalar(cst[:, 2, :], cst[:, 1, :], TINY, None, ALU.max))
                link.link(dve.reciprocal(cst[:, 3, :], cst[:, 2, :]))
                gate_c = gates[:, t, :].rearrange("p (h b) -> p h b", b=3)[:, :, 0]
                link.link(dve.tensor_tensor(cst[:, 2, :], cst[:, 3, :], gate_c, ALU.mult))
                src = need(dve, ("co", t)).rearrange("p (h d) -> p h d", h=HEADS)
                free(dve.tensor_tensor(otok[:, t, :].rearrange("p (h d) -> p h d", h=HEADS), src,
                                       cst[:, 2, :].unsqueeze(2).broadcast_to([P, HEADS, DK]), ALU.mult), ("co", t))
                was_read(dve, ("co", t))
            nu = len(UNITS)
            for i in range(nu + 2):
                if i < nu:
                    t = UNITS[i][0]
                    n = (t + 1) * P
                    src = need(dve, ("s", i))
                    if i >= 3:
                        dve.wait_ge(probs_ready, i - 2)
                    free(dve.tensor_tensor_reduce(out=sm[:, i % 3, 0:n], in0=src[:, 0:n],
                                                  in1=causal[:, (3 - t) * P:(3 - t) * P + n], scale=1.0, scalar=NEG,
                                                  op0=ALU.add, op1=ALU.max, accum_out=rmax[:, i:i + 1]), ("s", i))
                    was_read(dve, ("s", i))
                    dve.tensor_scalar(nmax[:, i:i + 1], rmax[:, i:i + 1], -DK_SCALE, None, ALU.mult)\
                       .then_inc(nmax_ready, 1)
                if i >= 2:
                    t, br, hd = UNITS[i - 2]
                    dve.wait_ge(probs_ready, i - 1)
                    link.link(dve.reciprocal(coef[:, i - 2:i - 1], rsum[:, i - 2:i - 1]))
                    link.link(dve.tensor_tensor(coef[:, i - 2:i - 1], coef[:, i - 2:i - 1],
                                                gates[:, t, 3 * hd + br:3 * hd + br + 1], ALU.mult))
                    src = need(dve, ("o", i - 2))
                    if br == 2:
                        dve.wait_ge(o_added, i - 2 - HEADS + 1)
                    o = otok[:, t, hd * DK:(hd + 1) * DK]
                    free(dve.scalar_tensor_tensor(out=o, in0=src[:, 0:DK], scalar=coef[:, i - 2:i - 1], in1=o,
                                                  op0=ALU.mult, op1=ALU.add), ("o", i - 2))
            for t in range(NM):
                norm(NT + t)
            for t in range(NM):
                copy_turned(NT + t)
            dve.wait_ge(s_read, nu)
            for j in range(2):
                for t in range(NM):
                    src = need(dve, ("xv", j, t))
                    free(dve.tensor_copy(xv[:, t, j * 512:(j + 1) * 512], src), ("xv", j, t))

            def item(ch, it):
                key, i = it[0], it[1]
                t0, n = CHUNKS[ch]
                w = n * P
                if key == "m":
                    dve.wait_ge(mg_ready, 2 * (KD * ch + i) + 2)
                    y = yT[ch][:, i, :]
                    src = need(dve, ("a", ch, i))
                    free(dve.tensor_tensor(y, src[:, 0:w], sg[:, 0, 0:w], ALU.mult), ("a", ch, i))
                    src = need(dve, ("b", ch, i))
                    free(dve.tensor_tensor(sg[:, 1, 0:w], src[:, 0:w], sg[:, 1, 0:w], ALU.mult), ("b", ch, i))
                    was_read(dve, ("a", ch, i))
                    was_read(dve, ("b", ch, i))
                    dve.tensor_tensor(y, y, sg[:, 1, 0:w], ALU.add).then_inc(y_ready, 1)
                elif key in ("mix", "xo"):
                    t = it[2]
                    src = need(dve, (key, ch, i, t))
                    part = h[:, t0 + t, i * 512:(i + 1) * 512]
                    free(dve.tensor_tensor(part, src, part, ALU.add), (key, ch, i, t))
                elif key in ("nx", "np"):
                    if i < n:
                        norm(norm_no(key[1], t0 + i))
                    if i:
                        copy_turned(norm_no(key[1], t0 + i - 1))
                elif key == "xa":
                    if i < XH * n:
                        u = unit_no(ch, i)
                        src = need(dve, ("xs", ch, i))
                        link.link(dve.tensor_reduce(xst[:, 0, u - 1:u], src[:, 0:MEM], AX.X, ALU.max))
                        dve.tensor_scalar(xst[:, 1, u - 1:u], xst[:, 0, u - 1:u], -XD_SCALE, None, ALU.mult)\
                           .then_inc(xnmax_ready, 1)
                    if 1 <= i <= XH * n:
                        f = i - 1
                        u = unit_no(ch, f)
                        dve.wait_ge(xexp_ready, u)
                        link.link(dve.reciprocal(xst[:, 3, u - 1:u], xst[:, 2, u - 1:u]))
                        if f >= 2:
                            need(dve, ("xpt", ch, f - 2))
                        dve.tensor_scalar(xpn[:, f % 2, :], xp[:, f % 2, :], xst[:, 3, u - 1:u], None, ALU.mult)\
                           .then_inc(xp_ready, 1)
                    if i >= 2 and (i - 2) % n == n - 1:
                        hd = (i - 2) // n
                        for c in range(2):
                            src = need(dve, ("xot", ch, hd, c))
                            free(dve.tensor_copy(xoT[ch][:, 2 * hd + c, :], src[:, 0:w]), ("xot", ch, hd, c))

            for it in items(0):
                item(0, it)

            peer = Chain(dve, dve_peer)

            def top16(values, rest, val, idx):
                peer.link(dve.max(val[:, 0:8], values))
                peer.step(dve.max_index(idx[:, 0:8], val[:, 0:8], values))
                peer.link(dve.match_replace(rest, val[:, 0:8], values, -3.0e38))
                peer.link(dve.max(val[:, 8:16], rest))
                peer.link(dve.max_index(idx[:, 8:16], val[:, 8:16], rest))

            def topk(q, slot, halves, ready, count, taken):
                at_least(dve, gate_ready, q)
                stand(dve, ready, count)
                for p in range(2):
                    top16(halves(p), sc_rest[:, p, :], hv[:, p, :], hi[:, p, :])
                grid = [P, TOPK, TOPK]
                peer.link(dve.tensor_tensor(cand[:], hv[:, 0, :].unsqueeze(2).broadcast_to(grid),
                                            hv[:, 1, :].unsqueeze(1).broadcast_to(grid), ALU.add))
                top16(cand[:].rearrange("p i j -> p (i j)"), cand_rest[:], best[:], pos[:])
                dve.tensor_scalar(pst[:, 0:1], best[:, 0:1], -1.0, None, ALU.mult).then_inc(soft_bias, 1)
                peer.step(dve.tensor_scalar(ij[:, 0, :], pos[:], 4, None, ALU.logical_shift_right))
                peer.step(dve.tensor_scalar(ij[:, 1, :], pos[:], TOPK - 1, None, ALU.bitwise_and))
                peer.link(dve.tensor_copy(hif[:], hi[:]))
                peer.link(dve.tensor_copy(ijf[:], ij[:]))
                for p in range(2):
                    peer.link(dve.tensor_tensor(hot[:], ijf[:, p, :].unsqueeze(2).broadcast_to(grid),
                                                iota16[:].unsqueeze(1).broadcast_to(grid), ALU.is_equal))
                    peer.link(dve.tensor_tensor(picked[:], hot[:], hif[:, p, :].unsqueeze(1).broadcast_to(grid),
                                                ALU.mult))
                    peer.link(dve.tensor_reduce(sel[:, p, :], picked[:], AX.X, ALU.add))
                at_least(dve, picks_taken, taken)
                dve.scalar_tensor_tensor(out=eidx[:, slot, :], in0=sel[:, 0, :], scalar=float(KEYS), in1=sel[:, 1, :],
                                         op0=ALU.mult, op1=ALU.add).then_inc(picks_ready, 1)
                dve.wait_ge(soft_exp, q + 1)
                peer.link(dve.reciprocal(pst[:, 2:3], pst[:, 1:2]))
                dve.tensor_scalar(gate[:, slot, :], ex[:], pst[:, 2:3], None, ALU.mult).then_inc(gate_ready, 1)

            def topk0(hd):
                topk(hd, N1 + hd % 2, lambda p: bank[:, SCORES0, p * KEYS:(p + 1) * KEYS], scores0_done, hd + 1, hd - 1)

            def topk1(hd, i):
                topk(pick_no(hd, i), i, lambda p: scs[:, i, p, :], sc_copied, 2 * hd + (1 if i < 2 else 2),
                     pick_no(hd, i) - N1 + 1)

            def dots(u_rows, act_rows, e0, signal):
                for j in range(len(u_rows)):
                    ins = dve.tensor_tensor_reduce(out=u_rows[j], in0=u_rows[j], in1=act_rows, scale=1.0, scalar=0.0,
                                                   op0=ALU.mult, op1=ALU.add, accum_out=dot[:, e0 + j:e0 + j + 1])
                ins.then_inc(signal, 1)

            def weigh(slot, es, signal):
                dve.tensor_tensor(wgt[:, es], gel[:, es], gate[:, slot, es], ALU.mult).then_inc(signal, 1)

            def weigh0(G):
                dve.wait_ge(gelu0_done, G + 1)
                e = G % NG0 * GE0
                weigh(N1 + G // NG0 % 2, slice(e, e + GE0), w0_ready)

            def add_row0(G, j):
                if j == 0:
                    dve.wait_ge(v0_loaded[G % VG0], 16 * GE0 * (G // VG0 + 1))
                    dve.wait_ge(w0_ready, G + 1)
                e = G % NG0 * GE0 + j
                at_least(dve, row0_added, G * GE0 + j)
                dve.scalar_tensor_tensor(out=h[:, 0, :], in0=V0[:, G % VG0, j, :], scalar=wgt[:, e:e + 1],
                                         in1=h[:, 0, :], op0=ALU.mult, op1=ALU.add).then_inc(row0_added, 1)

            topk0(0)
            steps = peer.n
            for G in range(ALL0 + 1):
                hd, k = divmod(G, NG0)
                if G == 0:
                    dve.wait_ge(gate_ready, 1)
                if G:
                    weigh0(G - 1)
                for j in range(GE0):
                    if G < ALL0:
                        if j == 0:
                            dve.wait_ge(u0_loaded[G % UG0], 16 * GE0 * (G // UG0 + 1))
                        dots([U0[:, G % UG0, j, :]], hp0[:], k * GE0 + j, dots0_done)
                    if G:
                        add_row0(G - 1, j)
                if G == ALL0:
                    break
                if hd + 1 < PH and k == 4:
                    topk0(hd + 1)
                for it in BESIDE[G]:
                    if it[0] == "t1":
                        topk1(0, it[1])
                    elif it[0] not in ("q1", "s1"):
                        item(1, it)

            def add_out1(b, i):
                dve.wait_ge(v1_used, NG * (b + 1))
                src = bank[:, OUT1 + 2 * i:OUT1 + 2 * i + 2, :].rearrange("p n c -> p (n c)")
                dve.tensor_tensor(h[:, i + 1, :], src, h[:, i + 1, :], ALU.add).then_inc(out1_added, 1)

            def weigh1(hd, i, k):
                dve.wait_ge(gelu1_done, (hd * N1 + i) * NG + k + 1)
                weigh(i, slice(k * GE, (k + 1) * GE), w1_ready)

            def head(hd, more):
                for i in range(N1):
                    b = hd * N1 + i
                    dve.wait_ge(gate_ready, pick_no(hd, i) + 1)
                    for k in range(NG):
                        dve.wait_ge(u1_loaded[k], 16 * GE * (b + 1))
                        dots([U1[:, k * GE + j, :] for j in range(GE)], hp1[:, i, :], k * GE, dots1_done)
                        if k:
                            weigh1(hd, i, k - 1)
                        if more and i == 2 and k == 1:
                            topk1(hd + 1, 1)
                    weigh1(hd, i, NG - 1)
                    if not (isinstance(b, int) and b == 0):
                        add_out1(b - 1, (i - 1) % N1)
                    if more and i >= 1:
                        topk1(hd + 1, 2 * (i - 1))

            head(0, True)
            with dve.Fori(1, PH - 1) as hd:
                peer.base, peer.n = hd * (N1 * steps) + (PICKS0 + N1) * steps, 0
                head(hd, True)
            peer.base, peer.n = (PICKS0 + N1 * PH) * steps, 0
            head(PH - 1, False)
            add_out1(PH * N1 - 1, N1 - 1)
            dve.wait_ge(gain_loaded[4], 16)
            dve.wait_ge(dots1_done, PH * N1 * NG)
            for t in range(NT):
                normalise(len(NORMS) + t, h[:, t, :], gb[4][:], hp0[:] if t == 0 else hp1[:, t - 1, :], final_ready)


def _panels(w):
    k, n = w.shape
    wide = 2048 // (k // P)
    return np.ascontiguousarray(w.reshape(k // P, P, n // wide, wide).transpose(2, 1, 0, 3)).reshape(-1, P, 2048)


def kernel(**inputs):
    import concourse.bacc as bacc
    from concourse.bass_utils import run_bass_kernel_spmd

    a = {k: np.asarray(v) for k, v in inputs.items()}
    w_in = a["w_in"]
    q0, kc0, vc0, ks0, vs0, kw0, vw0, g0, u0, v0, m0 = [int(i) for i in np.cumsum(
        [0, 512, 128, 128, 128, 128, 128, 128, 24, 512, 512])]
    cols = []
    for c in range(4):
        cols += [q0 + hd * DK + i for hd in (c, 4 + c) for i in range(DK)]
    for s in (kc0, vc0):
        for g in range(GROUPS):
            cols += [s + g * DK + i for _ in range(2) for i in range(DK)]
    for s, n in ((ks0, P), (kw0, P), (vs0, P), (vw0, P), (v0, GW), (u0, GW)):
        cols += list(range(s, s + n))
    for c in range(KD):
        for b in range(2):
            cols += list(range(m0 + b * D + c * P, m0 + b * D + (c + 1) * P))
    win = _panels(w_in[:, cols])
    w1 = [np.ascontiguousarray(a[f"cmp_w1_{s}"].reshape(2, BLOCK // 4, P, HID).transpose(0, 2, 1, 3)).reshape(2, P, 2048)
          for s in "kv"]
    w_panels = np.concatenate([win[0:8], w1[0], w1[1], win[8:10], _panels(a["w_xkv"]), _panels(a["w_nsa_out"]),
                               _panels(a["w_gmlp_out"]), win[10:18], _panels(a["w_mix_out"]), _panels(a["w_xq"]),
                               _panels(a["w_xo"])])
    peer_w = a["w_peer_q"].reshape(KD, P, PH, 2 * KEYS).transpose(2, 1, 0, 3)
    keys = a["peer_sub_keys"].transpose(0, 3, 1, 2).reshape(PH, P, 1, 2 * KEYS)
    pe = [a[f"cmp_pe_{s}"].reshape(BLOCK // 2, 2, DK).transpose(1, 2, 0).reshape(P, BLOCK // 2) for s in "kv"]
    arrays = {
        "x": a["x"].reshape(S, D), "mem": a["mem"].reshape(MEM, D),
        "gains": np.stack([a[k] for k in ("g_mix", "g_mem", "g_xattn", "g_peer", "g_final")]),
        "w_panels": w_panels,
        "w_gates": w_in[:, g0:g0 + 24].reshape(KD, P, 24).transpose(1, 0, 2),
        "cmp_pe": np.stack(pe, axis=1),
        "cmp_b1": np.stack([a[f"cmp_b1_{s}"].reshape(2, P).T for s in "kv"], axis=1),
        "cmp_w2": np.stack([a[f"cmp_w2_{s}"].reshape(2, P, DK).transpose(1, 0, 2) for s in "kv"], axis=1),
        "ln_gb": np.stack([a["gmlp_ln_g"], a["gmlp_ln_b"]]),
        "ws_t": a["gmlp_ws"].transpose(2, 0, 1),
        "bs": a["gmlp_bs"],
        "peer_w": np.concatenate([peer_w, keys], axis=2),
        "peer_u": a["peer_u"], "peer_v": a["peer_v"],
    }
    nc = bacc.Bacc("TRN2", target_bir_lowering=False, num_devices=1)
    feed, args = {}, []
    for name, v in arrays.items():
        v = np.ascontiguousarray(v)
        feed[name + "_dram"] = v
        args.append(nc.dram_tensor(name + "_dram", v.shape, mybir.dt.from_np(v.dtype), kind="ExternalInput").ap())
    args.append(nc.dram_tensor("out_dram", (S, D), F32, kind="ExternalOutput").ap())
    hybrid_block(nc, *args)
    r = run_bass_kernel_spmd(nc, [feed], core_ids=[0])
    return r.results[0]["out_dram"].reshape(1, S, D)
```

```python
import numpy as np
from contextlib import ExitStack

import concourse.bass as bass
from concourse import mybir

F32 = mybir.dt.float32
U32 = mybir.dt.uint32
ALU = mybir.AluOpType
ACT = mybir.ActivationFunctionType
AX = mybir.AxisListType

P = 128
S = 512
D = 1024
NT = S // P
KD = D // P
MEM = 256
NM = MEM // P
HEADS, DK, GROUPS = 8, 64, 2
BLOCK, STRIDE = 32, 16
NCMP = S // STRIDE - BLOCK // STRIDE + 1
HID = 256
GW = 512
XH, XD = 4, 256
PH, TOPK, KEYS = 8, 16, 128
EPS = 1e-6
NEG = -1e30
TINY = 1e-30
DK_SCALE = DK ** -0.5
XD_SCALE = XD ** -0.5

CHUNKS = [(0, 1), (1, NT - 1)]
N1 = NT - 1
PICKS0 = PH

GE = 4
NG = TOPK // GE
UG, VG = 4, 2
GE0 = 2
NG0 = TOPK // GE0
UG0, VG0 = 3, 2
ALL0 = PH * NG0
FIRST_TOPK = {0: 1, 3: 2}
FINAL_BESIDE = {0: 0, 2: 1}
BESIDE_FROM, BESIDE_GROUPS = 2, 62
PROJECT_AT, SCORES_AT, TOPK_AT = 0, 3, 4

NSLOT = 4


def chunk_panels(ch):
    out = []
    for c in range(KD):
        if c % 4 == 0:
            out += [((ch, "nsa_out", c // 4), 0), ((ch, "gmlp_out", c // 4), 1)]
        out.append(((ch, "merge", c), 2 + c % 2))
    rest = [(ch, "mix", j) for j in range(4)] + [(ch, "xq", j) for j in range(4)] + [(ch, "xo", j) for j in range(4)]
    return out + [(p, i % NSLOT) for i, p in enumerate(rest)]


PRE = ([("q", j) for j in range(2)] + [("kvc", j) for j in range(2)] + [("kT",), ("vsw",)] +
       [("v", j) for j in range(2)] + [("w1k", j) for j in range(2)] + [("w1v", j) for j in range(2)] +
       [("u", j) for j in range(2)] + [("xkv", j) for j in range(8)])
PANELS = [(p, (i + 2) % NSLOT) for i, p in enumerate(PRE)] + chunk_panels(0) + chunk_panels(1)


def source_panel(name):
    if not isinstance(name[0], int):
        return PRE.index(name)
    _, key, j = name
    first = {"nsa_out": 0, "gmlp_out": 2, "merge": 4, "mix": 12, "xq": 16, "xo": 20}[key]
    return len(PRE) + first + j


def last_result(panel):
    if isinstance(panel[0], int):
        ch, key, j = panel
        n = CHUNKS[ch][1]
        return {"nsa_out": ("m1", ch, 4 * j + 3), "gmlp_out": ("m1", ch, 4 * j + 3), "merge": ("m1", ch, j),
                "mix": ("mix", ch, j // 2, n - 1), "xq": ("xqt", ch, 2 * j + 1), "xo": ("xo", ch, j // 2, n - 1)}[key]
    key, j = panel[0], panel[1] if len(panel) > 1 else 0
    return {"q": ("q", 2 * j + 1), "kvc": ("kvc", 2 * j + 1), "kT": ("kw",), "vsw": ("vsw", NT - 1),
            "v": ("v", NT - 1), "w1k": ("hid", 0), "w1v": ("hid", 1), "u": ("u", 2 * j + 1),
            "xkv": ("xk", 2 * j + 1) if j < 4 else ("xv", (j - 4) // 2, NM - 1)}[key]


def slot_turns():
    seen, last, out = [0] * NSLOT, [None] * NSLOT, {}
    for name, s in PANELS:
        out[name] = (s, seen[s], last[s])
        seen[s] += 1
        last[s] = name
    return out


NORMS = ([("mix", t) for t in range(NT)] + [("mem", t) for t in range(NM)] +
         [(k, t) for t0, n in CHUNKS for k in "xp" for t in range(t0, t0 + n)])


def items(ch):
    n = CHUNKS[ch][1]
    out = [("y", c) for c in range(KD)]
    out += [it for i in range(n) for it in (("mix", 0, i), ("mix", 1, i), ("nx", i))] + [("nx", n)]
    out += [("xq", c) for c in range(KD)] + [("xa", e) for e in range(XH * n + 3)]
    return out + [it for i in range(n) for it in (("xo", 0, i), ("xo", 1, i), ("np", i))] + [("np", n)]


def item_results(ch, item):
    k, i = item[0], item[1]
    t0, n = CHUNKS[ch]
    if k == "y":
        return [(r, ch, i) for r in ("a", "b", "m0", "m1")]
    if k in ("mix", "xo"):
        return [(k, ch, i, item[2])]
    if k in ("nx", "np"):
        if i == 0:
            return []
        m = NORMS.index((k[1], t0 + i - 1))
        return [("turn", m, 0), ("turn", m, 1)]
    if k == "xq":
        return [("xqt", ch, i)]
    out = [("xs", ch, i)] if i < XH * n else []
    if i >= 3 and (i - 3) % n == n - 1:
        out += [("xot", ch, (i - 3) // n, 0), ("xot", ch, (i - 3) // n, 1)]
    if 2 <= i < XH * n + 2:
        out.append(("xpt", ch, i - 2))
    return out


def interleaved():
    cost = {"y": 12, "mix": 7, "nx": 2, "xq": 5, "xa": 3, "xo": 8, "np": 4, "q1": 4, "s1": 4, "t1": 20}
    seq = items(1) + [("q1", 0), ("q1", 1), ("s1", 0), ("s1", 1)] + [("t1", 0)]
    total, done, out = sum(cost[i[0]] for i in seq), 0, [[] for _ in range(ALL0)]
    for it in seq:
        out[BESIDE_FROM + done * (BESIDE_GROUPS - BESIDE_FROM) // total].append(it)
        done += cost[it[0]]
    assert out.index(next(g for g in out if ("q1", 0) in g)) > (PH - 2) * NG0 + TOPK_AT
    return out


def psum_turns():
    names = []
    for m in range(NT):
        names += [("turn", m, 0), ("turn", m, 1)]
    names += [("q", c) for c in range(4)] + [("kvc", c) for c in range(4)] + [("ks",), ("kw",)]
    names += [("vsw", t) for t in range(NT)] + [("gates",)] + [("v", t) for t in range(NT)]
    names += [("hid", 0), ("hid", 1)] + [("u", c) for c in range(4)]
    names += [n for m in range(NT, NT + NM) for n in (("turn", m, 0), ("turn", m, 1))]
    names += [n for it in FIRST for n in step_results(it)]
    out, last, used = {}, [None] * 8, [0] * 8
    beside = [n for it in items(1) for n in item_results(1, it)]
    for group, banks in ((names, 8), (beside, 6)):
        for i, n in enumerate(group):
            b = i % banks
            out[n] = (b, used[b], last[b])
            used[b] += 1
            last[b] = n
        if banks == 8:
            last_before = list(last)
    return out, last_before, last


def units():
    return [(t, br, h) for t in range(NT) for br in (1, 2) for h in range(HEADS)]


PT_LAG, O_LAG = 2, 4


def step_results(it):
    k, i = it[0], it[1]
    if k == "item":
        return item_results(0, it[1:])
    if k == "cmp":
        return [("kcmp",), ("vcmp",)]
    if k == "c":
        out = [("cs", i, 0), ("cs", i, 1)] if i < NT else []
        out += [("co", i - 2)] if i >= 2 else []
        return out + ([("cpt", i - 1, 0), ("cpt", i - 1, 1)] if 1 <= i <= NT else [])
    if k == "att":
        nu = len(units())
        return ([("s", i)] if i < nu else []) + ([("o", i - O_LAG)] if i >= O_LAG else []) + \
               ([("pt", i - PT_LAG)] if PT_LAG <= i < nu + PT_LAG else [])
    return [it]


def spread(a, b, cost):
    def price(it):
        return cost[it[1] if it[0] == "item" else it[0]]

    out, total_a, total_b = [], sum(map(price, a)), sum(map(price, b))
    a, b, done_a, done_b = list(a), list(b), 0, 0
    while a or b:
        if not b or (a and done_a * total_b <= done_b * total_a):
            done_a += price(a[0])
            out.append(a.pop(0))
        else:
            done_b += price(b[0])
            out.append(b.pop(0))
    return out


def first_part():
    cost = {"spatial": 1, "c": 1, "xk": 1, "xv": 2, "att": 2, "ot": 2, "y": 2, "mix": 2, "nx": 5, "xq": 1, "xa": 2,
            "xo": 2, "np": 5}
    n0 = len(units()) // NT + O_LAG
    out = [("cmp", 0)]
    out += spread([("spatial", t) for t in range(NT)] + [("c", i) for i in range(NT + 2)],
                  [("xk", c) for c in range(KD)], cost)
    out += spread([("att", i) for i in range(n0)], [("xv", j, t) for j in range(2) for t in range(NM)], cost)
    out += spread([("att", i) for i in range(n0, len(units()) + O_LAG)],
                  [("ot", 0)] + [("item",) + it for it in items(0)], cost)
    return out + [("ot", t) for t in range(1, NT)]


FIRST = first_part()


def at_least(eng, sem, value):
    if not isinstance(value, int) or value > 0:
        eng.wait_ge(sem, value)


def stand(eng, sem, value):
    at_least(eng, sem, value)
    if not isinstance(value, int):
        eng.nop(nofuse=True)


class Chain:

    def __init__(self, eng, sem):
        self.eng, self.sem, self.base, self.n = eng, sem, 0, 0

    def step(self, ins):
        ins.then_inc(self.sem, 1)
        self.n += 1

    def join(self, but=0):
        stand(self.eng, self.sem, self.base + self.n - but)

    def link(self, ins):
        self.step(ins)
        self.join()


def hybrid_block(nc, x, mem, gains, w_panels, w_gates, cmp_pe, cmp_b1, cmp_w2, ln_gb, ws_t, bs, peer_w,
                 peer_u, peer_v, out):
    ctx = ExitStack()
    with ctx:
        BASE = 16640

        def at(name, shape, kb, dt=F32):
            return nc.alloc_sbuf_tensor_at(name, shape, dt, offset=BASE + int(kb * 1024))

        ctx.enter_context(nc.sbuf_tensor("arena", [P, 52992], F32))

        h = at("h", [P, NT, D], 0)
        hnT = at("hnT", [P, KD, S], 16)
        hnX = [at("hnX0", [P, KD, P], 172), at("hnX1", [P, KD, N1 * P], 16)]
        W = [at(f"W{s}", [P, 2048], 40 + 8 * s) for s in range(NSLOT)]
        small_at = [32.0]

        def small(name, shape, dt=F32):
            n = (int(np.prod(shape[1:])) * 4 + 31) // 32 * 32
            v = at(name, shape, small_at[0], dt)
            small_at[0] += n / 1024
            assert small_at[0] <= 40
            return v

        ident = small("ident", [P, P])
        wg = small("wg", [P, KD, 24])
        gates = small("gates", [P, NT, 24])
        pe_sb = small("pe_sb", [P, 2, BLOCK // 2])
        b1_sb = small("b1_sb", [P, 2, 2])
        w2_sb = small("w2_sb", [P, 2, 2, DK])
        hid_kb = small_at[0]
        hidT = small("hidT", [P, 2, 2, GROUPS * NCMP])
        kcT = small("kcT", [P, NCMP])
        vc = small("vc", [NCMP, GROUPS, DK])
        cmask = small("cmask", [P, NT, NCMP])
        ckeep = small("ckeep", [P, NT, NCMP])
        ssq = small("ssq", [P, 20])
        rms = small("rms", [P, 20])
        rinv = small("rinv", [P, 20])
        vsum = small("vsum", [P, 4, NT])
        cst = small("cst", [P, 4, HEADS])
        rmax = small("rmax", [P, 64])
        nmax = small("nmax", [P, 64])
        rsum = small("rsum", [P, 64])
        coef = small("coef", [P, 64])
        xst = small("xst", [P, 4, XH * NT])
        eps_col = small("eps_col", [P, 1])
        iota16 = small("iota16", [P, TOPK])

        qT = at("qT", [P, 4, S], 72)
        ksT = at("ksT", [P, S], 80)
        kwT = at("kwT", [P, S], 82)
        vsw = at("vsw", [P, NT, 2, P], 84)
        blk = at("blk", [P, 2, BLOCK // 2, GROUPS, NCMP], 88)
        vn = at("vn", [P, NT, GW], 96)
        oT = at("oT", [P, 4, S], 104)
        uT = at("uT", [P, 4, S], 112)
        sm = at("sm", [P, 3, S], 120)
        pr = at("pr", [P, 4, S], 126)
        pt = at("pt", [P, 3, S], 178)
        yT = [at("yT0", [P, KD, P], 160), at("yT1", [P, KD, N1 * P], 124)]
        otok = at("otok", [P, NT, GW], 136)
        causal = at("causal", [P, 7 * P], 184)
        ln_sb = at("ln_sb", [P, 2, GW], 203)
        wsT = at("wsT", [P, 4, P], 134)
        bs_sb = at("bs_sb", [P, 4, P], 188)
        gv = at("gv", [P, GW], 176)
        xn = at("xn", [P, 2, D], 96)
        sg = [at("sg0", [P, 2, P], 164), at("sg1", [P, 2, N1 * P], 180)]
        gb = [at(f"gain{n}", [P, D], kb) for n, kb in enumerate((168, 172, 199, 203, 199))]
        xkT = at("xkT", [P, KD, MEM], 88)
        xv = at("xv", [P, NM, D], 144)
        xqT = [at("xqT0", [P, KD, P], 152), at("xqT1", [P, KD, N1 * P], 104)]
        xoT = [at("xoT0", [P, KD, P], 160), at("xoT1", [P, KD, N1 * P], 124)]
        mnT = at("mnT", [P, KD, MEM], 152)
        mtok = at("mtok", [P, NM, D], 160)
        xpT = [at("xpT0", [P, NM, P], 165), at("xpT1", [P, NM, N1 * P], 176)]
        xp = at("xp", [P, 2, MEM], 100)
        xpn = at("xpn", [P, 2, MEM], 102)
        hp0 = at("hp0", [P, D], 168)
        hp1 = at("hp1", [P, N1, D], 104)
        pw = at("pw", [P, KD + 1, 2 * KEYS], 190)
        eidx = at("eidx", [P, N1 + 2, TOPK], hid_kb, U32)
        row_no = at("row_no", [P, N1 + 2, TOPK], hid_kb + 0.3125, U32)
        gate = at("gate", [P, N1 + 2, TOPK], hid_kb + 0.625)
        sc_rest = at("sc_rest", [P, 2, KEYS], 185)
        cand = at("cand", [P, TOPK, TOPK], 186)
        cand_rest = at("cand_rest", [P, TOPK * TOPK], 187)
        hot = at("hot", [P, 2, TOPK, TOPK], 187)
        hv = at("hv", [P, 2, TOPK], 189)
        hi = at("hi", [P, 2, TOPK], 189.125, U32)
        hif = at("hif", [P, 2, TOPK], 189.25)
        ij = at("ij", [P, 2, TOPK], 189.375, U32)
        ijf = at("ijf", [P, 2, TOPK], 189.5)
        sel = at("sel", [P, 2, TOPK], 189.625)
        best = at("best", [P, TOPK], 189.75)
        pos = at("pos", [P, TOPK], 189.8125, U32)
        ex = at("ex", [P, TOPK], 189.875)
        pst = at("pst", [P, 4], 189.9375)
        dot = at("dot", [P, TOPK], hid_kb - 1)
        gel = at("gel", [P, TOPK], hid_kb - 1 + 0.0625)
        wgt = at("wgt", [P, TOPK], hid_kb - 1 + 0.125)
        U0 = [at(f"U0_{g}", [P, GE0, D], kb) for g, kb in enumerate((72, 80, 136))]
        V0 = at("V0", [P, VG0, GE0, D], 152)
        pq0 = at("pq0", [P, 2, P], 179)
        U1 = at("U1", [P, UG * GE, D], 40)
        V1 = [at(f"V1_{g}", [P, GE, D], kb) for g, kb in enumerate((136, 120))]
        pq1 = at("pq1", [P, 2, N1 * P], 176)
        scs = at("scs", [P, N1, 2, KEYS], 180)
        diag1 = at("diag1", [P, 2, GE, P], 152)

        bank = ctx.enter_context(nc.psum_tensor("bank", [P, 8, 512], F32))
        PROJ0, SCORES0 = 6, 7
        PROJ1, SCORES1, OUT1 = 0, 1, 2

        def sem(name):
            return ctx.enter_context(nc.semaphore(name))

        panel_loaded = [sem(f"panel_loaded{s}") for s in range(NSLOT)]
        bank_filled = [sem(f"bank_filled{b}") for b in range(8)]
        x_loaded = [sem(f"x_loaded{t}") for t in range(NT)]
        gain_loaded = [sem(f"gain_loaded{n}") for n in range(5)]
        mem_loaded, small_loaded, consts_ready = sem("mem_loaded"), sem("small_loaded"), sem("consts_ready")
        rms_ready, normed, turned_act, turned_dve = sem("rms_ready"), sem("normed"), sem("turned_act"), sem("turned_dve")
        spatial_read, cs_read, co_read, s_read, a_read, b_read = (sem("spatial_read"), sem("cs_read"), sem("co_read"),
                                                                  sem("s_read"), sem("a_read"), sem("b_read"))
        q_ready, blk_ready, kt_ready, vsw_ready = sem("q_ready"), sem("blk_ready"), sem("kt_ready"), sem("vsw_ready")
        gates_ready, v_gelu, v_centred, v_std = sem("gates_ready"), sem("v_gelu"), sem("v_centred"), sem("v_std")
        vn_ready, hid_ready, u_ready, cmp_ready = sem("vn_ready"), sem("hid_ready"), sem("u_ready"), sem("cmp_ready")
        og_ready, cs_ready, cexp_ready, cp_ready, cpt_ready = (sem("og_ready"), sem("cs_ready"), sem("cexp_ready"),
                                                              sem("cp_ready"), sem("cpt_ready"))
        nmax_ready, probs_ready, pt_ready, o_added = sem("nmax_ready"), sem("probs_ready"), sem("pt_ready"), sem("o_added")
        ot_ready, mg_ready, y_ready, h1_ready = sem("ot_ready"), sem("mg_ready"), sem("y_ready"), sem("h1_ready")
        xk_ready, xv_ready, xq_ready = sem("xk_ready"), sem("xv_ready"), sem("xq_ready")
        xnmax_ready, xexp_ready, xp_ready, xpt_ready, xo_ready, h2_ready = (
            sem("xnmax_ready"), sem("xexp_ready"), sem("xp_ready"), sem("xpt_ready"), sem("xo_ready"), sem("h2_ready"))
        pw_loaded, picks_taken, picks_ready, soft_bias, soft_exp, gate_ready = (
            sem("pw_loaded"), sem("picks_taken"), sem("picks_ready"), sem("soft_bias"), sem("soft_exp"), sem("gate_ready"))
        u0_loaded = [sem(f"u0_loaded{g}") for g in range(UG0)]
        v0_loaded = [sem(f"v0_loaded{g}") for g in range(VG0)]
        proj0_done, pq0_ready, scores0_done, dots0_done, gelu0_done, w0_ready, row0_added = (
            sem("proj0_done"), sem("pq0_ready"), sem("scores0_done"), sem("dots0_done"), sem("gelu0_done"),
            sem("w0_ready"), sem("row0_added"))
        u1_loaded = [sem(f"u1_loaded{g}") for g in range(UG)]
        v1_loaded = [sem(f"v1_loaded{g}") for g in range(VG)]
        proj1_done, pq1_ready, scores1_done, sc_copied = (
            sem("proj1_done"), sem("pq1_ready"), sem("scores1_done"), sem("sc_copied"))
        dots1_done, gelu1_done, w1_ready, diag1_ready, v1_used, out1_added = (
            sem("dots1_done"), sem("gelu1_done"), sem("w1_ready"), sem("diag1_ready"), sem("v1_used"), sem("out1_added"))
        final_ready, stored = sem("final_ready"), sem("stored")
        dve_chain, act_chain, pool_chain, dve_peer = sem("dve_chain"), sem("act_chain"), sem("pool_chain"), sem("dve_peer")

        slot_of = slot_turns()
        bank_of, last_before, last_results = psum_turns()
        UNITS = units()
        BESIDE = interleaved()

        def panel(name, k, n):
            return W[slot_of[name][0]][:, :].rearrange("p (k n) -> p k n", k=k, n=n)

        def has_panel(eng, name):
            s, n, _ = slot_of[name]
            eng.wait_ge(panel_loaded[s], 16 * (n + 1))

        def need(eng, name):
            b, n, _ = bank_of[name]
            eng.wait_ge(bank_filled[b], n + 1)
            return bank[:, b, :]

        def nth(ch, j, i):
            return 2 * CHUNKS[0][1] * ch + 2 * i + j + 1

        def unit_no(ch, e):
            return XH * CHUNKS[0][1] * ch + e + 1

        def read_signal(name):
            key, i = name[0], name[1] if len(name) > 1 else 0
            j = name[2] if len(name) > 2 else 0
            if key in ("mix", "xo"):
                return {"mix": h1_ready, "xo": h2_ready}[key], nth(*name[1:])
            if key in ("a", "b", "m0", "m1", "xqt"):
                n = KD * i + j + 1
                return {"a": (a_read, n), "b": (b_read, n), "m0": (mg_ready, 2 * n - 1), "m1": (mg_ready, 2 * n),
                        "xqt": (xq_ready, n)}[key]
            if key in ("xs", "xpt"):
                return {"xs": xexp_ready, "xpt": xpt_ready}[key], unit_no(i, j)
            if key == "xot":
                return xo_ready, KD * i + 2 * j + name[3] + 1
            return {"turn": (turned_dve if j else turned_act, i + 1), "q": (q_ready, i + 1), "kvc": (blk_ready, 4 * i + 4),
                    "ks": (kt_ready, 1), "kw": (kt_ready, 2), "vsw": (vsw_ready, i + 1), "gates": (gates_ready, 1),
                    "v": (v_gelu, i + 1), "hid": (hid_ready, 2 * i + 2), "u": (u_ready, i + 1),
                    "kcmp": (cmp_ready, 1), "vcmp": (cmp_ready, 2), "spatial": (spatial_read, i + 1),
                    "cs": (cs_read, 2 * i + j + 1), "cpt": (cpt_ready, 2 * i + j + 1), "co": (co_read, i + 1),
                    "s": (s_read, i + 1), "pt": (pt_ready, i + 1), "o": (o_added, i + 1), "ot": (ot_ready, i + 1),
                    "xk": (xk_ready, i + 1), "xv": (xv_ready, NM * i + j + 1)}[key]

        def free(ins, name):
            ins.then_inc(read_signal(name)[0], 1)

        def was_read(eng, name):
            eng.wait_ge(*read_signal(name))

        def norm_dst(m):
            kind, t = NORMS[m]
            if kind == "p":
                return hp0[:, :] if t == 0 else hp1[:, t - 1, :]
            return mtok[:, t, :] if kind == "mem" else xn[:, m % 2, :]

        def xn_free(eng, m):
            if NORMS[m][0] in ("mix", "x"):
                before = [b for b in range(m) if b % 2 == m % 2 and NORMS[b][0] in ("mix", "x")]
                if before:
                    need(eng, ("turn", before[-1], 1))

        def turned_dst(m, half):
            kind, t = NORMS[m]
            ks = slice(4 * half, 4 * half + 4)
            if kind == "mix":
                return hnT[:, ks, t * P:(t + 1) * P]
            if kind == "mem":
                return mnT[:, ks, t * P:(t + 1) * P]
            return hnX[0][:, ks, :] if t == 0 else hnX[1][:, ks, (t - 1) * P:t * P]

        def norm_no(kind, t):
            return NORMS.index((kind, t))

        def cols_of(ch):
            t0, n = CHUNKS[ch]
            return slice(t0 * P, (t0 + n) * P)

        def pick_no(hd, i):
            return PICKS0 + hd * N1 + i

        block = ctx.enter_context(nc.Block())

        @block.sync
        def _(sp):
            def gain(n):
                sp.dma_start(gb[n][:], gains[n, :].partition_broadcast(P)).then_inc(gain_loaded[n], 16)

            for t in range(NT):
                sp.dma_start(h[:, t, :], x[t * P:(t + 1) * P, :]).then_inc(x_loaded[t], 16)
                if t == 0:
                    gain(0)
            smalls = [(wg[:], w_gates), (pe_sb[:], cmp_pe), (b1_sb[:], cmp_b1), (w2_sb[:], cmp_w2),
                      (ln_sb[:], ln_gb.partition_broadcast(P)), (wsT[:], ws_t), (bs_sb[:], bs.partition_broadcast(P))]
            for i, (name, s) in enumerate(PANELS):
                before = slot_of[name][2]
                if i == len(PRE) + 4:
                    sp.wait_ge(vn_ready, NT)
                    gain(3)
                if before:
                    need(sp, last_result(before))
                sp.dma_start(W[s][:, :], w_panels[source_panel(name)]).then_inc(panel_loaded[s], 16)
                if i == 3:
                    for dst, src in smalls:
                        sp.dma_start(dst, src).then_inc(small_loaded, 16)
                    for n in (1, 2):
                        gain(n)
                    for t in range(NM):
                        sp.dma_start(mtok[:, t, :], mem[t * P:(t + 1) * P, :]).then_inc(mem_loaded, 16)
                    sp.dma_start(pw[:], peer_w[0]).then_inc(pw_loaded, 16)
            sp.wait_ge(normed, norm_no("x", NT - 1) + 1)
            gain(4)
            with sp.Fori(1, PH) as hd:
                sp.wait_ge(scores1_done, 2 * hd)
                sp.dma_start(pw[:], peer_w[bass.ds(hd, 1)].rearrange("o p k n -> (o p) k n")).then_inc(pw_loaded, 16)
            for t in range(NT):
                sp.wait_ge(final_ready, t + 1)
                sp.dma_start(out[t * P:(t + 1) * P, :], hp0[:, :] if t == 0 else hp1[:, t - 1, :]).then_inc(stored, 16)
            sp.wait_ge(stored, 16 * NT)

        @block.gpsimd
        def _(pool):
            pool.memset(ident[:], 0.0).then_inc(pool_chain, 1)
            pool.memset(causal[:], 0.0).then_inc(pool_chain, 1)
            pool.memset(cmask[:], 0.0).then_inc(pool_chain, 1)
            pool.memset(ckeep[:], 1.0).then_inc(pool_chain, 1)
            pool.memset(eps_col[:], EPS).then_inc(consts_ready, 1)
            pool.wait_ge(pool_chain, 4)
            pool.affine_select(out=ident[:], in_=ident[:], compare_op=ALU.not_equal, fill=1.0, base=0,
                               pattern=[[-1, P]], channel_multiplier=1).then_inc(consts_ready, 1)
            pool.affine_select(out=causal[:], in_=causal[:], compare_op=ALU.is_ge, fill=NEG, base=3 * P,
                               pattern=[[-1, 7 * P]], channel_multiplier=1).then_inc(consts_ready, 1)
            for m, f in ((cmask, NEG), (ckeep, 0.0)):
                pool.affine_select(out=m[:], in_=m[:], compare_op=ALU.is_ge, fill=f, base=1 - BLOCK,
                                   pattern=[[P, NT], [-STRIDE, NCMP]], channel_multiplier=1).then_inc(consts_ready, 1)
            pool.iota(iota16[:], [[1, TOPK]], base=0, channel_multiplier=0,
                      allow_small_or_imprecise_dtypes=True).then_inc(consts_ready, 1)
            pool.wait_ge(small_loaded, 16 * 7)
            pool.affine_select(out=wsT[:], in_=wsT[:], compare_op=ALU.is_ge, fill=0.0, base=0,
                               pattern=[[0, 4], [1, P]], channel_multiplier=-1).then_inc(consts_ready, 1)

            def gather(dst, table, slot, e, signal):
                pool.indirect_dma_start(dst, None, table, bass.IndirectOffsetOnAxis(
                    ap=row_no[:, slot, e:e + 1], axis=0)).then_inc(signal, 16)

            def take_picks(q, slot):
                stand(pool, picks_ready, q + 1)
                pool.tensor_copy(row_no[:, slot, :], eidx[:, slot, :]).then_inc(picks_taken, 1)
                stand(pool, picks_taken, q + 1)

            for G in range(ALL0 + 1):
                if G < ALL0 and G % NG0 == 0:
                    hd = G // NG0
                    at_least(pool, row0_added, (hd - 1) * TOPK)
                    take_picks(hd, N1 + hd % 2)
                for j in range(GE0):
                    if G < ALL0:
                        hd, k = divmod(G, NG0)
                        at_least(pool, dots0_done, GE0 * (G - UG0) + j + 1)
                        gather(U0[G % UG0][:, j, :], peer_u, N1 + hd % 2, k * GE0 + j, u0_loaded[G % UG0])
                    if G:
                        hd, k = divmod(G - 1, NG0)
                        at_least(pool, row0_added, GE0 * (G - 1 - VG0) + j + 1)
                        gather(V0[:, (G - 1) % VG0, j, :], peer_v, N1 + hd % 2, k * GE0 + j, v0_loaded[(G - 1) % VG0])


            def batch(hd, i):
                b = hd * N1 + i
                stand(pool, v1_used, NG * (b - N1 + 1))
                take_picks(PICKS0 + b, i)

                def rows_u(k):
                    stand(pool, dots1_done, b * NG + k - NG + 1)
                    for j in range(GE):
                        gather(U1[:, k * GE + j, :], peer_u, i, k * GE + j, u1_loaded[k])

                def rows_v(k):
                    stand(pool, v1_used, b * NG + k - VG + 1)
                    for j in range(GE):
                        gather(V1[k % VG][:, j, :], peer_v, i, k * GE + j, v1_loaded[k % VG])

                rows_u(0)
                rows_u(1)
                if isinstance(b, int) and b == 0:
                    pool.wait_ge(dots0_done, ALL0 * GE0)
                    pool.wait_ge(row0_added, ALL0 * GE0)
                rows_v(0)
                rows_u(2)
                rows_v(1)
                rows_u(3)
                rows_v(2)
                rows_v(3)

            for i in range(N1):
                batch(0, i)
            with pool.Fori(1, PH) as hd:
                for i in range(N1):
                    batch(hd, i)

        @block.tensor
        def _(pe):
            order = list(bank_of)

            def begin(name):
                assert order.pop(0) == name, name
                b, _, before = bank_of[name]
                if before:
                    was_read(pe, before)
                return bank[:, b, :]

            def filled(mm, name):
                mm.then_inc(bank_filled[bank_of[name][0]], 1)

            def all_turned(tiles):
                pe.wait_ge(turned_act, tiles)
                pe.wait_ge(turned_dve, tiles)

            def turn(m):
                pe.wait_ge(normed, m + 1)
                src = norm_dst(m)
                for half in range(2):
                    dst = begin(("turn", m, half))
                    for k in range(4):
                        kk = 4 * half + k
                        mm = pe.transpose(dst[:, k * P:(k + 1) * P], src[:, kk * P:(kk + 1) * P], ident[:])
                    filled(mm, ("turn", m, half))

            def product(name, w, act, k_tiles, width=512):
                dst = begin(name)[:, 0:width]
                for k in range(k_tiles):
                    mm = pe.matmul(dst, w(k), act(k), start=(k == 0), stop=(k == k_tiles - 1))
                filled(mm, name)

            def rows(name, act, first, j):
                dst = begin(name)
                for n in range(2):
                    pan = first[:-1] + (2 * j + n,)
                    has_panel(pe, pan)
                    w = panel(pan, KD, 256)
                    for k in range(KD):
                        mm = pe.matmul(dst[:, n * 256:(n + 1) * 256], act(k), w[:, k, :],
                                       start=(k == 0), stop=(k == KD - 1))
                filled(mm, name)

            def cols(key, first, c, act, width=512):
                pan = first[:-1] + (c // 2,)
                has_panel(pe, pan)
                w = panel(pan, KD, 256)
                product(key, lambda k: w[:, k, c % 2 * P:(c % 2 + 1) * P], act, KD, width)

            def hn(k):
                return hnT[:, k, :]

            pe.wait_ge(consts_ready, 6)
            for t in range(NT):
                turn(t)
            all_turned(NT)
            for key in ("q", "kvc"):
                for c in range(4):
                    cols((key, c), (key, 0), c, hn)
            has_panel(pe, ("kT",))
            w = panel(("kT",), KD, 256)
            for c, key in enumerate((("ks",), ("kw",))):
                product(key, lambda k: w[:, k, c * P:(c + 1) * P], hn, KD)
            has_panel(pe, ("vsw",))
            w = panel(("vsw",), KD, 256)
            for t in range(NT):
                product(("vsw", t), lambda k: hnT[:, k, t * P:(t + 1) * P], lambda k: w[:, k, :], KD, 256)
            pe.wait_ge(small_loaded, 16 * 7)
            dst = begin(("gates",))
            for t in range(NT):
                for k in range(KD):
                    mm = pe.matmul(dst[:, t * 24:(t + 1) * 24], hnT[:, k, t * P:(t + 1) * P], wg[:, k, :],
                                   start=(k == 0), stop=(k == KD - 1))
            filled(mm, ("gates",))
            for t in range(NT):
                rows(("v", t), lambda k: hnT[:, k, t * P:(t + 1) * P], ("v", 0), 0)
            for i, name in enumerate(("w1k", "w1v")):
                pe.wait_ge(blk_ready, 8 * (i + 1))
                w = []
                for j in range(2):
                    has_panel(pe, (name, j))
                    w.append(panel((name, j), BLOCK // 4, HID))
                dst = begin(("hid", i))
                for c in range(2):
                    for k in range(BLOCK // 2):
                        mm = pe.matmul(dst[:, c * P:c * P + 2 * NCMP], w[k // 8][:, k % 8, c * P:(c + 1) * P],
                                       blk[:, i, k, :, :].rearrange("p g c -> p (g c)"),
                                       start=(k == 0), stop=(k == BLOCK // 2 - 1))
                filled(mm, ("hid", i))
            for c in range(4):
                cols(("u", c), ("u", 0), c, hn)
            for t in range(NM):
                turn(NT + t)

            def compress():
                pe.wait_ge(hid_ready, 4)
                dst = begin(("kcmp",))
                for g in range(GROUPS):
                    for c in range(2):
                        mm = pe.matmul(dst[g * DK:(g + 1) * DK, 0:NCMP], w2_sb[:, 0, c, :],
                                       hidT[:, 0, c, g * NCMP:(g + 1) * NCMP], start=(c == 0), stop=(c == 1))
                filled(mm, ("kcmp",))
                dst = begin(("vcmp",))
                for g in range(GROUPS):
                    for c in range(2):
                        mm = pe.matmul(dst[0:NCMP, g * DK:(g + 1) * DK], hidT[:, 1, c, g * NCMP:(g + 1) * NCMP],
                                       w2_sb[:, 1, c, :], start=(c == 0), stop=(c == 1))
                filled(mm, ("vcmp",))

            def spatial(t):
                pe.wait_ge(consts_ready, 7)
                pe.wait_ge(vn_ready, t + 1)
                dst = begin(("spatial", t))
                for g in range(4):
                    mm = pe.matmul(dst[:, g * P:(g + 1) * P], vn[:, t, g * P:(g + 1) * P], wsT[:, g, :],
                                   start=True, stop=True)
                filled(mm, ("spatial", t))

            def q_of(hd, t):
                g = hd // 4
                return qT[g * DK:(g + 1) * DK, hd % 4, t * P:(t + 1) * P]

            def compressed(i):
                if i < NT:
                    pe.wait_ge(q_ready, 4)
                    pe.wait_ge(cmp_ready, 2)
                    for g in range(GROUPS):
                        dst = begin(("cs", i, g))
                        for c in range(4):
                            mm = pe.matmul(dst[:, c * NCMP:(c + 1) * NCMP], q_of(4 * g + c, i),
                                           kcT[g * DK:(g + 1) * DK, :], start=True, stop=True)
                        filled(mm, ("cs", i, g))
                if i >= 2:
                    pe.wait_ge(cpt_ready, 2 * (i - 1))
                    dst = begin(("co", i - 2))
                    for hd in range(HEADS):
                        mm = pe.matmul(dst[:, hd * DK:(hd + 1) * DK],
                                       pt[0:NCMP, hd // 4, hd % 4 * P:(hd % 4 + 1) * P], vc[:, hd // 4, :],
                                       start=True, stop=True)
                    filled(mm, ("co", i - 2))
                if 1 <= i <= NT:
                    pe.wait_ge(cp_ready, i)
                    for half in range(2):
                        dst = begin(("cpt", i - 1, half))
                        for j in range(4):
                            hd = 4 * half + j
                            mm = pe.transpose(dst[0:NCMP, j * P:(j + 1) * P],
                                              sm[:, (i - 1) % 3, hd * NCMP:(hd + 1) * NCMP], ident[:])
                        filled(mm, ("cpt", i - 1, half))

            nu = len(UNITS)

            def attend(i):
                if i < nu:
                    t, br, hd = UNITS[i]
                    g = hd // 4
                    kT = (ksT, kwT)[br - 1]
                    pe.wait_ge(kt_ready, 2)
                    dst = begin(("s", i))
                    n = (t + 1) * P
                    filled(pe.matmul(dst[:, 0:n], q_of(hd, t), kT[g * DK:(g + 1) * DK, 0:n], start=True, stop=True),
                           ("s", i))
                if i >= O_LAG:
                    u = i - O_LAG
                    t, br, hd = UNITS[u]
                    g = hd // 4
                    pe.wait_ge(vsw_ready, NT)
                    pe.wait_ge(pt_ready, u + 1)
                    dst = begin(("o", u))
                    for kb in range(t + 1):
                        mm = pe.matmul(dst[:, 0:DK], pt[:, u % 3, kb * P:(kb + 1) * P],
                                       vsw[:, kb, br - 1, g * DK:(g + 1) * DK], start=(kb == 0), stop=(kb == t))
                    filled(mm, ("o", u))
                if PT_LAG <= i < nu + PT_LAG:
                    u = i - PT_LAG
                    pe.wait_ge(probs_ready, u + 1)
                    dst = begin(("pt", u))
                    for kb in range(UNITS[u][0] + 1):
                        mm = pe.transpose(dst[:, kb * P:(kb + 1) * P], pr[:, u % 4, kb * P:(kb + 1) * P], ident[:])
                    filled(mm, ("pt", u))

            def turn_output(t):
                pe.wait_ge(o_added, 16 * (t + 1))
                dst = begin(("ot", t))
                for k in range(4):
                    mm = pe.transpose(dst[:, k * P:(k + 1) * P], otok[:, t, k * P:(k + 1) * P], ident[:])
                filled(mm, ("ot", t))

            def item(ch, it):
                key, i = it[0], it[1]
                t0, n = CHUNKS[ch]
                tok = cols_of(ch)
                if key == "y":
                    pe.wait_ge(ot_ready, t0 + n)
                    pe.wait_ge(og_ready, t0 + n)
                    for r, pan, src in (("a", "nsa_out", oT), ("b", "gmlp_out", uT)):
                        name = (ch, pan, i // 4)
                        has_panel(pe, name)
                        w = panel(name, 4, 512)
                        product((r, ch, i), lambda k: w[:, k, i % 4 * P:(i % 4 + 1) * P], lambda k: src[:, k, tok],
                                4, n * P)
                    name = (ch, "merge", i)
                    has_panel(pe, name)
                    w = panel(name, KD, 256)
                    for g in range(2):
                        product((f"m{g}", ch, i), lambda k: w[:, k, g * P:(g + 1) * P], lambda k: hnT[:, k, tok],
                                KD, n * P)
                elif key == "mix":
                    t = it[2]
                    pe.wait_ge(y_ready, KD * (ch + 1))
                    rows(("mix", ch, i, t), lambda k: yT[ch][:, k, t * P:(t + 1) * P], (ch, "mix", 0), i)
                elif key in ("nx", "np"):
                    if i:
                        turn(norm_no(key[1], t0 + i - 1))
                elif key == "xq":
                    all_turned(norm_no("x", t0 + n - 1) + 1)
                    cols(("xqt", ch, i), (ch, "xq", 0), i, lambda k: hnX[ch][:, k, :], n * P)
                elif key == "xa":
                    if i < XH * n:
                        hd, t = divmod(i, n)
                        pe.wait_ge(xk_ready, KD)
                        pe.wait_ge(xq_ready, KD * ch + 2 * (hd + 1))
                        dst = begin(("xs", ch, i))
                        for k in range(2):
                            mm = pe.matmul(dst[:, 0:MEM], xqT[ch][:, 2 * hd + k, t * P:(t + 1) * P],
                                           xkT[:, 2 * hd + k, :], start=(k == 0), stop=(k == 1))
                        filled(mm, ("xs", ch, i))
                    if i >= 3 and (i - 3) % n == n - 1:
                        hd = (i - 3) // n
                        pe.wait_ge(xv_ready, 2 * NM)
                        pe.wait_ge(xpt_ready, unit_no(ch, i - 3))
                        for c in range(2):
                            product(("xot", ch, hd, c), lambda m: xv[:, m, hd * XD + c * P:hd * XD + (c + 1) * P],
                                    lambda m: xpT[ch][:, m, 0:n * P], NM, n * P)
                    if 2 <= i < XH * n + 2:
                        pe.wait_ge(xp_ready, unit_no(ch, i - 2))
                        dst = begin(("xpt", ch, i - 2))
                        for m in range(NM):
                            mm = pe.transpose(dst[:, m * P:(m + 1) * P], xpn[:, i % 2, m * P:(m + 1) * P], ident[:])
                        filled(mm, ("xpt", ch, i - 2))
                elif key == "xo":
                    t = it[2]
                    pe.wait_ge(xo_ready, KD * (ch + 1))
                    rows(("xo", ch, i, t), lambda k: xoT[ch][:, k, t * P:(t + 1) * P], (ch, "xo", 0), i)

            for it in FIRST:
                key, i = it[0], it[1]
                if key == "item":
                    item(0, it[1:])
                elif key == "xk":
                    all_turned(NT + NM)
                    cols(it, ("xkv", 0), i, lambda k: mnT[:, k, :], MEM)
                elif key == "xv":
                    t = it[2]
                    rows(it, lambda k: mnT[:, k, t * P:(t + 1) * P], ("xkv", 0), 2 + i)
                else:
                    {"cmp": lambda _: compress(), "spatial": spatial, "c": compressed, "att": attend,
                     "ot": turn_output}[key](i)

            def project0(hd):
                pe.wait_ge(pw_loaded, 16 * (hd + 1))
                at_least(pe, pq0_ready, hd)
                for p in range(2):
                    for k in range(KD):
                        mm = pe.matmul(bank[:, PROJ0, p * P:(p + 1) * P], pw[:, k, p * P:(p + 1) * P], hnX[0][:, k, :],
                                       start=(k == 0), stop=(k == KD - 1))
                mm.then_inc(proj0_done, 1)

            def scores0(hd):
                pe.wait_ge(pq0_ready, hd + 1)
                at_least(pe, gate_ready, hd)
                for p in range(2):
                    mm = pe.matmul(bank[:, SCORES0, p * KEYS:(p + 1) * KEYS], pq0[:, p, :], pw[:, KD, p * P:(p + 1) * P],
                                   start=True, stop=True)
                mm.then_inc(scores0_done, 1)

            def project1(hd, p):
                if p == 0:
                    pe.wait_ge(pw_loaded, 16 * (PH + hd + 1))
                at_least(pe, pq1_ready, 2 * hd + p)
                for k in range(KD):
                    mm = pe.matmul(bank[:, PROJ1, 0:N1 * P], pw[:, k, p * P:(p + 1) * P], hnX[1][:, k, :],
                                   start=(k == 0), stop=(k == KD - 1))
                mm.then_inc(proj1_done, 1)

            def scores1(hd, part):
                pe.wait_ge(pq1_ready, 2 * hd + 2)
                at_least(pe, sc_copied, 2 * hd + part)
                tiles = range(2) if part == 0 else range(2, N1)
                for t in tiles:
                    for p in range(2):
                        at_col = (t % 2 * 2 + p) * KEYS
                        mm = pe.matmul(bank[:, SCORES1, at_col:at_col + KEYS], pq1[:, p, t * P:(t + 1) * P],
                                       pw[:, KD, p * P:(p + 1) * P], start=True, stop=True)
                mm.then_inc(scores1_done, 1)

            all_turned(norm_no("p", 0) + 1)
            for b in (PROJ0, SCORES0):
                was_read(pe, last_before[b])
            project0(0)
            scores0(0)
            for G in range(ALL0):
                hd, k = divmod(G, NG0)
                if hd + 1 < PH and k == PROJECT_AT:
                    project0(hd + 1)
                if hd + 1 < PH and k == SCORES_AT:
                    scores0(hd + 1)
                for it in BESIDE[G]:
                    if it == ("q1", 0):
                        all_turned(len(NORMS))
                        for name in last_results:
                            was_read(pe, name)
                    if it[0] == "q1":
                        project1(0, it[1])
                    elif it[0] == "s1":
                        scores1(0, it[1])
                    elif it[0] != "t1":
                        item(1, it)

            pe.wait_ge(pq0_ready, PH)
            pe.wait_ge(gate_ready, PICKS0)

            def mix1(hd, i, k, stop=NG - 1):
                b = hd * N1 + i
                pe.wait_ge(v1_loaded[k % VG], 16 * GE * (NG // VG * b + k // VG + 1))
                pe.wait_ge(diag1_ready, b * NG + k + 1)
                if k == 0:
                    at_least(pe, out1_added, b - N1 + 1)
                for j in range(GE):
                    for n in range(2):
                        mm = pe.matmul(bank[:, OUT1 + 2 * i + n, :], diag1[:, k % 2, j, :],
                                       V1[k % VG][:, j, n * 512:(n + 1) * 512],
                                       start=(k == 0 and j == 0), stop=(k == stop and j == GE - 1))
                mm.then_inc(v1_used, 1)

            def head(hd, more, last=False):
                for i in range(N1):
                    groups = NG - 1 if last and i == N1 - 1 else NG
                    for k in range(groups):
                        mix1(hd, i, k, groups - 1)
                        if more and i == 0 and k in (0, 2):
                            project1(hd + 1, k // 2)
                        if more and i == 1 and k in (0, 2):
                            scores1(hd + 1, k // 2)

            head(0, True)
            with pe.Fori(1, PH - 1) as hd:
                head(hd, True)
            head(PH - 1, False, last=True)

        @block.scalar
        def _(act):
            link = Chain(act, act_chain)

            def rms_of(m, src, waste):
                link.link(act.activation(waste, src, ACT.Square, accum_out=ssq[:, m:m + 1]))
                act.activation(rms[:, m:m + 1], ssq[:, m:m + 1], ACT.Sqrt, bias=eps_col[:], scale=1.0 / D)\
                   .then_inc(rms_ready, 1)

            def copy_turned(m):
                src = need(act, ("turn", m, 0)).rearrange("p (k n) -> p k n", k=4)
                free(act.activation(turned_dst(m, 0), src, ACT.Copy), ("turn", m, 0))

            act.wait_ge(consts_ready, 6)
            for t in range(NT):
                act.wait_ge(x_loaded[t], 16)
                rms_of(t, h[:, t, :], sm[:].rearrange("p a n -> p (a n)")[:, 0:D])
            for t in range(NT):
                copy_turned(t)
            for c in range(4):
                src = need(act, ("q", c))
                free(act.activation(qT[:, c, :], src, ACT.Copy), ("q", c))
            for key, dst in ((("ks",), ksT), (("kw",), kwT)):
                src = need(act, key)
                free(act.activation(dst[:], src, ACT.Copy), key)
            act.wait_ge(mem_loaded, 16 * NM)
            for t in range(NM):
                rms_of(NT + t, mtok[:, t, :], oT[:, 0:2, :].rearrange("p k n -> p (k n)"))
            src = need(act, ("gates",))
            free(act.activation(gates[:].rearrange("p t n -> p (t n)"), src[:, 0:NT * 24], ACT.Sigmoid), ("gates",))
            for t in range(NT):
                src = need(act, ("v", t))
                at_least(act, v_centred, t)
                free(act.activation(gv[:], src, ACT.Gelu, accum_out=vsum[:, 0, t:t + 1]), ("v", t))
                act.wait_ge(v_centred, t + 1)
                act.activation(vsum[:, 3, t:t + 1], vsum[:, 2, t:t + 1], ACT.Sqrt, bias=eps_col[:],
                               scale=1.0 / GW).then_inc(v_std, 1)
            act.wait_ge(small_loaded, 16 * 7)
            for i in range(2):
                src = need(act, ("hid", i))
                for c in range(2):
                    act.activation(hidT[:, i, c, :], src[:, c * P:c * P + 2 * NCMP], ACT.Gelu,
                                   bias=b1_sb[:, i, c:c + 1]).then_inc(hid_ready, 1)
            for c in range(4):
                src = need(act, ("u", c))
                free(act.activation(uT[:, c, :], src, ACT.Gelu), ("u", c))
            for t in range(NM):
                copy_turned(NT + t)

            def compressed(i):
                if i < NT:
                    act.wait_ge(cs_ready, i + 1)
                    act.activation(sm[:, i % 3, 0:HEADS * NCMP], sm[:, i % 3, 0:HEADS * NCMP], ACT.Exp,
                                   scale=DK_SCALE).then_inc(cexp_ready, 1)
                if 1 <= i <= NT:
                    if i >= 2:
                        need(act, ("co", i - 2))
                    for half in range(2):
                        src = need(act, ("cpt", i - 1, half))
                        free(act.activation(pt[0:NCMP, half, :], src[0:NCMP, :], ACT.Copy), ("cpt", i - 1, half))

            nu = len(UNITS)

            def attend(i):
                if i < nu:
                    n = (UNITS[i][0] + 1) * P
                    act.wait_ge(nmax_ready, i + 1)
                    if i >= 4:
                        need(act, ("pt", i - 4))
                    act.activation(pr[:, i % 4, 0:n], sm[:, i % 3, 0:n], ACT.Exp, bias=nmax[:, i:i + 1],
                                   scale=DK_SCALE, accum_out=rsum[:, i:i + 1]).then_inc(probs_ready, 1)
                if PT_LAG <= i < nu + PT_LAG:
                    u = i - PT_LAG
                    n = (UNITS[u][0] + 1) * P
                    src = need(act, ("pt", u))
                    need(act, ("o", u - 3) if u >= 3 else ("co", NT - 1))
                    free(act.activation(pt[:, u % 3, 0:n], src[:, 0:n], ACT.Copy), ("pt", u))

            def item(ch, it):
                key, i = it[0], it[1]
                t0, n = CHUNKS[ch]
                if key == "y":
                    at_least(act, y_ready, KD * ch + i)
                    for g in range(2):
                        src = need(act, (f"m{g}", ch, i))
                        free(act.activation(sg[ch][:, g, 0:n * P], src[:, 0:n * P], ACT.Sigmoid), (f"m{g}", ch, i))
                elif key in ("nx", "np"):
                    if i < n:
                        m = norm_no(key[1], t0 + i)
                        act.wait_ge(h1_ready if key == "nx" else h2_ready, nth(ch, 1, i))
                        xn_free(act, m)
                        rms_of(m, h[:, t0 + i, :], norm_dst(m))
                    if i:
                        copy_turned(norm_no(key[1], t0 + i - 1))
                elif key == "xq":
                    src = need(act, ("xqt", ch, i))
                    free(act.activation(xqT[ch][:, i, :], src[:, 0:n * P], ACT.Copy), ("xqt", ch, i))
                elif key == "xa":
                    if i < XH * n:
                        u = unit_no(ch, i)
                        src = need(act, ("xs", ch, i))
                        act.wait_ge(xnmax_ready, u)
                        at_least(act, xp_ready, u - 2)
                        free(act.activation(xp[:, i % 2, :], src[:, 0:MEM], ACT.Exp, bias=xst[:, 1, u - 1:u],
                                            scale=XD_SCALE, accum_out=xst[:, 2, u - 1:u]), ("xs", ch, i))
                    if 2 <= i < XH * n + 2:
                        hd, t = divmod(i - 2, n)
                        src = need(act, ("xpt", ch, i - 2)).rearrange("p (m n) -> p m n", n=P)
                        if hd and t == 0:
                            need(act, ("xot", ch, hd - 1, 1))
                        free(act.activation(xpT[ch][:, :, t * P:(t + 1) * P], src[:, 0:NM, :], ACT.Copy),
                             ("xpt", ch, i - 2))

            for it in FIRST:
                key, i = it[0], it[1]
                if key == "item":
                    item(0, it[1:])
                elif key == "c":
                    compressed(i)
                elif key == "att":
                    attend(i)
                elif key == "xk":
                    src = need(act, it)
                    free(act.activation(xkT[:, i, :], src[:, 0:MEM], ACT.Copy), it)
                elif key == "ot":
                    src = need(act, it).rearrange("p (k n) -> p k n", k=4)
                    free(act.activation(oT[:, :, i * P:(i + 1) * P], src, ACT.Copy), it)

            def soft(q):
                act.wait_ge(soft_bias, q + 1)
                act.activation(ex[:], best[:], ACT.Exp, bias=pst[:, 0:1], accum_out=pst[:, 1:2])\
                   .then_inc(soft_exp, 1)

            def copy_query0(hd):
                act.wait_ge(proj0_done, hd + 1)
                act.activation(pq0[:].rearrange("p a n -> p (a n)"), bank[:, PROJ0, 0:2 * P], ACT.Copy)\
                   .then_inc(pq0_ready, 1)

            def next_head0(hd):
                act.wait_ge(scores0_done, hd + 1)
                act.dma_start(pw[:], peer_w[(hd + 1) % PH]).then_inc(pw_loaded, 16)

            def copy_query1(hd, p):
                act.wait_ge(proj1_done, 2 * hd + p + 1)
                act.activation(pq1[:, p, :], bank[:, PROJ1, 0:N1 * P], ACT.Copy).then_inc(pq1_ready, 1)

            def copy_scores1(hd, part):
                act.wait_ge(scores1_done, 2 * hd + part + 1)
                act.wait_ge(gate_ready, pick_no(hd, 0))
                tiles = slice(0, 2) if part == 0 else slice(2, N1)
                n = 2 * KEYS * (2 if part == 0 else N1 - 2)
                act.activation(scs[:, tiles, :, :].rearrange("p t a n -> p (t a n)"), bank[:, SCORES1, 0:n], ACT.Copy)\
                   .then_inc(sc_copied, 1)

            def diags(diag, slot, e0, count, signal):
                for j in range(count):
                    ins = act.activation(diag[:, slot, j, :], ident[:], ACT.Copy, scale=wgt[:, e0 + j:e0 + j + 1])
                ins.then_inc(signal, 1)

            copy_query0(0)
            next_head0(0)
            soft(0)
            for G in range(ALL0):
                hd, k = divmod(G, NG0)
                e = k * GE0
                act.wait_ge(dots0_done, (G + 1) * GE0)
                act.activation(gel[:, e:e + GE0], dot[:, e:e + GE0], ACT.Gelu).then_inc(gelu0_done, 1)
                if hd + 1 < PH and k == PROJECT_AT:
                    copy_query0(hd + 1)
                if hd + 1 < PH and k == TOPK_AT:
                    next_head0(hd + 1)
                    soft(hd + 1)
                for it in BESIDE[G]:
                    if it[0] == "q1":
                        copy_query1(0, it[1])
                    elif it[0] == "s1":
                        copy_scores1(0, it[1])
                    elif it[0] == "t1":
                        soft(pick_no(0, it[1]))
                    else:
                        item(1, it)

            def gelus1(hd, i, k):
                act.wait_ge(dots1_done, (hd * N1 + i) * NG + k + 1)
                act.activation(gel[:, k * GE:(k + 1) * GE], dot[:, k * GE:(k + 1) * GE], ACT.Gelu)\
                   .then_inc(gelu1_done, 1)

            def diags1(hd, i, k):
                G = (hd * N1 + i) * NG + k
                act.wait_ge(w1_ready, G + 1)
                at_least(act, v1_used, G - 1)
                diags(diag1, k % 2, k * GE, GE, diag1_ready)

            def head(hd, more, first=False, last=False):
                for i in range(N1):
                    for k in range(NG):
                        gelus1(hd, i, k)
                        if k:
                            diags1(hd, i, k - 1)
                        if first and i == 0 and k in FIRST_TOPK:
                            soft(pick_no(hd, FIRST_TOPK[k]))
                        if last and k == 1 and i in FINAL_BESIDE:
                            final_rms(FINAL_BESIDE[i])
                        if more and i == 0 and k == 2:
                            copy_query1(hd + 1, 0)
                        if more and i == 1 and k == 2:
                            copy_scores1(hd + 1, 0)
                        if more and i == 2 and k == 1:
                            soft(pick_no(hd + 1, 1))
                    if not (last and i == N1 - 1):
                        diags1(hd, i, NG - 1)
                    if more and i == 0:
                        copy_query1(hd + 1, 1)
                    if more and i == 1:
                        copy_scores1(hd + 1, 1)
                        soft(pick_no(hd + 1, 0))
                    if more and i == 2:
                        soft(pick_no(hd + 1, 2))

            def final_rms(t):
                if t:
                    act.wait_ge(out1_added, (PH - 1) * N1 + t)
                rms_of(len(NORMS) + t, h[:, t, :], hnX[0][:].rearrange("p k n -> p (k n)"))

            act.wait_ge(row0_added, ALL0 * GE0)
            head(0, True, first=True)
            with act.Fori(1, PH - 1) as hd:
                head(hd, True)
            head(PH - 1, False, last=True)
            for t in range(2, NT):
                final_rms(t)

        @block.vector
        def _(dve):
            link = Chain(dve, dve_chain)

            def normalise(m, src, gain, dst, signal):
                dve.wait_ge(rms_ready, m + 1)
                link.link(dve.reciprocal(rinv[:, m:m + 1], rms[:, m:m + 1]))
                dve.scalar_tensor_tensor(out=dst, in0=src, scalar=rinv[:, m:m + 1], in1=gain,
                                         op0=ALU.mult, op1=ALU.mult).then_inc(signal, 1)

            def norm(m):
                kind, t = NORMS[m]
                n = ("mix", "mem", "x", "p").index(kind)
                dve.wait_ge(gain_loaded[n], 16)
                xn_free(dve, m)
                normalise(m, (mtok if kind == "mem" else h)[:, t, :], gb[n][:], norm_dst(m), normed)

            def copy_turned(m):
                src = need(dve, ("turn", m, 1)).rearrange("p (k n) -> p k n", k=4)
                free(dve.tensor_copy(turned_dst(m, 1), src), ("turn", m, 1))

            for t in range(NT):
                dve.wait_ge(x_loaded[t], 16)
                norm(t)
            for t in range(NT):
                copy_turned(t)
            dve.wait_ge(small_loaded, 16 * 7)
            for i in range(2):
                for g in range(GROUPS):
                    src = need(dve, ("kvc", 2 * i + g))
                    for par in range(2):
                        rows = slice(par * DK, (par + 1) * DK)
                        tok = src[rows, :].rearrange("p (c l q) -> p q l c", q=2, l=STRIDE // 2)[:, par, :, :]
                        for part in range(2):
                            ls = slice(part * STRIDE // 2, (part + 1) * STRIDE // 2)
                            pe_b = pe_sb[rows, i, ls].unsqueeze(2).broadcast_to([DK, STRIDE // 2, NCMP])
                            dve.tensor_tensor(blk[rows, i, ls, g, :], tok[:, :, part:part + NCMP], pe_b, ALU.add)\
                               .then_inc(blk_ready, 1)
            for t in range(NT):
                src = need(dve, ("vsw", t))
                free(dve.tensor_copy(vsw[:, t, :, :].rearrange("p b n -> p (b n)"), src[:, 0:256]), ("vsw", t))
            for t in range(NM):
                norm(NT + t)
            dve.wait_ge(turned_act, NT)
            for t in range(NT):
                dve.wait_ge(v_gelu, t + 1)
                link.link(dve.tensor_scalar(vsum[:, 1, t:t + 1], vsum[:, 0, t:t + 1], -1.0 / GW, None, ALU.mult))
                link.link(dve.tensor_scalar(vn[:, t, :], gv[:], vsum[:, 1, t:t + 1], None, ALU.add))
                dve.tensor_tensor_reduce(out=gv[:], in0=vn[:, t, :], in1=vn[:, t, :], scale=1.0, scalar=0.0,
                                         op0=ALU.mult, op1=ALU.add, accum_out=vsum[:, 2, t:t + 1])\
                   .then_inc(v_centred, 1)
                dve.wait_ge(v_std, t + 1)
                link.link(dve.reciprocal(vsum[:, 0, t:t + 1], vsum[:, 3, t:t + 1]))
                link.link(dve.scalar_tensor_tensor(out=vn[:, t, :], in0=vn[:, t, :], scalar=vsum[:, 0, t:t + 1],
                                                   in1=ln_sb[:, 0, :], op0=ALU.mult, op1=ALU.mult))
                dve.tensor_tensor(vn[:, t, :], vn[:, t, :], ln_sb[:, 1, :], ALU.add).then_inc(vn_ready, 1)
            for t in range(NM):
                copy_turned(NT + t)

            def compress():
                src = need(dve, ("kcmp",))
                free(dve.tensor_copy(kcT[:], src[:, 0:NCMP]), ("kcmp",))
                src = need(dve, ("vcmp",))
                free(dve.tensor_copy(vc[:].rearrange("p g n -> p (g n)"), src[0:NCMP, 0:GROUPS * DK]), ("vcmp",))

            def spatial(t):
                dve.wait_ge(u_ready, 4)
                src = need(dve, ("spatial", t))
                tmp = gv[:].rearrange("p (g n) -> p g n", g=4)
                at_least(dve, og_ready, t)
                free(dve.tensor_tensor(gv[:], src, bs_sb[:].rearrange("p g n -> p (g n)"), ALU.add), ("spatial", t))
                was_read(dve, ("spatial", t))
                cols = slice(t * P, (t + 1) * P)
                dve.tensor_tensor(uT[:, :, cols], tmp, uT[:, :, cols], ALU.mult).then_inc(og_ready, 1)

            def compressed(i):
                shape = [P, HEADS, NCMP]
                if i < NT:
                    s8 = sm[:, i % 3, 0:HEADS * NCMP].rearrange("p (h c) -> p h c", h=HEADS)
                    mask = cmask[:, i, :].unsqueeze(1).broadcast_to([P, 4, NCMP])
                    keep = ckeep[:, i, :].unsqueeze(1).broadcast_to(shape)
                    if i >= 3:
                        dve.wait_ge(co_read, i - 2)
                    for g in range(GROUPS):
                        src = need(dve, ("cs", i, g))[:, 0:4 * NCMP].rearrange("p (h c) -> p h c", h=4)
                        free(dve.tensor_tensor(s8[:, 4 * g:4 * g + 4, :], src, mask, ALU.add), ("cs", i, g))
                    was_read(dve, ("cs", i, 1))
                    link.link(dve.tensor_reduce(cst[:, 0, :], s8, AX.X, ALU.max))
                    dve.tensor_tensor(s8, s8, cst[:, 0, :].unsqueeze(2).broadcast_to(shape), ALU.subtract)\
                       .then_inc(cs_ready, 1)
                    dve.wait_ge(cexp_ready, i + 1)
                    dve.tensor_tensor(s8, s8, keep, ALU.mult).then_inc(cp_ready, 1)
                if i >= 2:
                    t = i - 2
                    s8 = sm[:, t % 3, 0:HEADS * NCMP].rearrange("p (h c) -> p h c", h=HEADS)
                    dve.wait_ge(gates_ready, 1)
                    dve.wait_ge(cp_ready, t + 1)
                    link.link(dve.tensor_reduce(cst[:, 1, :], s8, AX.X, ALU.add))
                    link.link(dve.tensor_scalar(cst[:, 2, :], cst[:, 1, :], TINY, None, ALU.max))
                    link.link(dve.reciprocal(cst[:, 3, :], cst[:, 2, :]))
                    gate_c = gates[:, t, :].rearrange("p (h b) -> p h b", b=3)[:, :, 0]
                    link.link(dve.tensor_tensor(cst[:, 2, :], cst[:, 3, :], gate_c, ALU.mult))
                    src = need(dve, ("co", t)).rearrange("p (h d) -> p h d", h=HEADS)
                    free(dve.tensor_tensor(otok[:, t, :].rearrange("p (h d) -> p h d", h=HEADS), src,
                                           cst[:, 2, :].unsqueeze(2).broadcast_to([P, HEADS, DK]), ALU.mult), ("co", t))
                    was_read(dve, ("co", t))

            nu = len(UNITS)

            def attend(i):
                if i < nu:
                    t = UNITS[i][0]
                    n = (t + 1) * P
                    src = need(dve, ("s", i))
                    if i >= 3:
                        dve.wait_ge(probs_ready, i - 2)
                    free(dve.tensor_tensor_reduce(out=sm[:, i % 3, 0:n], in0=src[:, 0:n],
                                                  in1=causal[:, (3 - t) * P:(3 - t) * P + n], scale=1.0, scalar=NEG,
                                                  op0=ALU.add, op1=ALU.max, accum_out=rmax[:, i:i + 1]), ("s", i))
                    was_read(dve, ("s", i))
                    dve.tensor_scalar(nmax[:, i:i + 1], rmax[:, i:i + 1], -DK_SCALE, None, ALU.mult)\
                       .then_inc(nmax_ready, 1)
                if i >= O_LAG:
                    u = i - O_LAG
                    t, br, hd = UNITS[u]
                    dve.wait_ge(probs_ready, u + 1)
                    link.link(dve.reciprocal(coef[:, u:u + 1], rsum[:, u:u + 1]))
                    link.link(dve.tensor_tensor(coef[:, u:u + 1], coef[:, u:u + 1],
                                                gates[:, t, 3 * hd + br:3 * hd + br + 1], ALU.mult))
                    src = need(dve, ("o", u))
                    if br == 2:
                        dve.wait_ge(o_added, u - HEADS + 1)
                    o = otok[:, t, hd * DK:(hd + 1) * DK]
                    free(dve.scalar_tensor_tensor(out=o, in0=src[:, 0:DK], scalar=coef[:, u:u + 1], in1=o,
                                                  op0=ALU.mult, op1=ALU.add), ("o", u))

            def item(ch, it):
                key, i = it[0], it[1]
                t0, n = CHUNKS[ch]
                w = n * P
                if key == "y":
                    dve.wait_ge(mg_ready, 2 * (KD * ch + i) + 2)
                    y = yT[ch][:, i, :]
                    src = need(dve, ("a", ch, i))
                    free(dve.tensor_tensor(y, src[:, 0:w], sg[ch][:, 0, 0:w], ALU.mult), ("a", ch, i))
                    src = need(dve, ("b", ch, i))
                    free(dve.tensor_tensor(sg[ch][:, 1, 0:w], src[:, 0:w], sg[ch][:, 1, 0:w], ALU.mult), ("b", ch, i))
                    was_read(dve, ("a", ch, i))
                    was_read(dve, ("b", ch, i))
                    dve.tensor_tensor(y, y, sg[ch][:, 1, 0:w], ALU.add).then_inc(y_ready, 1)
                elif key in ("mix", "xo"):
                    t = it[2]
                    src = need(dve, (key, ch, i, t))
                    part = h[:, t0 + t, i * 512:(i + 1) * 512]
                    free(dve.tensor_tensor(part, src, part, ALU.add), (key, ch, i, t))
                elif key in ("nx", "np"):
                    if i < n:
                        norm(norm_no(key[1], t0 + i))
                    if i:
                        copy_turned(norm_no(key[1], t0 + i - 1))
                elif key == "xa":
                    if i < XH * n:
                        u = unit_no(ch, i)
                        src = need(dve, ("xs", ch, i))
                        link.link(dve.tensor_reduce(xst[:, 0, u - 1:u], src[:, 0:MEM], AX.X, ALU.max))
                        dve.tensor_scalar(xst[:, 1, u - 1:u], xst[:, 0, u - 1:u], -XD_SCALE, None, ALU.mult)\
                           .then_inc(xnmax_ready, 1)
                    if 1 <= i <= XH * n:
                        f = i - 1
                        u = unit_no(ch, f)
                        dve.wait_ge(xexp_ready, u)
                        link.link(dve.reciprocal(xst[:, 3, u - 1:u], xst[:, 2, u - 1:u]))
                        if f >= 2:
                            need(dve, ("xpt", ch, f - 2))
                        dve.tensor_scalar(xpn[:, f % 2, :], xp[:, f % 2, :], xst[:, 3, u - 1:u], None, ALU.mult)\
                           .then_inc(xp_ready, 1)
                    if i >= 3 and (i - 3) % n == n - 1:
                        hd = (i - 3) // n
                        for c in range(2):
                            src = need(dve, ("xot", ch, hd, c))
                            free(dve.tensor_copy(xoT[ch][:, 2 * hd + c, :], src[:, 0:w]), ("xot", ch, hd, c))

            for it in FIRST:
                key, i = it[0], it[1]
                if key == "item":
                    item(0, it[1:])
                elif key == "xv":
                    t = it[2]
                    free(dve.tensor_copy(xv[:, t, i * 512:(i + 1) * 512], need(dve, it)), it)
                elif key == "cmp":
                    compress()
                elif key in ("spatial", "c", "att"):
                    {"spatial": spatial, "c": compressed, "att": attend}[key](i)

            peer = Chain(dve, dve_peer)

            def top16(rows):
                n = len(rows)
                for values, rest, val, idx in rows:
                    peer.step(dve.max(val[:, 0:8], values))
                for k, (values, rest, val, idx) in enumerate(rows):
                    peer.join(n - 1 - k + 2 * k)
                    peer.step(dve.max_index(idx[:, 0:8], val[:, 0:8], values))
                    peer.step(dve.match_replace(rest, val[:, 0:8], values, -3.0e38))
                for k, (values, rest, val, idx) in enumerate(rows):
                    peer.join(2 * (n - 1 - k) + k)
                    peer.step(dve.max(val[:, 8:16], rest))
                for k, (values, rest, val, idx) in enumerate(rows):
                    peer.join(n - 1)
                    peer.step(dve.max_index(idx[:, 8:16], val[:, 8:16], rest))

            def topk(q, slot, halves, ready, count, taken):
                at_least(dve, gate_ready, q)
                stand(dve, ready, count)
                top16([(halves(p), sc_rest[:, p, :], hv[:, p, :], hi[:, p, :]) for p in range(2)])
                peer.join()
                grid = [P, TOPK, TOPK]
                peer.link(dve.tensor_tensor(cand[:], hv[:, 0, :].unsqueeze(2).broadcast_to(grid),
                                            hv[:, 1, :].unsqueeze(1).broadcast_to(grid), ALU.add))
                peer.step(dve.tensor_copy(hif[:], hi[:]))
                top16([(cand[:].rearrange("p i j -> p (i j)"), cand_rest[:], best[:], pos[:])])
                peer.join()
                dve.tensor_scalar(pst[:, 0:1], best[:, 0:1], -1.0, None, ALU.mult).then_inc(soft_bias, 1)
                peer.step(dve.tensor_scalar(ij[:, 0, :], pos[:], 4, None, ALU.logical_shift_right))
                peer.step(dve.tensor_scalar(ij[:, 1, :], pos[:], TOPK - 1, None, ALU.bitwise_and))
                peer.join()
                peer.link(dve.tensor_copy(ijf[:], ij[:]))
                both = [P, 2 * TOPK, TOPK]
                flat = hot[:].rearrange("p a i j -> p (a i) j")
                peer.link(dve.tensor_tensor(flat, ijf[:].rearrange("p a i -> p (a i)").unsqueeze(2).broadcast_to(both),
                                            iota16[:].unsqueeze(1).broadcast_to(both), ALU.is_equal))
                peer.link(dve.tensor_tensor(hot[:], hot[:], hif[:].unsqueeze(2).broadcast_to([P, 2, TOPK, TOPK]),
                                            ALU.mult))
                peer.link(dve.tensor_reduce(sel[:].rearrange("p a i -> p (a i)"), flat, AX.X, ALU.add))
                at_least(dve, picks_taken, taken)
                dve.scalar_tensor_tensor(out=eidx[:, slot, :], in0=sel[:, 0, :], scalar=float(KEYS), in1=sel[:, 1, :],
                                         op0=ALU.mult, op1=ALU.add).then_inc(picks_ready, 1)
                dve.wait_ge(soft_exp, q + 1)
                peer.link(dve.reciprocal(pst[:, 2:3], pst[:, 1:2]))
                dve.tensor_scalar(gate[:, slot, :], ex[:], pst[:, 2:3], None, ALU.mult).then_inc(gate_ready, 1)

            def topk0(hd):
                topk(hd, N1 + hd % 2, lambda p: bank[:, SCORES0, p * KEYS:(p + 1) * KEYS], scores0_done, hd + 1, hd - 1)

            def topk1(hd, i):
                topk(pick_no(hd, i), i, lambda p: scs[:, i, p, :], sc_copied, 2 * hd + (1 if i < 2 else 2),
                     pick_no(hd, i) - N1 + 1)

            def dots(u_rows, act_rows, e0, signal):
                for j in range(len(u_rows)):
                    ins = dve.tensor_tensor_reduce(out=u_rows[j], in0=u_rows[j], in1=act_rows, scale=1.0, scalar=0.0,
                                                   op0=ALU.mult, op1=ALU.add, accum_out=dot[:, e0 + j:e0 + j + 1])
                ins.then_inc(signal, 1)

            def weigh(slot, es, signal):
                dve.tensor_tensor(wgt[:, es], gel[:, es], gate[:, slot, es], ALU.mult).then_inc(signal, 1)

            def weigh0(G):
                dve.wait_ge(gelu0_done, G + 1)
                e = G % NG0 * GE0
                weigh(N1 + G // NG0 % 2, slice(e, e + GE0), w0_ready)

            def add_row0(G, j):
                if j == 0:
                    dve.wait_ge(v0_loaded[G % VG0], 16 * GE0 * (G // VG0 + 1))
                    dve.wait_ge(w0_ready, G + 1)
                e = G % NG0 * GE0 + j
                at_least(dve, row0_added, G * GE0 + j)
                dve.scalar_tensor_tensor(out=h[:, 0, :], in0=V0[:, G % VG0, j, :], scalar=wgt[:, e:e + 1],
                                         in1=h[:, 0, :], op0=ALU.mult, op1=ALU.add).then_inc(row0_added, 1)

            topk0(0)
            steps = peer.n
            for G in range(ALL0 + 1):
                hd, k = divmod(G, NG0)
                if G == 0:
                    dve.wait_ge(gate_ready, 1)
                if G:
                    weigh0(G - 1)
                for j in range(GE0):
                    if G < ALL0:
                        if j == 0:
                            dve.wait_ge(u0_loaded[G % UG0], 16 * GE0 * (G // UG0 + 1))
                        dots([U0[G % UG0][:, j, :]], hp0[:], k * GE0 + j, dots0_done)
                    if G:
                        add_row0(G - 1, j)
                if G == ALL0:
                    break
                if hd + 1 < PH and k == TOPK_AT:
                    topk0(hd + 1)
                for it in BESIDE[G]:
                    if it[0] == "t1":
                        topk1(0, it[1])
                    elif it[0] not in ("q1", "s1"):
                        item(1, it)

            def add_out1(b, i, behind=0):
                dve.wait_ge(v1_used, NG * (b + 1) - behind)
                src = bank[:, OUT1 + 2 * i:OUT1 + 2 * i + 2, :].rearrange("p n c -> p (n c)")
                dve.tensor_tensor(h[:, i + 1, :], src, h[:, i + 1, :], ALU.add).then_inc(out1_added, 1)

            def weigh1(hd, i, k):
                dve.wait_ge(gelu1_done, (hd * N1 + i) * NG + k + 1)
                weigh(i, slice(k * GE, (k + 1) * GE), w1_ready)

            def head(hd, more, first=False, last=False):
                for i in range(N1):
                    b = hd * N1 + i
                    dve.wait_ge(gate_ready, pick_no(hd, i) + 1)
                    for k in range(NG):
                        dve.wait_ge(u1_loaded[k], 16 * GE * (b + 1))
                        dots([U1[:, k * GE + j, :] for j in range(GE)], hp1[:, i, :], k * GE, dots1_done)
                        if k:
                            weigh1(hd, i, k - 1)
                        if first and i == 0 and k in FIRST_TOPK:
                            topk1(hd, FIRST_TOPK[k])
                        if last and k == 2 and i in FINAL_BESIDE:
                            final_norm(FINAL_BESIDE[i])
                        if more and i == 2 and k == 1:
                            topk1(hd + 1, 1)
                    weigh1(hd, i, NG - 1)
                    if not (isinstance(b, int) and b == 0):
                        add_out1(b - 1, (i - 1) % N1)
                    if more and i >= 1:
                        topk1(hd + 1, 2 * (i - 1))

            def final_norm(t):
                dve.wait_ge(gain_loaded[4], 16)
                if t:
                    dve.wait_ge(dots1_done, ((PH - 1) * N1 + t) * NG)
                normalise(len(NORMS) + t, h[:, t, :], gb[4][:], hp0[:] if t == 0 else hp1[:, t - 1, :], final_ready)

            head(0, True, first=True)
            with dve.Fori(1, PH - 1) as hd:
                peer.base, peer.n = hd * (N1 * steps) + (PICKS0 + N1) * steps, 0
                head(hd, True)
            peer.base, peer.n = (PICKS0 + N1 * PH) * steps, 0
            head(PH - 1, False, last=True)
            final_norm(NT - 2)
            dve.wait_ge(v1_loaded[(NG - 1) % VG], 16 * GE * (NG // VG * PH * N1))
            dve.wait_ge(w1_ready, PH * N1 * NG)
            for j in range(GE):
                e = (NG - 1) * GE + j
                link.link(dve.scalar_tensor_tensor(out=h[:, N1, :], in0=V1[(NG - 1) % VG][:, j, :],
                                                   scalar=wgt[:, e:e + 1], in1=h[:, N1, :], op0=ALU.mult, op1=ALU.add))
            add_out1(PH * N1 - 1, N1 - 1, behind=1)
            final_norm(NT - 1)


def _panels(w):
    k, n = w.shape
    wide = 2048 // (k // P)
    return np.ascontiguousarray(w.reshape(k // P, P, n // wide, wide).transpose(2, 1, 0, 3)).reshape(-1, P, 2048)


def kernel(**inputs):
    import concourse.bacc as bacc
    from concourse.bass_utils import run_bass_kernel_spmd

    a = {k: np.asarray(v) for k, v in inputs.items()}
    w_in = a["w_in"]
    q0, kc0, vc0, ks0, vs0, kw0, vw0, g0, u0, v0, m0 = [int(i) for i in np.cumsum(
        [0, 512, 128, 128, 128, 128, 128, 128, 24, 512, 512])]
    cols = []
    for c in range(4):
        cols += [q0 + hd * DK + i for hd in (c, 4 + c) for i in range(DK)]
    for s in (kc0, vc0):
        for g in range(GROUPS):
            cols += [s + g * DK + i for _ in range(2) for i in range(DK)]
    for s, n in ((ks0, P), (kw0, P), (vs0, P), (vw0, P), (v0, GW), (u0, GW)):
        cols += list(range(s, s + n))
    for c in range(KD):
        for b in range(2):
            cols += list(range(m0 + b * D + c * P, m0 + b * D + (c + 1) * P))
    win = _panels(w_in[:, cols])
    w1 = [np.ascontiguousarray(a[f"cmp_w1_{s}"].reshape(2, BLOCK // 4, P, HID).transpose(0, 2, 1, 3)).reshape(2, P, 2048)
          for s in "kv"]
    w_panels = np.concatenate([win[0:8], w1[0], w1[1], win[8:10], _panels(a["w_xkv"]), _panels(a["w_nsa_out"]),
                               _panels(a["w_gmlp_out"]), win[10:18], _panels(a["w_mix_out"]), _panels(a["w_xq"]),
                               _panels(a["w_xo"])])
    peer_w = a["w_peer_q"].reshape(KD, P, PH, 2 * KEYS).transpose(2, 1, 0, 3)
    keys = a["peer_sub_keys"].transpose(0, 3, 1, 2).reshape(PH, P, 1, 2 * KEYS)
    pe = [a[f"cmp_pe_{s}"].reshape(BLOCK // 2, 2, DK).transpose(1, 2, 0).reshape(P, BLOCK // 2) for s in "kv"]
    arrays = {
        "x": a["x"].reshape(S, D), "mem": a["mem"].reshape(MEM, D),
        "gains": np.stack([a[k] for k in ("g_mix", "g_mem", "g_xattn", "g_peer", "g_final")]),
        "w_panels": w_panels,
        "w_gates": w_in[:, g0:g0 + 24].reshape(KD, P, 24).transpose(1, 0, 2),
        "cmp_pe": np.stack(pe, axis=1),
        "cmp_b1": np.stack([a[f"cmp_b1_{s}"].reshape(2, P).T for s in "kv"], axis=1),
        "cmp_w2": np.stack([a[f"cmp_w2_{s}"].reshape(2, P, DK).transpose(1, 0, 2) for s in "kv"], axis=1),
        "ln_gb": np.stack([a["gmlp_ln_g"], a["gmlp_ln_b"]]),
        "ws_t": a["gmlp_ws"].transpose(2, 0, 1),
        "bs": a["gmlp_bs"],
        "peer_w": np.concatenate([peer_w, keys], axis=2),
        "peer_u": a["peer_u"], "peer_v": a["peer_v"],
    }
    nc = bacc.Bacc("TRN2", target_bir_lowering=False, num_devices=1)
    feed, args = {}, []
    for name, v in arrays.items():
        v = np.ascontiguousarray(v)
        feed[name + "_dram"] = v
        args.append(nc.dram_tensor(name + "_dram", v.shape, mybir.dt.from_np(v.dtype), kind="ExternalInput").ap())
    args.append(nc.dram_tensor("out_dram", (S, D), F32, kind="ExternalOutput").ap())
    hybrid_block(nc, *args)
    r = run_bass_kernel_spmd(nc, [feed], core_ids=[0])
    return r.results[0]["out_dram"].reshape(1, S, D)
```
